# Optimizing a Trainium2 kernel written in Bass

```python
import math
import jax, jax.numpy as jnp
from jax import lax
import numpy as np

D_MODEL = 1024
BATCH = 1
SEQ = 256
DEPTH = 2
DEC_BATCH = 8
DEC_SEQ = 4
PAST_LEN = 1024
PAGE_SIZE = 128

N_EVEN = (DEPTH + 1) // 2
N_ODD = DEPTH // 2
HD_A = 64
D_A = D_MODEL // 2
H_A = D_A // HD_A
MOBA_BLOCK = 256
MOBA_TOPK = 3
Q_CHUNK = 16
N_BUCKETS = 32
MAX_DISTANCE = 128
C_CONV = D_MODEL // 2
CONV_W = 31
D_IN_EVEN = 3 * D_A + 2 * C_CONV
D_MIX_EVEN = D_A + C_CONV
D_GM = D_MODEL
GM_CHUNK = 128
G_C = 8
CG = D_GM // G_C
N_MEM = 256
H_X = 4
HD_X = D_MODEL // H_X
N_EXPERTS = 16
N_GROUPS = 4
EPG = N_EXPERTS // N_GROUPS
TOP_K = 2
D_FF = 512
ALPHA = (2 * DEPTH) ** 0.25
BETA = (8 * DEPTH) ** -0.25
LN_EPS = 1e-5

kernel_name = 'hybrid_moba_conv_gmlp_moe_decoder_step'

def layer_norm(x, g, b):
    xf = x.astype(jnp.float32)
    mu = jnp.mean(xf, -1, keepdims=True)
    var = jnp.mean(jnp.square(xf - mu), -1, keepdims=True)
    return ((xf - mu) * lax.rsqrt(var + LN_EPS) * g.astype(jnp.float32) + b.astype(jnp.float32)).astype(x.dtype)

def t5_bucket(rel):
    n = jnp.maximum(rel, 0)
    max_exact = N_BUCKETS // 2
    nf = jnp.maximum(n, 1).astype(jnp.float32)
    large = max_exact + (jnp.log(nf / max_exact) / math.log(MAX_DISTANCE / max_exact)
                         * (N_BUCKETS - max_exact)).astype(jnp.int32)
    large = jnp.minimum(large, N_BUCKETS - 1)
    return jnp.where(n < max_exact, n, large)

def moba_core(q, kb, vb, kmean, qpos, bias_t):
    B, H, Q, _ = q.shape
    nb = kb.shape[1]
    qblk = qpos // MOBA_BLOCK
    gate = jnp.einsum('bhqd,bnhd->bhqn', q.astype(jnp.float32), kmean)
    fully_past = jnp.arange(nb)[None, :] < qblk[:, None]
    gate = jnp.where(fully_past[None, None], gate, -jnp.inf)
    n_sel = min(MOBA_TOPK, nb)
    _, top_idx = lax.top_k(gate, n_sel)
    top_ok = top_idx < qblk[None, None, :, None]
    own = jnp.broadcast_to(qblk[None, None, :, None], (B, H, Q, 1)).astype(jnp.int32)
    sel = jnp.concatenate([top_idx.astype(jnp.int32), own], -1)
    sel_ok = jnp.concatenate([top_ok, jnp.ones((B, H, Q, 1), bool)], -1)
    bi = jnp.arange(B)[:, None, None, None]
    hi = jnp.arange(H)[None, :, None, None]
    kg = kb[bi, sel, :, hi, :]
    vg = vb[bi, sel, :, hi, :]
    kpos = sel[..., None] * MOBA_BLOCK + jnp.arange(MOBA_BLOCK, dtype=jnp.int32)
    qp = qpos[None, None, :, None, None]
    logits = jnp.einsum('bhqd,bhqskd->bhqsk', q, kg, preferred_element_type=jnp.float32) * (HD_A ** -0.5)
    bias = bias_t[jnp.arange(H)[None, :, None, None, None], t5_bucket(qp - kpos)].astype(jnp.float32)
    mask = sel_ok[..., None] & (kpos <= qp)
    logits = jnp.where(mask, logits + bias, -jnp.inf)
    p = jax.nn.softmax(logits.reshape(B, H, Q, -1), axis=-1).reshape(logits.shape)
    return jnp.einsum('bhqsk,bhqskd->bhqd', p.astype(vb.dtype), vg)

def to_blocks(k):
    B, L = k.shape[:2]
    nb = -(-L // MOBA_BLOCK)
    k = jnp.pad(k, ((0, 0), (0, nb * MOBA_BLOCK - L), (0, 0), (0, 0)))
    return k.reshape(B, nb, MOBA_BLOCK, H_A, HD_A)

def moba_prompt(q, k, v, bias_t):
    B, S = q.shape[:2]
    kb, vb = to_blocks(k), to_blocks(v)
    kmean = jnp.mean(kb, axis=2, dtype=jnp.float32)
    nqc = S // Q_CHUNK
    qc = q.reshape(B, nqc, Q_CHUNK, H_A, HD_A).transpose(1, 0, 3, 2, 4)
    pos = jnp.arange(S, dtype=jnp.int32).reshape(nqc, Q_CHUNK)
    out = lax.map(lambda a: moba_core(a[0], kb, vb, kmean, a[1], bias_t), (qc, pos))
    return out.transpose(1, 0, 3, 2, 4).reshape(B, S, D_A)

def moba_sample(q, k_new, v_new, pool_k, pool_v, page_table, bias_t):
    DB, DS = q.shape[:2]
    past_len = page_table.shape[1] * PAGE_SIZE
    total = past_len + DS
    nb = -(-total // MOBA_BLOCK)

    def assemble(pool, new):
        past = pool[page_table].reshape(DB, past_len, H_A, HD_A).astype(new.dtype)
        pad = jnp.zeros((DB, nb * MOBA_BLOCK - total, H_A, HD_A), new.dtype)
        return jnp.concatenate([past, new, pad], 1).reshape(DB, nb, MOBA_BLOCK, H_A, HD_A)

    kb, vb = assemble(pool_k, k_new), assemble(pool_v, v_new)
    kmean = jnp.mean(kb, axis=2, dtype=jnp.float32)
    qpos = past_len + jnp.arange(DS, dtype=jnp.int32)
    out = moba_core(q.transpose(0, 2, 1, 3), kb, vb, kmean, qpos, bias_t)
    return out.transpose(0, 2, 1, 3).reshape(DB, DS, D_A)

def even_in(x, w_in):
    B, L, _ = x.shape
    h = x @ w_in
    q, k, v, a, g = jnp.split(h, [D_A, 2 * D_A, 3 * D_A, 3 * D_A + C_CONV], axis=-1)
    shp = (B, L, H_A, HD_A)
    return q.reshape(shp), k.reshape(shp), v.reshape(shp), a, g

def conv_branch(a, gate_in, prev, w, b, ln_g, ln_b):
    u = a * jax.nn.sigmoid(gate_in)
    u_ext = jnp.concatenate([prev.astype(u.dtype), u], 1)
    y = lax.conv_general_dilated(u_ext, w[:, None, :], window_strides=(1,), padding='VALID',
                                 dimension_numbers=('NWC', 'WIO', 'NWC'),
                                 feature_group_count=C_CONV) + b
    y = jax.nn.silu(layer_norm(y, ln_g, ln_b))
    return y, u_ext[:, -(CONV_W - 1):]

def odd_in(x, w_in, g, b):
    z = jax.nn.gelu(x @ w_in, approximate=False)
    u, v = jnp.split(z, 2, axis=-1)
    return u, layer_norm(v, g, b)

def spatial_gate(u, v, w_s, b_s):
    B, NC, T, _ = v.shape
    v5 = v.reshape(B, NC, T, G_C, CG)
    mix = jnp.einsum('gts,bnsgc->bntgc', w_s, v5) + b_s.T[None, None, :, :, None]
    return u * mix.reshape(B, NC, T, D_GM)

def mem_kv(mem, w_kv):
    B = mem.shape[0]
    kv = mem @ w_kv
    k, v = jnp.split(kv, 2, axis=-1)
    return k.reshape(B, N_MEM, H_X, HD_X), v.reshape(B, N_MEM, H_X, HD_X)

def cross_attn(x, mk, mv, wq, wo):
    B, L, _ = x.shape
    q = (x @ wq).reshape(B, L, H_X, HD_X)
    s = jnp.einsum('blhd,bmhd->bhlm', q, mk.astype(q.dtype), preferred_element_type=jnp.float32) * (HD_X ** -0.5)
    p = jax.nn.softmax(s, axis=-1).astype(x.dtype)
    o = jnp.einsum('bhlm,bmhd->blhd', p, mv.astype(x.dtype)).reshape(B, L, D_MODEL)
    return o @ wo

def moe_tokens(x, w_router, r_bias, wg, wu, wd):
    T = x.shape[0]
    scores = jax.nn.sigmoid(jnp.einsum('td,de->te', x, w_router, preferred_element_type=jnp.float32))
    sel = (scores + r_bias.astype(jnp.float32)).reshape(T, N_GROUPS, EPG)
    grp_score = jnp.sum(lax.top_k(sel, TOP_K)[0], -1)
    best = jnp.argmax(grp_score, -1)
    in_grp = sel[jnp.arange(T), best]
    _, loc = lax.top_k(in_grp, TOP_K)
    idx = best[:, None] * EPG + loc
    w = jnp.take_along_axis(scores, idx, -1)
    w = w / jnp.sum(w, -1, keepdims=True)
    combine = jnp.sum(jax.nn.one_hot(idx, N_EXPERTS, dtype=jnp.float32) * w[..., None], axis=1)
    h = jax.nn.silu(jnp.einsum('td,edf->tef', x, wg)) * jnp.einsum('td,edf->tef', x, wu)
    h = h * combine[..., None].astype(h.dtype)
    return jnp.einsum('tef,efd->td', h, wd)

def moe(x, w_router, r_bias, wg, wu, wd):
    return lax.map(lambda xb: moe_tokens(xb, w_router, r_bias, wg, wu, wd), x)

def setup_inputs(seed: int = 0) -> dict:
    key = jax.random.key(seed)
    ks = jax.random.split(key, 40)
    f32 = jnp.float32
    n_pages = PAST_LEN // PAGE_SIZE
    n_used = DEC_BATCH * n_pages
    n_phys = n_used + n_used // 4

    def nrm(i, shape, scale=1.0):
        return jax.random.normal(ks[i], shape, f32) * scale

    page_table = jax.random.permutation(ks[0], n_phys)[:n_used].reshape(DEC_BATCH, n_pages).astype(jnp.int32)
    col_even = jnp.concatenate([jnp.ones((2 * D_A,), f32), jnp.full((D_A,), BETA, f32),
                                jnp.full((C_CONV,), BETA, f32), jnp.ones((C_CONV,), f32)])
    col_xkv = jnp.concatenate([jnp.ones((D_MODEL,), f32), jnp.full((D_MODEL,), BETA, f32)])
    col_odd = jnp.concatenate([jnp.full((D_GM,), BETA, f32), jnp.ones((D_GM,), f32)])
    return {
        'x_prompt': nrm(1, (BATCH, SEQ, D_MODEL)),
        'x_sample': nrm(2, (DEC_BATCH, DEC_SEQ, D_MODEL)),
        'cache_k': nrm(3, (N_EVEN, n_phys, PAGE_SIZE, H_A, HD_A)),
        'cache_v': nrm(4, (N_EVEN, n_phys, PAGE_SIZE, H_A, HD_A)),
        'state_conv': nrm(5, (N_EVEN, DEC_BATCH, CONV_W - 1, C_CONV), 0.5),
        'cache_mem_k': nrm(6, (DEPTH, DEC_BATCH, N_MEM, H_X, HD_X)),
        'cache_mem_v': nrm(7, (DEPTH, DEC_BATCH, N_MEM, H_X, HD_X)),
        'page_table': page_table,
        'mem_prompt': nrm(8, (BATCH, N_MEM, D_MODEL)),
        'rel_bias': nrm(9, (N_BUCKETS, H_A), 0.2),
        'w_in_even': nrm(10, (N_EVEN, D_MODEL, D_IN_EVEN), D_MODEL ** -0.5) * col_even,
        'conv_w': nrm(11, (N_EVEN, CONV_W, C_CONV), CONV_W ** -0.5),
        'conv_b': nrm(12, (N_EVEN, C_CONV), 0.02),
        'conv_ln_g': 1.0 + nrm(13, (N_EVEN, C_CONV), 0.02),
        'conv_ln_b': nrm(14, (N_EVEN, C_CONV), 0.02),
        'w_out_even': nrm(15, (N_EVEN, D_MIX_EVEN, D_MODEL), BETA * D_MIX_EVEN ** -0.5),
        'w_in_odd': nrm(16, (N_ODD, D_MODEL, 2 * D_GM), D_MODEL ** -0.5) * col_odd,
        'sgu_ln_g': 1.0 + nrm(17, (N_ODD, D_GM), 0.02),
        'sgu_ln_b': nrm(18, (N_ODD, D_GM), 0.02),
        'sgu_w': nrm(19, (N_ODD, G_C, GM_CHUNK, GM_CHUNK), GM_CHUNK ** -0.5),
        'sgu_b': 1.0 + nrm(20, (N_ODD, G_C, GM_CHUNK), 0.02),
        'w_out_odd': nrm(21, (N_ODD, D_GM, D_MODEL), BETA * D_GM ** -0.5),
        'w_xq': nrm(22, (DEPTH, D_MODEL, D_MODEL), D_MODEL ** -0.5),
        'w_xkv': nrm(23, (DEPTH, D_MODEL, 2 * D_MODEL), D_MODEL ** -0.5) * col_xkv,
        'w_xo': nrm(24, (DEPTH, D_MODEL, D_MODEL), BETA * D_MODEL ** -0.5),
        'w_router': nrm(25, (D_MODEL, N_EXPERTS), D_MODEL ** -0.5),
        'router_bias': nrm(26, (N_EXPERTS,), 0.01),
        'w_exp_gate': nrm(27, (DEPTH, N_EXPERTS, D_MODEL, D_FF), D_MODEL ** -0.5),
        'w_exp_up': nrm(28, (DEPTH, N_EXPERTS, D_MODEL, D_FF), BETA * D_MODEL ** -0.5),
        'w_exp_down': nrm(29, (DEPTH, N_EXPERTS, D_FF, D_MODEL), BETA * D_FF ** -0.5),
        'ln_g': 1.0 + nrm(30, (DEPTH, 3, D_MODEL), 0.02),
        'ln_b': nrm(31, (DEPTH, 3, D_MODEL), 0.02),
    }

def reference(x_prompt, x_sample, cache_k, cache_v, state_conv, cache_mem_k, cache_mem_v, page_table,
              mem_prompt, rel_bias, w_in_even, conv_w, conv_b, conv_ln_g, conv_ln_b, w_out_even,
              w_in_odd, sgu_ln_g, sgu_ln_b, sgu_w, sgu_b, w_out_odd, w_xq, w_xkv, w_xo,
              w_router, router_bias, w_exp_gate, w_exp_up, w_exp_down, ln_g, ln_b):
    bias_t = rel_bias.T
    causal = jnp.tril(jnp.ones((GM_CHUNK, GM_CHUNK), dtype=sgu_w.dtype))
    xp, xs = x_prompt, x_sample
    B, S, _ = xp.shape
    DB, DS, _ = xs.shape
    k_p, v_p, k_s, v_s, c_p, c_s, mk_p, mv_p, gv_s = ([] for _ in range(9))
    for l in range(DEPTH):
        if l % 2 == 0:
            e = l // 2
            q, k, v, a, g = even_in(xp, w_in_even[e])
            att = moba_prompt(q, k, v, bias_t)
            cv, cst = conv_branch(a, g, jnp.zeros((B, CONV_W - 1, C_CONV), xp.dtype),
                                  conv_w[e], conv_b[e], conv_ln_g[e], conv_ln_b[e])
            mix_p = jnp.concatenate([att, cv], -1) @ w_out_even[e]
            k_p.append(k); v_p.append(v); c_p.append(cst)
            q, k, v, a, g = even_in(xs, w_in_even[e])
            att = moba_sample(q, k, v, cache_k[e], cache_v[e], page_table, bias_t)
            cv, cst = conv_branch(a, g, state_conv[e], conv_w[e], conv_b[e], conv_ln_g[e], conv_ln_b[e])
            mix_s = jnp.concatenate([att, cv], -1) @ w_out_even[e]
            k_s.append(k); v_s.append(v); c_s.append(cst)
        else:
            o = l // 2
            ws = sgu_w[o] * causal
            u, vv = odd_in(xp, w_in_odd[o], sgu_ln_g[o], sgu_ln_b[o])
            nc = S // GM_CHUNK
            mix_p = spatial_gate(u.reshape(B, nc, GM_CHUNK, D_GM), vv.reshape(B, nc, GM_CHUNK, D_GM),
                                 ws, sgu_b[o]).reshape(B, S, D_GM) @ w_out_odd[o]
            u, vv = odd_in(xs, w_in_odd[o], sgu_ln_g[o], sgu_ln_b[o])
            mix_s = spatial_gate(u[:, None], vv[:, None], ws[:, :DS, :DS],
                                 sgu_b[o][:, :DS]).reshape(DB, DS, D_GM) @ w_out_odd[o]
            gv_s.append(vv)
        xp = layer_norm(ALPHA * xp + mix_p, ln_g[l, 0], ln_b[l, 0])
        xs = layer_norm(ALPHA * xs + mix_s, ln_g[l, 0], ln_b[l, 0])
        mk, mv = mem_kv(mem_prompt, w_xkv[l])
        mk_p.append(mk); mv_p.append(mv)
        xp = layer_norm(ALPHA * xp + cross_attn(xp, mk, mv, w_xq[l], w_xo[l]), ln_g[l, 1], ln_b[l, 1])
        xs = layer_norm(ALPHA * xs + cross_attn(xs, cache_mem_k[l], cache_mem_v[l], w_xq[l], w_xo[l]),
                        ln_g[l, 1], ln_b[l, 1])
        xp = layer_norm(ALPHA * xp + moe(xp, w_router, router_bias, w_exp_gate[l], w_exp_up[l], w_exp_down[l]),
                        ln_g[l, 2], ln_b[l, 2])
        xs = layer_norm(ALPHA * xs + moe(xs, w_router, router_bias, w_exp_gate[l], w_exp_up[l], w_exp_down[l]),
                        ln_g[l, 2], ln_b[l, 2])
    new_k_prompt = jnp.stack(k_p)
    new_v_prompt = jnp.stack(v_p)
    new_k_sample = jnp.stack(k_s)
    new_v_sample = jnp.stack(v_s)
    new_conv_prompt = jnp.stack(c_p)
    new_conv_sample = jnp.stack(c_s)
    new_mem_k_prompt = jnp.stack(mk_p)
    new_mem_v_prompt = jnp.stack(mv_p)
    new_gmlp_v_sample = jnp.stack(gv_s)
    return (xp, xs, new_k_prompt, new_v_prompt, new_k_sample, new_v_sample, new_conv_prompt,
            new_conv_sample, new_mem_k_prompt, new_mem_v_prompt, new_gmlp_v_sample)


_drawn_inputs = setup_inputs


def setup_inputs(seed=0):
    import zlib

    import numpy as np

    out = dict(_drawn_inputs(seed))
    spreads = {}
    factors = {'rel_bias': 6.645,
     'conv_b': 3.619,
     'conv_ln_g': 9.942,
     'conv_ln_b': 6.514,
     'sgu_ln_g': 8.233,
     'sgu_ln_b': 8.336,
     'sgu_b': 27.265,
     'cache_k': 3.576,
     'cache_v': 2.852}
    for name, (base, spread) in spreads.items():
        noise = np.random.default_rng([zlib.crc32(name.encode()), seed]).standard_normal(out[name].shape)
        drawn = base * np.exp(spread * noise) if base else spread * noise
        out[name] = __import__('jax').numpy.asarray(drawn.astype(out[name].dtype))
    for name, factor in factors.items():
        out[name] = (out[name] * factor).astype(out[name].dtype)
    return out
```

```python
from contextlib import ExitStack

import numpy as np

import concourse.bass as bass
from concourse import mybir

ALU = mybir.AluOpType
ACT = mybir.ActivationFunctionType
X = mybir.AxisListType.X
F32 = mybir.dt.float32
I32 = mybir.dt.int32

P = 128
D = 1024
SEQ = 256
DB, DS = 8, 4
NTOK = SEQ + DB * DS
S0 = SEQ
DEPTH = 2
PAST, PAGE = 1024, 128
NPAGE = PAST // PAGE
NPHYS = DB * NPAGE * 5 // 4
DA, HA, HD = 512, 8, 64
CC, CW = 512, 31
NB_BUCKET, MAXDIST = 32, 128
NMEM, HX, HDX = 256, 4, 256
NE, NG, EPG, DFF = 16, 4, 4, 512
FT = D // P
ALPHA = (2 * DEPTH) ** 0.25
EPS = 1e-5
NEG = -1e30
MOBA = 256
NBLK = PAST // MOBA

SLOTS = 6
UNIT = 8 * 512
NACC = 4

C_ID, C_OWN, C_IDX, C_FIRST, C_TRI = 0, 128, 192, 196, 200
NCONST = 216
T_OH4, T_OHS = 0, 380
NTABLE = 380 + PAST + DB * DS


def bucket(n):
    n = np.maximum(n, 0)
    half = NB_BUCKET // 2
    nf = np.maximum(n, 1).astype(np.float32)
    large = half + (np.log(nf / np.float32(half)) / np.float32(np.log(MAXDIST / half))
                    * np.float32(NB_BUCKET - half)).astype(np.int32)
    return np.where(n < half, n, np.minimum(large, NB_BUCKET - 1))


def shape_constants():
    c = np.zeros((P, NCONST), np.float32)
    c[:, C_ID:C_ID + P] = np.eye(P)
    row = np.arange(P)
    b4, q = row // 32, row % 4
    for g in range(2):
        for b in range(DB):
            for j in range(DS):
                seen = (b == 4 * g + b4) & (j <= q)
                c[:, C_OWN + 32 * g + 4 * b + j] = np.where(seen, 0.0, NEG)
    c[:, C_IDX:C_IDX + 4] = np.arange(1, 5)
    c[:, C_FIRST:C_FIRST + 4] = np.arange(4, 0, -1)
    e = np.arange(4)
    c[:, C_TRI:C_TRI + 16] = (e[None, :] < e[:, None]).astype(np.float32).reshape(-1)
    t = np.zeros((P, NTABLE), np.float32)
    for j in range(4):
        n = np.arange(380) - 252 + 128 - j
        t[32 * j + bucket(n)[n >= 0], T_OH4 + np.arange(380)[n >= 0]] = 1
        k = np.arange(PAST)
        t[32 * j + bucket(PAST + j - k), T_OHS + k] = 1
        for b in range(DB):
            for i in range(j + 1):
                t[32 * j + bucket(np.array(j - i)), T_OHS + PAST + 4 * b + i] = 1
    sel = np.zeros((NE, NE, P), np.float32)
    for i in range(NE):
        sel[i, i] = 1
    return c, t, sel.reshape(NE, NE * P)


def unit_order():
    u = [("in_even", n) for n in (0, 1, 2, 4, 3)]
    for g in range(2):
        u += [("K", 4 * g + b) for b in range(4)] + [("V", 4 * g + b) for b in range(4)]
    for l in range(DEPTH):
        if l:
            u += [("in_odd", n) for n in range(4)]
        u += [("out", l, n) for n in range(2)]
        u += [("xkv", l, n) for n in range(4)]
        u += [("xq", l, n) for n in range(2)]
        u += [("mem", l, b) for b in range(DB)]
        u += [("xo", l, n) for n in range(2)]
        u += [("moe", l, n) for n in range(3 * NE)]
    return u


def tile_order():
    t = []

    def add(stage, n, owners):
        t.extend((stage, i, owners[i % len(owners)]) for i in range(n))

    add("x", 8, "vs")
    add("par", 1, "v")
    add("cpar", 1, "v")
    add("state", 4, "vs")
    add("dbias", 4, "v")
    add("sbias", 3, "ssv")
    add("q", 4, "vs")
    add("k", 4, "vs")
    add("v", 3, "vs")
    add("g", 4, "s")
    add("a", 4, "v")
    add("ktok", 3, "vs")
    add("ps", 8, "v")
    add("kt0", 8, "vs")
    add("cnew", 2, "vs")
    for s, i in PTPO:
        t.append((s, i, "vs"[i % 2]))
    for b in (1, 2, 3):
        add(f"kt{b}", 8, "vs")
    add("spt0", 3, "vsv")
    for b in (4, 5, 6, 7):
        add(f"kt{b}", 8, "vs")
    add("cmean", 1, "v")
    add("cvar", 1, "v")
    add("spt1", 3, "vsv")
    for l in range(DEPTH):
        if l:
            add("u", 8, "s")
            add("vv", 8, "s")
            add("vmean", 1, "v")
            add("vvar", 1, "v")
            add("wm", 2, "v")
            add("vtok", 6, "vs")
            add("mix", 8, "v")
        add(f"o{l}", 8, "v")
        add(f"mean{3 * l}", 1, "v")
        add(f"memT{l}", 8, "s")
        add(f"var{3 * l}", 1, "v")
        add(f"mk{l}", 4, "vs")
        add(f"mv{l}", 4, "vs")
        add(f"mktok{l}", 4, "vs")
        add(f"xq{l}", 8, "vs")
        add(f"xs{l}", 4, "s")
        for b in range(4):
            add(f"xkt{l}{b}", 4, "vs")
        for s, i in XPTPO:
            t.append((f"{s}{l}", i, "vs"[i % 2]))
        add(f"xspt{l}0", 1, "v")
        for b in range(4, 8):
            add(f"xkt{l}{b}", 4, "vs")
        add(f"xspt{l}1", 1, "v")
        add(f"xo{l}", 8, "v")
        add(f"mean{3 * l + 1}", 1, "v")
        add(f"var{3 * l + 1}", 1, "v")
        add(f"router{l}", 1, "s")
        add(f"combT{l}", 1, "v")
        add(f"cb{l}", 16, "vs")
        for e in range(NE):
            for j in range(4):
                t.append((f"moe{l}", 16 * e + 2 * j, "s"))
                t.append((f"moe{l}", 16 * e + 2 * j + 1, "v"))
            for j in range(8):
                t.append((f"moe{l}", 16 * e + 8 + j, "v"))
        add(f"mean{3 * l + 2}", 1, "v")
        add(f"var{3 * l + 2}", 1, "v")
    add("y", 6, "vs")
    return t


PTPO = [("pt", 0), ("pt", 1), ("pt", 2), ("pt", 3), ("po", 0), ("pt", 4), ("pt", 5), ("po", 1),
        ("pt", 6), ("pt", 7), ("po", 2), ("po", 3)]
XPTPO = [("xpt", 0), ("xpt", 1), ("xpo", 0), ("xpt", 2), ("xpo", 1), ("xpt", 3), ("xpo", 2), ("xpo", 3)]


def build(nc, x_prompt, x_sample, cache_k, cache_v, state_conv, cache_mem_k, cache_mem_v, page_table,
          mem_prompt, rel_bias, w_in_even, conv_w, conv_b, conv_ln_g, conv_ln_b, w_out_even, w_in_odd,
          sgu_ln_g, sgu_ln_b, sgu_w, sgu_b, w_out_odd, w_xq, w_xkv, w_xo, w_router, router_bias,
          w_exp_gate, w_exp_up, w_exp_down, ln_g, ln_b, const, table, selrow,
          y_prompt, y_sample, new_k_prompt, new_v_prompt, new_k_sample, new_v_sample,
          new_conv_prompt, new_conv_sample, new_mem_k, new_mem_v, new_gmlp_v):
    units = unit_order()
    UIDX = {u: i for i, u in enumerate(units)}
    tiles = tile_order()
    TIDX = {(s, i): n for n, (s, i, _) in enumerate(tiles)}
    OWNER = [o for _, _, o in tiles]
    CUM = {"v": [0], "s": [0]}
    for o in OWNER:
        for k in "vs":
            CUM[k].append(CUM[k][-1] + (o == k))

    with ExitStack() as ctx:
        def sb(name, shape, dt=F32):
            return ctx.enter_context(nc.sbuf_tensor(name, shape, dt))

        def sem(name):
            return ctx.enter_context(nc.semaphore(name))

        ring = sb("ring", [P, SLOTS, UNIT])
        xT = sb("xT", [P, FT, NTOK])
        zT = sb("zT", [P, FT, NTOK])
        mixT = sb("mixT", [P, FT, NTOK])
        qT = sb("qT", [P, FT, NTOK])
        arena = sb("arena", [P, 17408])
        cst = sb("cst", [P, NCONST])
        ones_d = sb("ones_d", [P, P])
        ones_c = sb("ones_c", [P, P])
        parT = sb("parT", [P, FT, 14])
        cparT = sb("cparT", [P, 4, 34])
        wrt = sb("wrt", [P, FT, NE])
        rbias = sb("rbias", [P, NE])
        rs = sb("rs", [P, NTOK])
        std = sb("std", [P, NTOK])
        st = sb("st", [P, 256])
        pages = sb("pages", [1, DB * NPAGE], I32)
        acc = ctx.enter_context(nc.psum_tensor("acc", [P, NACC, 512], F32))
        psS = ctx.enter_context(nc.psum_tensor("psS", [P, 2, 512], F32))
        psN = ctx.enter_context(nc.psum_tensor("psN", [P, 512], F32))
        psV = ctx.enter_context(nc.psum_tensor("psV", [P, 512], F32))

        def view(off, *shape):
            n = int(np.prod(shape))
            v = arena[:, off:off + n]
            if len(shape) == 2:
                return v.rearrange("p (a b) -> p a b", b=shape[1])
            if len(shape) == 3:
                return v.rearrange("p (a b c) -> p a b c", b=shape[1], c=shape[2])
            return v

        ident = cst[:, C_ID:C_ID + P]
        KT = view(0, 2, 4, 512)
        tab = view(0, NTABLE)
        prow = view(1536, 1024)
        crow = view(2560, 512)
        strow = view(3072, 2, 512)
        BIAS = view(4096, 8, 384)
        QBD = arena[:, 4096:5120].rearrange("p (b f m) -> p b f m", f=4, m=32)
        cnew = view(5120, 2, 512)
        SALL = view(7168, 8, 384)
        xtok = view(7168, 3, 1024)
        SS = view(7168, 1056)
        PTS = view(8224, 9, 128)
        UP = view(10240, 4, 286)
        US = view(11384, 4, 8, 34)
        kT = view(12472, 4, NTOK)
        vtok = view(13624, 3, 512)
        SBIAS = view(15160, 1024)
        OBIAS = view(16184, 2, 32)
        PTP = view(16248, 2, 384)
        RB4 = view(17016, 32)
        SBL = view(17048, 128)
        ktok = zT[:, 0:6, :].rearrange("p a b -> p (a b)")[:, 0:1536].rearrange("p (a b) -> p a b", b=512)
        memT = view(0, 8, 256)
        XP = view(0, 2, 256)
        XPTS = view(512, 2, 128)
        mkT = view(2048, 8, 256)
        mvtok = view(4096, 2, 1024)
        mktok = view(6144, 2, 1024)
        PX = view(8192, 8, 256)
        XPT = view(10240, 2, 512)
        QX = arena[:, 11264:13312].rearrange("p (b f m) -> p b f m", f=8, m=32)
        MKT = view(13312, 2, 8, 256)
        memtok = view(13312, 2, 1024)
        CB = view(0, NE, NTOK)
        H = view(4608, 2, 4, NTOK)
        SG = view(6912, 2, 4, NTOK)
        UPC = view(9216, 2, NTOK)
        combT = arena[0:NE, 9792:9792 + NTOK]
        SEL = arena[0:NE, 10080:10080 + NE * P].rearrange("p (e m) -> p e m", e=NE)
        RT = arena[:, 12128:12128 + 672]
        vT = view(0, 8, NTOK)
        gvtok = view(2304, 3, 1024)
        WLD = view(12800, 8, 128)
        BSG = view(13824, 8, 128)
        WBD = arena[0:32, 14848:15104].rearrange("p (g t) -> p g t", g=8)
        WMT = view(15104, 8, 128)
        ytok = view(0, 3, 1024)

        unit_in = [sem(f"unit_in{i}") for i in range(SLOTS)]
        values_used = sem("values_used")
        acc_full = sem("acc_full")
        emptied = {"v": sem("emptied_by_dve"), "s": sem("emptied_by_act")}
        in_x = sem("in_x")
        in_const = sem("in_const")
        in_rows = sem("in_rows")
        in_rb = sem("sample_bias_operand")
        rb_zero = sem("rb_zero")
        rb_in = sem("rb_in")
        in_misc = sem("in_router_bias")
        in_pages = sem("in_pages")
        ones_set = sem("ones_set")
        dve_step = sem("dve_step")
        conv_step = sem("conv_step")
        bias_masked = sem("bias_masked")
        u_pads = sem("u_pads")
        qbd_ready = sem("qbd_ready")
        scores_full = sem("scores_full")
        scores_read = sem("scores_read")
        negmax = sem("negmax")
        exp_done = sem("exp_done")
        probs = sem("probs")
        smp_out = sem("smp_out")
        smp_read = sem("smp_read")
        centered = sem("centered")
        squared = sem("squared")
        std_ready = sem("std_ready")
        scaled = sem("scaled")
        x_ready = sem("x_ready")
        cen_c = None
        sq_c = sem("conv_squared")
        std_c = sem("conv_std")
        scl_c = sem("conv_scaled")
        cv_ready = sem("conv_ready")
        cen_v = sem("v_centered")
        sq_v = sem("v_squared")
        std_v = sem("v_std")
        scl_v = sem("v_scaled")
        vn_ready = sem("v_ready")
        mem_in = sem("mem_in")
        qx_ready = sem("qx_ready")
        sel_in = sem("sel_in")
        comb_ready = sem("comb_ready")
        z_init = sem("z_init")
        h_ready = sem("h_ready")
        g_in = sem("gmlp_in")
        wbd_zero = sem("wbd_zero")
        wbd_in = sem("wbd_in")
        w_masked = sem("w_masked")
        mixed = sem("mixed")
        out_even = sem("out_even")
        out_mem = sem("out_mem")
        out_rest = sem("out_rest")

        kt_read = sem("kt_read")
        xk_read = sem("xk_read")
        ucmp = sb("ucmp", [P, 4, 32])

        def ACC(stage, i):
            return acc[:, TIDX[stage, i] % NACC, :]

        def full(eng, stage, i):
            eng.wait_ge(acc_full, TIDX[stage, i] + 1)

        def bank_free(pe, stage, i):
            n = TIDX[stage, i] - NACC
            if n >= 0:
                o = OWNER[n]
                pe.wait_ge(emptied[o], CUM[o][n + 1])

        def evacuated(eng, stage, i):
            n = TIDX[stage, i]
            eng.wait_ge(emptied[OWNER[n]], CUM[OWNER[n]][n + 1])

        def owned(who, stage, n):
            return [i for i in range(n) if OWNER[TIDX[stage, i]] == who]

        def slot(u):
            return ring[:, u % SLOTS, :]

        LANDED = []
        total = [0] * SLOTS
        for n, k in enumerate(units):
            total[n % SLOTS] += 16 * (8 if k[0] in "KV" else 2 if k[0] == "mem" else 1)
            LANDED.append(total[n % SLOTS])

        def arrived(eng, u, more=0):
            eng.wait_ge(unit_in[u % SLOTS], LANDED[u] + more)

        def xr(nth):
            return 8 * (nth + 1)

        READER = {("in_even", 0): ("q", 3), ("in_even", 1): ("k", 3), ("in_even", 2): ("v", 2),
                  ("in_even", 4): ("g", 3), ("in_even", 3): ("a", 3)}
        for b in range(DB):
            READER["K", b] = (f"kt{b}", 7)
        for n in range(4):
            READER["in_odd", n] = (("u", "vv")[n // 2], 4 * (n % 2) + 3)
        for l in range(DEPTH):
            for n in range(2):
                READER["out", l, n] = (f"o{l}", 4 * n + 3)
                READER["xq", l, n] = (f"xq{l}", 4 * n + 3)
                READER["xo", l, n] = (f"xo{l}", 4 * n + 3)
                READER["xkv", l, n] = (f"mk{l}", 2 * n + 1)
                READER["xkv", l, 2 + n] = (f"mv{l}", 2 * n + 1)
            for e in range(NE):
                for n, t in enumerate((6, 7, 15)):
                    READER["moe", l, 3 * e + n] = (f"moe{l}", 16 * e + t)

        def slot_free(sp, u):
            if u < SLOTS:
                return
            k = units[u - SLOTS]
            if k[0] in ("V", "mem"):
                sp.wait_ge(values_used, 1 + (k[1] if k[0] == "V" else DB * (1 + k[1]) + k[2]))
            else:
                sp.wait_ge(acc_full, TIDX[READER[k]] + 1)

        block = ctx.enter_context(nc.Block())

        @block.sync
        def _(sp):
            sp.dma_start(xtok[:, 0:2, :], x_prompt[0].rearrange("(t p) d -> p t d", p=P)).then_inc(in_x, 16)
            sp.dma_start(xtok[0:32, 2, :], x_sample.rearrange("b s d -> (b s) d")).then_inc(in_x, 16)
            sp.dma_start(pages[:, :], page_table.rearrange("(a b) n -> a (b n)", a=1)).then_inc(in_pages, 16)

            def mat(w, n):
                return w[:, 512 * n:512 * n + 512].rearrange("(k p) n -> p k n", p=P)

            def load(u, dst8):
                kind = units[u]
                s = unit_in[u % SLOTS]
                if kind[0] in "KV":
                    cache = cache_k if kind[0] == "K" else cache_v
                    for p in range(NPAGE):
                        at = kind[1] * NPAGE + p
                        page = sp.value_load(pages[0:1, at:at + 1], min_val=0, max_val=NPHYS - 1)
                        sp.dma_start(dst8[:, p, :],
                                     cache[0, bass.ds(page, 1)].rearrange("a t h d -> (a t) (h d)")).then_inc(s, 16)
                    return
                if kind[0] == "mem":
                    _, l, b = kind
                    d2 = slot(u).rearrange("p (c t n) -> p c t n", c=2, n=1024)
                    for i, m in enumerate((cache_mem_k, cache_mem_v)):
                        sp.dma_start(d2[:, i], m[l, b].rearrange("(t p) h d -> p t (h d)", p=P)).then_inc(s, 16)
                    return
                if kind[0] == "in_even":
                    src = mat(w_in_even[0], kind[1])
                elif kind[0] == "in_odd":
                    src = mat(w_in_odd[0], kind[1])
                else:
                    _, l, n = kind
                    src = mat({"out": (w_out_even, w_out_odd)[l][0], "xkv": w_xkv[l], "xq": w_xq[l],
                               "xo": w_xo[l]}[kind[0]], n)
                sp.dma_start(dst8, src).then_inc(s, 16)

            u = 0
            while u < len(units):
                if units[u][0] == "K" and units[u][1] == 0:
                    sp.wait_ge(in_pages, 16)
                if units[u][0] != "moe":
                    slot_free(sp, u)
                    load(u, slot(u).rearrange("p (k n) -> p k n", k=8))
                    u += 1
                    continue
                l = units[u][1]

                def expert_pair(i, first):
                    for j in range(6):
                        if first:
                            slot_free(sp, u + j)
                        else:
                            sp.wait_ge(acc_full, TIDX[READER[units[u + j]]] + 1 - 32 + 32 * i)
                        e = 2 * i + j // 3
                        w = (w_exp_gate, w_exp_up, w_exp_down)[j % 3]
                        k = 8 if j % 3 < 2 else 4
                        sp.dma_start(slot(u + j).rearrange("p (k n) -> p k n", k=k),
                                     w[l, bass.ds(e, 1)].rearrange("a (k p) n -> p (a k) n", p=P))\
                          .then_inc(unit_in[(u + j) % SLOTS], 16)

                expert_pair(0, True)
                with sp.Fori(1, NE // 2) as i:
                    expert_pair(i, False)
                u += 3 * NE

        @block.tensor
        def _(pe):
            def mm(out, lhsT, rhs, first, last):
                return pe.matmul(out, lhsT, rhs, start=first, stop=last)

            def project(stage, u, rhs, j0, ready=None, cols=NTOK):
                W = slot(u).rearrange("p (k n) -> p k n", k=8)
                arrived(pe, u)
                for j in range(4):
                    bank_free(pe, stage, j0 + j)
                    for k in range(8):
                        if ready and j == 0:
                            ready(k)
                        last = mm(ACC(stage, j0 + j)[:, 0:cols], W[:, k, P * j:P * j + P], rhs[:, k, :], k == 0, k == 7)
                    last.then_inc(acc_full, 1)

            def mean_tile(stage, zz, ones, n, ready):
                bank_free(pe, stage, 0)
                for k in range(n):
                    ready(k)
                    last = mm(ACC(stage, 0)[:, 0:NTOK], ones[:, :], zz[:, k, :], k == 0, k == n - 1)
                last.then_inc(acc_full, 1)

            pe.wait_ge(in_const, 32)
            pe.wait_ge(in_x, 32)
            for i in range(8):
                bank_free(pe, "x", i)
                for t in range(3):
                    n = P if t < 2 else 32
                    last = pe.transpose(ACC("x", i)[:, P * t:P * t + n], xtok[0:n, t, P * i:P * i + P], ident[0:n, 0:n])
                last.then_inc(acc_full, 1)
            pe.wait_ge(in_rows, 16 * 11)
            bank_free(pe, "par", 0)
            for i in range(8):
                last = pe.transpose(ACC("par", 0)[:, 14 * i:14 * i + 14], prow[0:14, P * i:P * i + P], ident[0:14, 0:14])
            last.then_inc(acc_full, 1)
            bank_free(pe, "cpar", 0)
            for i in range(4):
                last = pe.transpose(ACC("cpar", 0)[:, 34 * i:34 * i + 34], crow[0:34, P * i:P * i + P], ident[0:34, 0:34])
            last.then_inc(acc_full, 1)
            for i in range(4):
                bank_free(pe, "state", i)
                for t in range(2):
                    last = pe.transpose(ACC("state", i)[:, 120 * t:120 * t + 120], strow[0:120, t, P * i:P * i + P],
                                        ident[0:120, 0:120])
                last.then_inc(acc_full, 1)
            pe.wait_ge(rb_in, 64)
            for i in range(4):
                bank_free(pe, "dbias", i)
                for t in range(16):
                    w = 252 - 4 * (16 * i + t)
                    last = mm(ACC("dbias", i)[:, 32 * t:32 * t + 32], tab[:, T_OH4 + w:T_OH4 + w + P], RB4, True, True)
                last.then_inc(acc_full, 1)
            pe.wait_ge(in_rb, 1)
            for i in range(3):
                n = 512 if i < 2 else 32
                bank_free(pe, "sbias", i)
                mm(ACC("sbias", i)[:, 0:n], SBL, tab[:, T_OHS + 512 * i:T_OHS + 512 * i + n], True, True)\
                    .then_inc(acc_full, 1)

            for i in range(8):
                evacuated(pe, "x", i)
            project("q", 0, xT, 0)
            project("k", 1, xT, 0)
            arrived(pe, 2)
            W = slot(2).rearrange("p (k n) -> p k n", k=8)
            for t in range(3):
                n = P if t < 2 else 32
                bank_free(pe, "v", t)
                for k in range(8):
                    last = mm(ACC("v", t)[0:n, :], xT[:, k, P * t:P * t + n], W[:, k, :], k == 0, k == 7)
                last.then_inc(acc_full, 1)
            project("g", 3, xT, 0)
            project("a", 4, xT, 0)
            for t in range(3):
                n = P if t < 2 else 32
                bank_free(pe, "ktok", t)
                for f in range(4):
                    evacuated(pe, "k", f)
                    last = pe.transpose(ACC("ktok", t)[0:n, P * f:P * f + P], kT[:, f, P * t:P * t + n], ident)
                last.then_inc(acc_full, 1)

            for h in range(8):
                r = slice(64 * (h % 2), 64 * (h % 2) + 64)
                evacuated(pe, "q", h // 2)
                bank_free(pe, "ps", h)
                mm(ACC("ps", h)[:, 0:128], qT[r, h // 2, 0:128], kT[r, h // 2, 0:128], True, True)
                mm(ACC("ps", h)[:, 128:384], qT[r, h // 2, 128:256], kT[r, h // 2, 0:256], True, True)\
                    .then_inc(acc_full, 1)

            def sample_keys(b):
                u = UIDX["K", b]
                K = slot(u).rearrange("p (k n) -> p k n", k=8)
                arrived(pe, u)
                g, b4 = b // 4, b % 4
                rows = slice(32 * b4, 32 * b4 + 32)
                if b4 == 0 and g:
                    pe.wait_ge(scores_read, 1)
                if b == 0:
                    pe.wait_ge(qbd_ready, 1)
                for half in range(2):
                    for f in range(4):
                        i = 4 * half + f
                        bank_free(pe, f"kt{b}", i)
                        for p in range(4):
                            last = pe.transpose(ACC(f"kt{b}", i)[:, P * p:P * p + P],
                                                K[:, 4 * half + p, P * f:P * f + P], ident)
                        last.then_inc(acc_full, 1)
                    for f in range(4):
                        evacuated(pe, f"kt{b}", 4 * half + f)
                        mm(psS[rows, half, :], QBD[:, b, f, :], KT[:, half, f, :], f == 0, f == 3)\
                            .then_inc(kt_read, 1)
                for f in range(4):
                    last = mm(psN[rows, 0:32], QBD[:, b, f, :], kT[:, f, S0:NTOK], f == 0, f == 3)
                if b4 == 3:
                    last.then_inc(scores_full, 1)

            def sample_values(g):
                pe.wait_ge(probs, 1 + 1 + g)
                for i in range(3):
                    bank_free(pe, f"spt{g}", i)
                    if i < 2:
                        for c in range(4):
                            k = 4 * i + c
                            last = pe.transpose(ACC(f"spt{g}", i)[:, P * c:P * c + P], SS[:, P * k:P * k + P], ident)
                    else:
                        last = pe.transpose(ACC(f"spt{g}", i)[0:32, 0:P], SS[:, PAST:PAST + 32], ident)
                    last.then_inc(acc_full, 1)
                for i in range(3):
                    evacuated(pe, f"spt{g}", i)
                for b4 in range(4):
                    b = 4 * g + b4
                    u = UIDX["V", b]
                    V = slot(u).rearrange("p (k n) -> p k n", k=8)
                    arrived(pe, u)
                    for f in range(4):
                        out = psV[:, 32 * b + 8 * f:32 * b + 8 * f + 8]
                        c = 32 * b4 + 8 * f
                        for k in range(8):
                            last = mm(out, V[:, k, P * f:P * f + P], PTS[:, k, c:c + 8], k == 0, False)
                        if f == 3:
                            last.then_inc(values_used, 1)
                        last = mm(out, vtok[0:32, 2, P * f:P * f + P], PTS[0:32, 8, c:c + 8], False, True)
                    if b4 == 3:
                        last.then_inc(smp_out, 1)

            sample_keys(0)
            evacuated(pe, "a", 3)
            for i in range(2):
                n = 30 if i == 0 else 32
                bank_free(pe, "cnew", i)
                for f in range(4):
                    src = UP[:, f, 256:286] if i == 0 else ucmp[:, f, :]
                    last = pe.transpose(ACC("cnew", i)[0:n, P * f:P * f + P], src, ident)
                last.then_inc(acc_full, 1)
            pe.wait_ge(probs, 1)
            for s, i in PTPO:
                bank_free(pe, s, i)
                if s == "pt":
                    for c in range(3):
                        last = pe.transpose(ACC(s, i)[:, P * c:P * c + P], SALL[:, i, P * c:P * c + P], ident)
                else:
                    for h in (2 * i, 2 * i + 1):
                        evacuated(pe, "pt", h)
                        if i == 0:
                            evacuated(pe, "v", 0), evacuated(pe, "v", 1), evacuated(pe, "v", 2)
                        o = ACC(s, i)[64 * (h % 2):64 * (h % 2) + 64, :]
                        mm(o[:, 0:256], vtok[:, 0, 64 * h:64 * h + 64], PTP[:, h % 2, 0:256], True, False)
                        last = mm(o[:, 128:256], vtok[:, 1, 64 * h:64 * h + 64], PTP[:, h % 2, 256:384], False, True)
                last.then_inc(acc_full, 1)
            for b in (1, 2, 3):
                sample_keys(b)
            sample_values(0)
            for b in (4, 5, 6, 7):
                sample_keys(b)
            mean_tile("cmean", mixT[:, 4:8, :], ones_c, 4, lambda k: pe.wait_ge(conv_step, 8 * (CW - 1) + 2 * k + 2))
            mean_tile("cvar", zT, ones_c, 4, lambda k: pe.wait_ge(sq_c, 1))
            sample_values(1)

            def cross(l):
                nth = 3 * l + 1
                u0 = UIDX["xkv", l, 0]
                def mem_keys(i):
                    u = u0 + i // 2
                    W = slot(u).rearrange("p (k n) -> p k n", k=8)
                    arrived(pe, u)
                    bank_free(pe, f"mk{l}", i)
                    for c in range(2):
                        j = 2 * (i % 2) + c
                        for k in range(8):
                            last = mm(ACC(f"mk{l}", i)[:, 256 * c:256 * c + 256], W[:, k, P * j:P * j + P],
                                      memT[:, k, :], k == 0, k == 7)
                    last.then_inc(acc_full, 1)

                mean_tile(f"mean{3 * l}", zT, ones_d, 8, lambda k: evacuated(pe, f"o{l}", k))
                pe.wait_ge(mem_in, 16 * (l + 1))
                for i in range(8):
                    bank_free(pe, f"memT{l}", i)
                    for t in range(2):
                        last = pe.transpose(ACC(f"memT{l}", i)[:, P * t:P * t + P], memtok[:, t, P * i:P * i + P], ident)
                    last.then_inc(acc_full, 1)
                mean_tile(f"var{3 * l}", mixT, ones_d, 8, lambda k: pe.wait_ge(squared, 4 * 3 * l + k // 2 + 1))
                for i in range(8):
                    evacuated(pe, f"memT{l}", i)
                for i in range(4):
                    mem_keys(i)
                for i in range(4):
                    n, t = i // 2, i % 2
                    u = u0 + 2 + n
                    W = slot(u).rearrange("p (k n) -> p k n", k=8)
                    arrived(pe, u)
                    bank_free(pe, f"mv{l}", i)
                    for k in range(8):
                        last = mm(ACC(f"mv{l}", i), memT[:, k, P * t:P * t + P], W[:, k, :], k == 0, k == 7)
                    last.then_inc(acc_full, 1)
                for i in range(4):
                    t, n = i // 2, i % 2
                    bank_free(pe, f"mktok{l}", i)
                    for f in range(4):
                        evacuated(pe, f"mk{l}", (4 * n + f) // 2)
                        last = pe.transpose(ACC(f"mktok{l}", i)[:, P * f:P * f + P],
                                            mkT[:, 4 * n + f, P * t:P * t + P], ident)
                    last.then_inc(acc_full, 1)
                for n in range(2):
                    project(f"xq{l}", UIDX["xq", l, n], xT, 4 * n,
                            lambda k: pe.wait_ge(x_ready, xr(3 * l - 1) + k + 1))
                for h in range(4):
                    evacuated(pe, f"xq{l}", 2 * h), evacuated(pe, f"xq{l}", 2 * h + 1)
                    bank_free(pe, f"xs{l}", h)
                    for t in range(2):
                        for c in range(2):
                            last = mm(ACC(f"xs{l}", h)[:, 256 * t:256 * t + 256], qT[:, 2 * h + c, P * t:P * t + P],
                                      mkT[:, 2 * h + c, :], c == 0, c == 1)
                    last.then_inc(acc_full, 1)

                def keys(b):
                    u = UIDX["mem", l, b]
                    K = slot(u).rearrange("p (c t n) -> p c t n", c=2, n=1024)[:, 0]
                    arrived(pe, u)
                    b4 = b % 4
                    if b == 0:
                        pe.wait_ge(qx_ready, l + 1)
                    if b == 4:
                        pe.wait_ge(exp_done, 26 + 2 * l + 1)
                    for i in range(4):
                        bank_free(pe, f"xkt{l}{b}", i)
                        for c in range(4):
                            f, t = 2 * i + c // 2, c % 2
                            last = pe.transpose(ACC(f"xkt{l}{b}", i)[:, P * c:P * c + P], K[:, t, P * f:P * f + P], ident)
                        last.then_inc(acc_full, 1)
                    for f in range(8):
                        evacuated(pe, f"xkt{l}{b}", f // 2)
                        last = mm(psS[32 * b4:32 * b4 + 32, 0, 0:256], QX[:, b, f, :], MKT[:, b % 2, f, :], f == 0, f == 7)
                    last.then_inc(xk_read, 1)

                def values(g):
                    bank_free(pe, f"xspt{l}{g}", 0)
                    pe.wait_ge(probs, 3 + (DEPTH + 1) * l + 1 + g + 1)
                    for t in range(2):
                        last = pe.transpose(ACC(f"xspt{l}{g}", 0)[:, P * t:P * t + P], XP[:, g, P * t:P * t + P], ident)
                    last.then_inc(acc_full, 1)
                    evacuated(pe, f"xspt{l}{g}", 0)
                    if g == 0:
                        pe.wait_ge(smp_read, 2 + l)
                    for b4 in range(4):
                        b = 4 * g + b4
                        u = UIDX["mem", l, b]
                        V = slot(u).rearrange("p (c t n) -> p c t n", c=2, n=1024)[:, 1]
                        for f in range(8):
                            for t in range(2):
                                c = 32 * b4 + 4 * (f // 2)
                                last = mm(psV[:, 32 * b + 4 * f:32 * b + 4 * f + 4], V[:, t, P * f:P * f + P],
                                          XPTS[:, t, c:c + 4], t == 0, t == 1)
                        last.then_inc(values_used, 1)

                for b in range(4):
                    keys(b)
                pe.wait_ge(probs, 3 + (DEPTH + 1) * l + 1)
                for s, i in XPTPO:
                    bank_free(pe, f"{s}{l}", i)
                    if s == "xpt":
                        for c in range(4):
                            kt, t = c // 2, c % 2
                            last = pe.transpose(ACC(f"xpt{l}", i)[:, P * c:P * c + P], PX[:, 2 * i + t, P * kt:P * kt + P], ident)
                    else:
                        evacuated(pe, f"xpt{l}", i)
                        if i == 0:
                            for n in range(4):
                                evacuated(pe, f"mv{l}", n)
                        for c in range(2):
                            for kt in range(2):
                                w = 256 * i + P * c
                                last = mm(ACC(f"xpo{l}", i)[:, 256 * c:256 * c + 256], mvtok[:, kt, w:w + P],
                                          XPT[:, i % 2, 256 * kt:256 * kt + 256], kt == 0, kt == 1)
                    last.then_inc(acc_full, 1)
                values(0)
                for b in range(4, 8):
                    keys(b)
                values(1)
                pe.wait_ge(smp_read, 3 + l)
                for i in range(4):
                    evacuated(pe, f"xpo{l}", i)
                for n in range(2):
                    project(f"xo{l}", UIDX["xo", l, n], mixT, 4 * n)
                mean_tile(f"mean{nth}", zT, ones_d, 8, lambda k: evacuated(pe, f"xo{l}", k))
                mean_tile(f"var{nth}", mixT, ones_d, 8, lambda k: pe.wait_ge(squared, 4 * nth + k // 2 + 1))

            def experts(l):
                bank_free(pe, f"router{l}", 0)
                for t in range(3):
                    a = min(P * t, NTOK - P)
                    for k in range(8):
                        if t == 0:
                            pe.wait_ge(x_ready, xr(3 * l) + k + 1)
                        last = mm(ACC(f"router{l}", 0)[:, NE * t:NE * t + NE], xT[:, k, a:a + P], wrt[:, k, :], k == 0, k == 7)
                last.then_inc(acc_full, 1)
                pe.wait_ge(comb_ready, l + 1)
                bank_free(pe, f"combT{l}", 0)
                for t in range(3):
                    a = min(P * t, NTOK - P)
                    last = pe.transpose(ACC(f"combT{l}", 0)[0:NE, a:a + P], RT[:, 16 * t:16 * t + 16], ident)
                last.then_inc(acc_full, 1)
                pe.wait_ge(sel_in, 16 * (l + 1))
                evacuated(pe, f"combT{l}", 0)
                for e in range(NE):
                    bank_free(pe, f"cb{l}", e)
                    mm(ACC(f"cb{l}", e)[:, 0:NTOK], SEL[:, e, :], combT, True, True).then_inc(acc_full, 1)
                for e in range(NE):
                    evacuated(pe, f"cb{l}", e)
                t0 = TIDX[f"moe{l}", 0]
                u0 = UIDX["moe", l, 0]
                with pe.Fori(0, NE // 2) as i:
                    def free(n):
                        if n < NACC:
                            pe.wait_ge(emptied["v"], CUM["v"][t0] - (NACC - 1 - n) + 24 * i)
                        else:
                            o = OWNER[t0 + n - NACC]
                            pe.wait_ge(emptied[o], CUM[o][t0 + n - NACC + 1] + (24 if o == "v" else 8) * i)

                    def bank(n):
                        return acc[:, (t0 + n) % NACC, 0:NTOK]

                    for e in range(2):
                        Wg = slot(u0 + 3 * e).rearrange("p (k n) -> p k n", k=8)
                        Wu = slot(u0 + 3 * e + 1).rearrange("p (k n) -> p k n", k=8)
                        Wd = slot(u0 + 3 * e + 2).rearrange("p (k n) -> p k n", k=4)
                        arrived(pe, u0 + 3 * e, 16 * i)
                        for j in range(4):
                            for c, W in enumerate((Wg, Wu)):
                                n = 16 * e + 2 * j + c
                                free(n)
                                if j == 0 and c == 1:
                                    arrived(pe, u0 + 3 * e + 1, 16 * i)
                                for k in range(8):
                                    last = mm(bank(n), W[:, k, P * j:P * j + P], xT[:, k, :], k == 0, k == 7)
                                last.then_inc(acc_full, 1)
                        arrived(pe, u0 + 3 * e + 2, 16 * i)
                        for j in range(8):
                            n = 16 * e + 8 + j
                            free(n)
                            for k in range(4):
                                if j == 0:
                                    pe.wait_ge(h_ready, 4 * NE * l + 4 * e + k + 1 + 8 * i)
                                last = mm(bank(n), Wd[:, k, P * j:P * j + P], H[:, e, k, :], k == 0, k == 3)
                            last.then_inc(acc_full, 1)
                nth = 3 * l + 2
                last_moe = 16 * NE - 8
                mean_tile(f"mean{nth}", zT, ones_d, 8, lambda k: evacuated(pe, f"moe{l}", last_moe + k))
                mean_tile(f"var{nth}", mixT, ones_d, 8, lambda k: pe.wait_ge(squared, 4 * nth + k // 2 + 1))

            for l in range(DEPTH):
                if l:
                    for n in range(2):
                        project("u", UIDX["in_odd", n], xT, 4 * n, lambda k: pe.wait_ge(x_ready, xr(2)))
                    for n in range(2):
                        project("vv", UIDX["in_odd", 2 + n], xT, 4 * n)
                    mean_tile("vmean", vT, ones_d, 8, lambda k: evacuated(pe, "vv", k))
                    mean_tile("vvar", mixT, ones_d, 8, lambda k: pe.wait_ge(sq_v, k // 2 + 1))
                    pe.wait_ge(w_masked, 1)
                    for i in range(2):
                        bank_free(pe, "wm", i)
                        for g in range(4):
                            last = pe.transpose(ACC("wm", i)[:, P * g:P * g + P], WLD[:, 4 * i + g, :], ident)
                        last.then_inc(acc_full, 1)
                    for i in range(6):
                        t, half = i // 2, i % 2
                        n = P if t < 2 else 32
                        bank_free(pe, "vtok", i)
                        for f in range(4):
                            if i < 2:
                                pe.wait_ge(vn_ready, 4 * half + f + 1)
                            last = pe.transpose(ACC("vtok", i)[0:n, P * f:P * f + P],
                                                vT[:, 4 * half + f, P * t:P * t + n], ident)
                        last.then_inc(acc_full, 1)
                    for i in range(6):
                        evacuated(pe, "vtok", i)
                    evacuated(pe, "wm", 1)
                    pe.wait_ge(w_masked, 2)
                    for g in range(8):
                        bank_free(pe, "mix", g)
                        for t in range(2):
                            mm(ACC("mix", g)[:, P * t:P * t + P], gvtok[:, t, P * g:P * g + P], WMT[:, g, :], True, True)
                        mm(ACC("mix", g)[:, S0:NTOK], gvtok[0:32, 2, P * g:P * g + P], WBD[:, g, :], True, True)\
                            .then_inc(acc_full, 1)
                if l:
                    pe.wait_ge(mixed, 8)
                else:
                    pe.wait_ge(smp_read, 2)
                    pe.wait_ge(cv_ready, 4)
                    for i in range(4):
                        evacuated(pe, "po", i)
                for n in range(2):
                    project(f"o{l}", UIDX["out", l, n], mixT, 4 * n)
                cross(l)
                experts(l)
            pe.wait_ge(x_ready, xr(5))
            for i in range(6):
                t, half = i // 2, i % 2
                n = P if t < 2 else 32
                bank_free(pe, "y", i)
                for f in range(4):
                    last = pe.transpose(ACC("y", i)[0:n, P * f:P * f + P], xT[:, 4 * half + f, P * t:P * t + n], ident)
                last.then_inc(acc_full, 1)

        def evac(eng, who, stage, n, body):
            for i in owned(who, stage, n):
                full(eng, stage, i)
                body(i, ACC(stage, i)).then_inc(emptied[who], 1)

        def copier(eng, who):
            if who == "v":
                return eng.tensor_copy
            return lambda out, in_: eng.activation(out, in_, ACT.Copy)

        def scaler(eng, who):
            if who == "v":
                return lambda out, in_, c: eng.tensor_scalar(out, in_, c, None, ALU.mult)
            return lambda out, in_, c: eng.activation(out, in_, ACT.Copy, scale=c)

        def common(eng, who, between=lambda: None):
            copy, scale = copier(eng, who), scaler(eng, who)

            def rows(i):
                return P if i < 2 else 32

            def xkt(l, b):
                def body(i, a):
                    if b >= 2:
                        eng.wait_ge(xk_read, 8 * l + b - 1)
                    elif l and b < 2:
                        eng.wait_ge(xk_read, 8 * l)
                    return copy(MKT[:, b % 2, 2 * i:2 * i + 2, :], a.rearrange("p (f m) -> p f m", f=2))
                evac(eng, who, f"xkt{l}{b}", 4, body)

            def kt(b):
                def body(i, a):
                    between()
                    if b:
                        eng.wait_ge(kt_read, 8 * (b - 1) + i + 1)
                    return copy(KT[:, i // 4, i % 4, :], a)
                evac(eng, who, f"kt{b}", 8, body)

            return dict(
                x=lambda: evac(eng, who, "x", 8, lambda i, a: copy(xT[:, i, :], a[:, 0:NTOK])),
                state=lambda: evac(eng, who, "state", 4, lambda i, a: copy(
                    US[:, i, :, 0:30], a[:, 0:240].rearrange("p (b t) -> p b t", b=8))),
                q=lambda: evac(eng, who, "q", 4, lambda i, a: scale(qT[:, i, :], a[:, 0:NTOK], HD ** -0.5)),
                k=lambda: evac(eng, who, "k", 4, lambda i, a: copy(kT[:, i, :], a[:, 0:NTOK])),
                v=lambda: evac(eng, who, "v", 3, lambda i, a: copy(vtok[0:rows(i), i, :], a[0:rows(i), :])),
                ktok=lambda: evac(eng, who, "ktok", 3, lambda i, a: copy(ktok[0:rows(i), i, :], a[0:rows(i), :])),
                cnew=lambda: evac(eng, who, "cnew", 2, lambda i, a: copy(
                    cnew[0:30 + 2 * i, i, :], a[0:30 + 2 * i, :])),
                kt=kt,
                spt=lambda g: evac(eng, who, f"spt{g}", 3, lambda i, a: (
                    copy(PTS[:, 4 * i:4 * i + 4, :], a.rearrange("p (k m) -> p k m", k=4)) if i < 2 else
                    copy(PTS[0:32, 8, :], a[0:32, 0:P]))),
                mk=lambda l: evac(eng, who, f"mk{l}", 4, lambda i, a: copy(
                    mkT[:, 2 * i:2 * i + 2, :], a.rearrange("p (f m) -> p f m", f=2))),
                mv=lambda l: evac(eng, who, f"mv{l}", 4, lambda i, a: copy(
                    mvtok[:, i % 2, 512 * (i // 2):512 * (i // 2) + 512], a)),
                mktok=lambda l: evac(eng, who, f"mktok{l}", 4, lambda i, a: copy(
                    mktok[:, i // 2, 512 * (i % 2):512 * (i % 2) + 512], a)),
                xq=lambda l: evac(eng, who, f"xq{l}", 8, lambda i, a: scale(qT[:, i, :], a[:, 0:NTOK], HDX ** -0.5)),
                xkt=xkt,
                cb=lambda l: evac(eng, who, f"cb{l}", 16, lambda i, a: copy(CB[:, i, :], a[:, 0:NTOK])),
                vtok=lambda: evac(eng, who, "vtok", 6, lambda i, a: copy(
                    gvtok[0:rows(i // 2), i // 2, 512 * (i % 2):512 * (i % 2) + 512], a[0:rows(i // 2), :])),
                y=lambda: evac(eng, who, "y", 6, lambda i, a: copy(
                    ytok[0:rows(i // 2), i // 2, 512 * (i % 2):512 * (i % 2) + 512], a[0:rows(i // 2), :])),
            )

        def ptpo(eng, who, table, l=None):
            copy = copier(eng, who)
            for s, i in table:
                stage = s if l is None else f"{s}{l}"
                if OWNER[TIDX[stage, i]] != who:
                    continue
                full(eng, stage, i)
                a = ACC(stage, i)
                if s == "pt":
                    if i >= 2:
                        full(eng, "po", i // 2 - 1)
                    ins = copy(PTP[:, i % 2, :], a[:, 0:384])
                elif s == "po":
                    ins = copy(mixT[:, i, 0:SEQ], a[:, 0:SEQ])
                elif s == "xpt":
                    if i >= 2:
                        full(eng, f"xpo{l}", i - 2)
                    ins = copy(XPT[:, i % 2, :], a)
                else:
                    ins = copy(mixT[:, 2 * i:2 * i + 2, 0:SEQ], a.rearrange("p (f q) -> p f q", f=2))
                ins.then_inc(emptied[who], 1)

        @block.vector
        def _(dve):
            steps = [0]

            def link(ins):
                steps[0] += 1
                ins.then_inc(dve_step, 1)
                dve.wait_ge(dve_step, steps[0])

            taps = [(w, f, part) for w in range(CW) for f in range(4) for part in range(2)]

            def conv_taps(n):
                for _ in range(min(n, len(taps) - done[0])):
                    w, f, part = taps[done[0]]
                    y = mixT[:, 4 + f, 0:SEQ] if part == 0 else mixT[:, 4 + f, S0:NTOK].rearrange("p (b s) -> p b s", b=8)
                    u = UP[:, f, w:w + SEQ] if part == 0 else US[:, f, :, w:w + DS]
                    tap = cparT[:, f, w:w + 1]
                    if w:
                        dve.wait_ge(conv_step, done[0] - 7)
                        ins = dve.scalar_tensor_tensor(out=y, in0=u, scalar=tap, in1=y, op0=ALU.mult, op1=ALU.add)
                    else:
                        ins = dve.tensor_scalar(y, u, tap, cparT[:, f, 31:32], ALU.mult, ALU.add)
                    ins.then_inc(conv_step, 1)
                    done[0] += 1

            done = [0]
            cm = common(dve, "v", lambda: conv_taps(8))
            dve.memset(ones_d[:, :], 1.0 / D).then_inc(ones_set, 1)
            dve.memset(ones_c[:, :], 1.0 / CC).then_inc(ones_set, 1)
            dve.memset(RB4, 0.0).then_inc(rb_zero, 1)
            cm["x"]()
            full(dve, "par", 0)
            dve.tensor_copy(parT[:, :, :], ACC("par", 0)[:, 0:112].rearrange("p (f c) -> p f c", f=8)).then_inc(emptied["v"], 1)
            full(dve, "cpar", 0)
            dve.tensor_copy(cparT[:, :, :], ACC("cpar", 0)[:, 0:136].rearrange("p (f c) -> p f c", f=4)).then_inc(emptied["v"], 1)
            dve.memset(UP[:, :, 0:30], 0.0).then_inc(u_pads, 1)
            dve.wait_ge(rb_in, 64)
            src = RB4.rearrange("p (q h) -> p h q", q=4)
            for b in range(4):
                last = dve.tensor_copy(SBL[:, 32 * b:32 * b + 32].rearrange("p (h q) -> p h q", q=4), src)
            last.then_inc(in_rb, 1)
            cm["state"]()
            for i in range(4):
                full(dve, "dbias", i)
                a = ACC("dbias", i).rearrange("p (m h) -> p h m", h=8)
                ins = dve.tensor_copy(BIAS[:, :, 128 + 64 * i:192 + 64 * i], a)
                if i >= 2:
                    ins = dve.tensor_copy(BIAS[:, :, 64 * i - 128:64 * i - 64], a)
                ins.then_inc(emptied["v"], 1)
            full(dve, "sbias", 2)
            for g in range(2):
                last = dve.tensor_tensor(OBIAS[:, g, :], ACC("sbias", 2)[:, 0:32],
                                         cst[:, C_OWN + 32 * g:C_OWN + 32 * g + 32], ALU.add)
            last.then_inc(emptied["v"], 1)
            cm["q"]()
            cm["k"]()
            cm["v"]()
            for i in range(4):
                evacuated(dve, "g", i)
                full(dve, "a", i)
                a = ACC("a", i)
                dve.tensor_tensor(UP[:, i, 30:286], a[:, 0:SEQ], zT[:, i, 0:SEQ], ALU.mult)
                dve.tensor_tensor(ucmp[:, i, :], a[:, S0:NTOK], zT[:, i, S0:NTOK], ALU.mult)
                dve.tensor_tensor(US[:, i, :, 30:34], a[:, S0:NTOK].rearrange("p (b s) -> p b s", b=8),
                                  zT[:, i, S0:NTOK].rearrange("p (b s) -> p b s", b=8), ALU.mult)\
                    .then_inc(emptied["v"], 1)
            evacuated(dve, "a", 3)
            cm["ktok"]()
            for i in range(4):
                evacuated(dve, "state", i)
            dve.wait_ge(bias_masked, 2)
            for h in range(8):
                full(dve, "ps", h)
                last = dve.tensor_tensor(SALL[:, h, :], ACC("ps", h)[:, 0:384], BIAS[:, h, :], ALU.add)
                last.then_inc(emptied["v"], 1)
            evacuated(dve, "ps", 7)
            dve.tensor_reduce(st[:, 0:8], SALL[:, :, 0:128], X, ALU.max)
            link(dve.tensor_reduce(st[:, 8:16], SALL[:, :, 128:384], X, ALU.max))
            dve.tensor_scalar(st[:, 16:32], st[:, 0:16], -1.0, None, ALU.mult).then_inc(negmax, 1)
            link(dve.memset(QBD, 0.0))
            for f in range(4):
                for r in range(2):
                    h = 2 * f + r
                    last = dve.tensor_copy(QBD[64 * r:64 * r + 64, :, f, 4 * h:4 * h + 4],
                                           qT[64 * r:64 * r + 64, f, S0:NTOK].rearrange("p (b q) -> p b q", q=4))
            last.then_inc(qbd_ready, 1)
            cm["kt"](0)
            cm["cnew"]()
            dve.wait_ge(exp_done, 16)
            link(dve.reciprocal(st[:, 48:64], st[:, 32:48]))
            dve.tensor_tensor(SALL[:, :, 0:128], SALL[:, :, 0:128], st[:, 48:56].unsqueeze(2).to_broadcast([P, 8, 128]), ALU.mult)
            dve.tensor_tensor(SALL[:, :, 128:384], SALL[:, :, 128:384],
                              st[:, 56:64].unsqueeze(2).to_broadcast([P, 8, 256]), ALU.mult).then_inc(probs, 1)
            ptpo(dve, "v", PTPO)

            def sample_softmax(g):
                dve.wait_ge(scores_full, g + 1)
                gs, v, bm, pen = st[:, 64:68], st[:, 68:72], st[:, 72:77], st[:, 80:85]
                mn, mx, sm, rc, nb = st[:, 77:78], st[:, 78:79], st[:, 79:80], st[:, 85:86], st[:, 88:93]
                dve.tensor_reduce(gs, psS[:, :, :].rearrange("p a (c k) -> p (a c) k", k=MOBA), X, ALU.add)
                dve.tensor_tensor(SS[:, 0:PAST], psS[:, :, :].rearrange("p a k -> p (a k)"), SBIAS, ALU.add)
                dve.tensor_tensor(SS[:, PAST:PAST + 32], psN[:, 0:32], OBIAS[:, g, :], ALU.add).then_inc(scores_read, 1)
                dve.wait_ge(scores_read, g + 1)
                dve.tensor_reduce(bm[:, 0:4], SS[:, 0:PAST].rearrange("p (c k) -> p c k", k=MOBA), X, ALU.max)
                dve.tensor_reduce(bm[:, 4:5], SS[:, PAST:PAST + 32], X, ALU.max)
                link(dve.tensor_reduce(mn, gs, X, ALU.min))
                link(dve.scalar_tensor_tensor(out=v, in0=gs, scalar=mn, in1=cst[:, C_IDX:C_IDX + 4],
                                              op0=ALU.is_equal, op1=ALU.mult))
                link(dve.tensor_reduce(mx, v, X, ALU.max))
                dve.memset(pen[:, 4:5], 0.0)
                link(dve.tensor_scalar(pen[:, 0:4], v, mx, NEG, ALU.is_equal, ALU.mult))
                link(dve.tensor_tensor(bm[:, 0:4], bm[:, 0:4], pen[:, 0:4], ALU.add))
                link(dve.tensor_reduce(sm, bm, X, ALU.max))
                dve.tensor_scalar(nb, pen, sm, None, ALU.subtract).then_inc(negmax, 1)
                dve.wait_ge(exp_done, 16 + 5 * (g + 1))
                link(dve.tensor_reduce(rc, st[:, 96:101], X, ALU.add))
                link(dve.reciprocal(rc, rc))
                dve.tensor_scalar(SS, SS, rc, None, ALU.mult).then_inc(probs, 1)

            for b in (1, 2, 3):
                cm["kt"](b)
            sample_softmax(0)
            cm["spt"](0)
            for b in (4, 5, 6, 7):
                cm["kt"](b)
            conv_taps(len(taps))

            def center(stage, zz, n, done, step):
                full(dve, stage, 0)
                m = ACC(stage, 0)[:, 0:NTOK].unsqueeze(1).to_broadcast([P, step, NTOK])
                for c in range(0, n, step):
                    ins = dve.tensor_tensor(zz[:, c:c + step, :], zz[:, c:c + step, :], m, ALU.subtract)
                    ins.then_inc(done if c + step < n else emptied["v"], 1)

            def rstd(stage, signal_std, count):
                full(dve, stage, 0)
                dve.tensor_scalar(rs[:, :], ACC(stage, 0)[:, 0:NTOK], EPS, None, ALU.add)\
                    .then_inc(emptied["v"], 1)
                dve.wait_ge(signal_std, count)
                link(dve.reciprocal(rs[:, :], std[:, :]))

            center("cmean", mixT[:, 4:8, :], 4, cen_c, 4)
            rstd("cvar", std_c, 1)
            for f in range(4):
                dve.tensor_tensor(mixT[:, 4 + f, :], mixT[:, 4 + f, :], rs[:, :], ALU.mult).then_inc(scl_c, 1)
            sample_softmax(1)
            cm["spt"](1)
            dve.wait_ge(smp_out, 2)
            pv = psV[:, 0:256].rearrange("p (b f c) -> p f b c", b=8, f=4)
            for r in range(2):
                rr = slice(64 * r, 64 * r + 64)
                dve.tensor_copy(mixT[rr, 0:4, S0:NTOK].rearrange("p f (b q) -> p f b q", q=4),
                                pv[rr, :, :, 4 * r:4 * r + 4]).then_inc(smp_read, 1)

            def residual(stage):
                for i in range(8):
                    full(dve, stage, i)
                    dve.scalar_tensor_tensor(out=zT[:, i, :], in0=xT[:, i, :], scalar=ALPHA, in1=ACC(stage, i)[:, 0:NTOK],
                                             op0=ALU.mult, op1=ALU.add).then_inc(emptied["v"], 1)

            def normalise(nth):
                rstd(f"var{nth}", std_ready, nth + 1)
                for f in range(8):
                    dve.scalar_tensor_tensor(out=zT[:, f, :], in0=zT[:, f, :], scalar=parT[:, f, nth:nth + 1],
                                             in1=rs[:, :], op0=ALU.mult, op1=ALU.mult).then_inc(scaled, 1)

            for l in range(DEPTH):
                if l:
                    center("vmean", vT, 8, cen_v, 2)
                    rstd("vvar", std_v, 1)
                    for f in range(8):
                        dve.scalar_tensor_tensor(out=vT[:, f, :], in0=vT[:, f, :], scalar=parT[:, f, 12:13],
                                                 in1=rs[:, :], op0=ALU.mult, op1=ALU.mult).then_inc(scl_v, 1)
                    evac(dve, "v", "wm", 2, lambda i, a: dve.tensor_copy(
                        WMT[:, 4 * i:4 * i + 4, :], a.rearrange("p (g t) -> p g t", g=4)))
                    cm["vtok"]()
                    for i in range(8):
                        evacuated(dve, "u", i)
                    for g in range(8):
                        full(dve, "mix", g)
                        a = ACC("mix", g)
                        dve.tensor_tensor(mixT[:, g, 0:SEQ].rearrange("p (n t) -> p n t", n=2),
                                          a[:, 0:SEQ].rearrange("p (n t) -> p n t", n=2),
                                          BSG[:, g, :].unsqueeze(1).to_broadcast([P, 2, P]), ALU.add)
                        dve.tensor_tensor(mixT[:, g, S0:NTOK].rearrange("p (b s) -> p b s", b=8),
                                          a[:, S0:NTOK].rearrange("p (b s) -> p b s", b=8),
                                          BSG[:, g, 0:DS].unsqueeze(1).to_broadcast([P, DB, DS]), ALU.add)\
                            .then_inc(emptied["v"], 1)
                        evacuated(dve, "mix", g)
                        dve.tensor_tensor(mixT[:, g, :], mixT[:, g, :], qT[:, g, :], ALU.mult).then_inc(mixed, 1)
                residual(f"o{l}")
                evacuated(dve, f"o{l}", 7)
                center(f"mean{3 * l}", zT, 8, centered, 2)
                normalise(3 * l)
                cm["mk"](l)
                cm["mv"](l)
                cm["mktok"](l)
                link(dve.memset(QX, 0.0))
                cm["xq"](l)
                for i in range(8):
                    evacuated(dve, f"xq{l}", i)
                for f in range(8):
                    h = f // 2
                    last = dve.tensor_copy(QX[:, :, f, 4 * h:4 * h + 4],
                                           qT[:, f, S0:NTOK].rearrange("p (b q) -> p b q", q=4))
                last.then_inc(qx_ready, 1)
                for h in range(4):
                    full(dve, f"xs{l}", h)
                    link(dve.tensor_reduce(st[:, 2 * h:2 * h + 2], ACC(f"xs{l}", h).rearrange("p (t k) -> p t k", t=2),
                                           X, ALU.max))
                    dve.tensor_scalar(st[:, 16 + 2 * h:18 + 2 * h], st[:, 2 * h:2 * h + 2], -1.0, None, ALU.mult)\
                        .then_inc(negmax, 1)
                for b in range(4):
                    cm["xkt"](l, b)
                ex = 26 + 2 * l
                evacuated(dve, f"xs{l}", 3)
                link(dve.reciprocal(st[:, 48:56], st[:, 32:40]))
                dve.tensor_tensor(PX, PX, st[:, 48:56].unsqueeze(2).to_broadcast([P, 8, 256]), ALU.mult).then_inc(probs, 1)

                def mem_softmax(g):
                    dve.wait_ge(xk_read, 8 * l + 4 * g + 4)
                    link(dve.tensor_reduce(st[:, 64:65], psS[:, 0, 0:256], X, ALU.max))
                    dve.tensor_scalar(st[:, 65 + g:66 + g], st[:, 64:65], -1.0, None, ALU.mult).then_inc(negmax, 1)
                    dve.wait_ge(exp_done, ex + g + 1)
                    link(dve.reciprocal(st[:, 70:71], st[:, 68 + g:69 + g]))
                    dve.tensor_scalar(XP[:, g, :], XP[:, g, :], st[:, 70:71], None, ALU.mult).then_inc(probs, 1)
                    evac(dve, "v", f"xspt{l}{g}", 1, lambda i, a: dve.tensor_copy(
                        XPTS, a[:, 0:256].rearrange("p (t m) -> p t m", t=2)))

                ptpo(dve, "v", XPTPO, l)
                mem_softmax(0)
                for b in range(4, 8):
                    cm["xkt"](l, b)
                mem_softmax(1)
                dve.wait_ge(values_used, DB * (2 + l))
                dve.tensor_copy(mixT[:, :, S0:NTOK].rearrange("p f (b q) -> p f b q", q=4),
                                psV[:, 0:256].rearrange("p (b f q) -> p f b q", b=8, f=8)).then_inc(smp_read, 1)
                residual(f"xo{l}")
                evacuated(dve, f"xo{l}", 7)
                center(f"mean{3 * l + 1}", zT, 8, centered, 2)
                normalise(3 * l + 1)

                evacuated(dve, f"router{l}", 0)
                sc, sel, cmp_ = RT[:, 48:96], RT[:, 96:144], RT[:, 144:336]
                eq = RT[:, 336:528]
                comb = RT[:, 0:48]
                top, gsc, v, best = RT[:, 528:576], RT[:, 576:588], RT[:, 588:600], RT[:, 600:612]
                mx, tmp = RT[:, 612:615], RT[:, 616:664]
                link(dve.tensor_tensor(sel.rearrange("p (t e) -> p t e", t=3), sc.rearrange("p (t e) -> p t e", t=3),
                                       rbias[:, :].unsqueeze(1).to_broadcast([P, 3, NE]), ALU.add))
                s3 = sel.rearrange("p (g e) -> p g e", e=4)
                other = s3.unsqueeze(2).to_broadcast([P, 12, 4, 4])
                self_ = s3.unsqueeze(3).to_broadcast([P, 12, 4, 4])
                c4 = cmp_.rearrange("p (g e o) -> p g e o", e=4, o=4)
                e4 = eq.rearrange("p (g e o) -> p g e o", e=4, o=4)
                dve.tensor_tensor(c4, other, self_, ALU.is_gt)
                link(dve.tensor_tensor(e4, other, self_, ALU.is_equal))
                link(dve.tensor_tensor(eq.rearrange("p (g c) -> p g c", c=16), eq.rearrange("p (g c) -> p g c", c=16),
                                       cst[:, C_TRI:C_TRI + 16].unsqueeze(1).to_broadcast([P, 12, 16]), ALU.mult))
                link(dve.tensor_tensor(cmp_, cmp_, eq, ALU.add))
                link(dve.tensor_reduce(top, cmp_.rearrange("p (g o) -> p g o", o=4), X, ALU.add))
                link(dve.tensor_scalar(top, top, 1.5, None, ALU.is_lt))
                link(dve.tensor_tensor(tmp, sel, top, ALU.mult))
                link(dve.tensor_reduce(gsc, tmp.rearrange("p (g e) -> p g e", e=4), X, ALU.add))
                g3 = gsc.rearrange("p (t g) -> p t g", g=4)
                v3 = v.rearrange("p (t g) -> p t g", g=4)
                b3 = best.rearrange("p (t g) -> p t g", g=4)
                link(dve.tensor_reduce(mx, g3, X, ALU.max))
                link(dve.tensor_tensor(v3, g3, mx.unsqueeze(2).to_broadcast([P, 3, 4]), ALU.is_equal))
                link(dve.tensor_tensor(v3, v3, cst[:, C_FIRST:C_FIRST + 4].unsqueeze(1).to_broadcast([P, 3, 4]), ALU.mult))
                link(dve.tensor_reduce(mx, v3, X, ALU.max))
                link(dve.tensor_tensor(b3, v3, mx.unsqueeze(2).to_broadcast([P, 3, 4]), ALU.is_equal))
                link(dve.tensor_tensor(top.rearrange("p (g e) -> p g e", e=4), top.rearrange("p (g e) -> p g e", e=4),
                                       best.unsqueeze(2).to_broadcast([P, 12, 4]), ALU.mult))
                link(dve.tensor_tensor(tmp, sc, top, ALU.mult))
                link(dve.tensor_reduce(mx, tmp.rearrange("p (t e) -> p t e", t=3), X, ALU.add))
                link(dve.reciprocal(mx, mx))
                dve.tensor_tensor(comb.rearrange("p (t e) -> p t e", t=3), tmp.rearrange("p (t e) -> p t e", t=3),
                                  mx.unsqueeze(2).to_broadcast([P, 3, NE]), ALU.mult).then_inc(comb_ready, 1)
                dve.wait_ge(x_ready, xr(3 * l + 1))
                dve.tensor_scalar(zT[:, :, :], xT[:, :, :], ALPHA, None, ALU.mult).then_inc(z_init, 1)
                evac(dve, "v", f"combT{l}", 1, lambda i, a: dve.tensor_copy(combT, a[0:NE, 0:NTOK]))
                cm["cb"](l)
                dve.wait_ge(z_init, l + 1)
                for i in owned("s", f"cb{l}", 16):
                    evacuated(dve, f"cb{l}", i)
                for i in owned("v", f"cb{l}", 16):
                    evacuated(dve, f"cb{l}", i)
                t0 = TIDX[f"moe{l}", 0]
                v0 = CUM["v"][t0]
                with dve.Fori(0, NE // 2) as i:
                    for e in range(2):
                        for j in range(4):
                            n = 16 * e + 2 * j + 1
                            dve.wait_ge(acc_full, t0 + n + 1 + 32 * i)
                            dve.tensor_tensor(UPC[:, j % 2, :], acc[:, (t0 + n) % NACC, 0:NTOK],
                                              CB[:, bass.ds(2 * i + e, 1), :].rearrange("p a n -> p (a n)"), ALU.mult)\
                                .then_inc(emptied["v"], 1)
                            dve.wait_ge(emptied["v"], v0 + 12 * e + j + 1 + 24 * i)
                            dve.wait_ge(emptied["s"], CUM["s"][t0] + 4 * e + j + 1 + 8 * i)
                            dve.tensor_tensor(H[:, e, j, :], UPC[:, j % 2, :], SG[:, e, j, :], ALU.mult).then_inc(h_ready, 1)
                        for j in range(8):
                            n = 16 * e + 8 + j
                            dve.wait_ge(acc_full, t0 + n + 1 + 32 * i)
                            dve.tensor_tensor(zT[:, j, :], zT[:, j, :], acc[:, (t0 + n) % NACC, 0:NTOK], ALU.add)\
                                .then_inc(emptied["v"], 1)
                evacuated(dve, f"moe{l}", 16 * NE - 1)
                center(f"mean{3 * l + 2}", zT, 8, centered, 2)
                normalise(3 * l + 2)
            cm["y"]()

        @block.scalar
        def _(act):
            cm = common(act, "s")
            act.dma_start(cst[:, :], const).then_inc(in_const, 16)
            act.dma_start(tab, table).then_inc(in_const, 16)
            act.dma_start(prow[0:6, :], ln_g.rearrange("l k d -> (l k) d")).then_inc(in_rows, 16)
            act.dma_start(prow[6:12, :], ln_b.rearrange("l k d -> (l k) d")).then_inc(in_rows, 16)
            act.dma_start(prow[12:13, :], sgu_ln_g).then_inc(in_rows, 16)
            act.dma_start(prow[13:14, :], sgu_ln_b).then_inc(in_rows, 16)
            act.dma_start(crow[0:31, :], conv_w[0]).then_inc(in_rows, 16)
            for i, w in enumerate((conv_b, conv_ln_g, conv_ln_b)):
                act.dma_start(crow[31 + i:32 + i, :], w).then_inc(in_rows, 16)
            for t in range(2):
                act.dma_start(strow[0:120, t, :], state_conv[0, 4 * t:4 * t + 4].rearrange("b t c -> (b t) c")).then_inc(in_rows, 16)
            act.dma_start(wrt[:, :, :], w_router.rearrange("(k p) e -> p k e", p=P)).then_inc(in_rows, 16)
            act.dma_start(rbias[:, :], router_bias.rearrange("(a e) -> a e", a=1).to_broadcast([P, NE])).then_inc(in_misc, 16)
            act.wait_ge(rb_zero, 1)
            for j in range(4):
                act.dma_start(RB4[32 * j:32 * j + 32, 8 * j:8 * j + 8], rel_bias).then_inc(rb_in, 16)
            cm["x"]()
            cm["state"]()
            for i in range(2):
                full(act, "sbias", i)
                act.activation(SBIAS[:, 512 * i:512 * i + 512], ACC("sbias", i), ACT.Copy).then_inc(emptied["s"], 1)
            cm["q"]()
            cm["k"]()
            cm["v"]()
            for i in range(4):
                full(act, "g", i)
                act.activation(zT[:, i, :], ACC("g", i)[:, 0:NTOK], ACT.Sigmoid).then_inc(emptied["s"], 1)
            evacuated(act, "a", 3)
            cm["ktok"]()
            act.wait_ge(negmax, 1)
            for h in range(8):
                for t in range(2):
                    r = slice(0, 128) if t == 0 else slice(128, 384)
                    act.activation(SALL[:, h, r], SALL[:, h, r], ACT.Exp, bias=st[:, 16 + 8 * t + h:17 + 8 * t + h],
                                   accum_out=st[:, 32 + 8 * t + h:33 + 8 * t + h]).then_inc(exp_done, 1)
            cm["kt"](0)
            cm["cnew"]()
            ptpo(act, "s", PTPO)

            def sample_softmax(g):
                act.wait_ge(negmax, 2 + g)
                for j in range(5):
                    r = slice(MOBA * j, MOBA * j + MOBA) if j < 4 else slice(PAST, PAST + 32)
                    act.activation(SS[:, r], SS[:, r], ACT.Exp, bias=st[:, 88 + j:89 + j],
                                   accum_out=st[:, 96 + j:97 + j]).then_inc(exp_done, 1)

            for b in (1, 2, 3):
                cm["kt"](b)
            sample_softmax(0)
            cm["spt"](0)
            for b in (4, 5, 6, 7):
                cm["kt"](b)

            def root(signal, stage):
                evacuated(act, stage, 0)
                act.activation(std[:, :], rs[:, :], ACT.Sqrt).then_inc(signal, 1)

            evacuated(act, "cmean", 0)
            act.wait_ge(out_even, 16 * 2)
            act.activation(zT[:, 0:4, :], mixT[:, 4:8, :], ACT.Square).then_inc(sq_c, 1)
            root(std_c, "cvar")
            for f in range(4):
                act.wait_ge(scl_c, f + 1)
                act.activation(mixT[:, 4 + f, :], mixT[:, 4 + f, :], ACT.Silu, bias=cparT[:, f, 33:34],
                               scale=cparT[:, f, 32:33]).then_inc(cv_ready, 1)
            sample_softmax(1)
            cm["spt"](1)

            def squares(nth):
                for c in range(4):
                    if c < 3:
                        act.wait_ge(centered, 3 * nth + c + 1)
                    else:
                        evacuated(act, f"mean{nth}", 0)
                    act.activation(mixT[:, 2 * c:2 * c + 2, :], zT[:, 2 * c:2 * c + 2, :], ACT.Square).then_inc(squared, 1)

            def finish(nth):
                root(std_ready, f"var{nth}")
                for f in range(8):
                    act.wait_ge(scaled, 8 * nth + f + 1)
                    act.activation(xT[:, f, :], zT[:, f, :], ACT.Identity, bias=parT[:, f, 6 + nth:7 + nth]).then_inc(x_ready, 1)

            for l in range(DEPTH):
                if l:
                    for i in range(8):
                        full(act, "u", i)
                        act.activation(qT[:, i, :], ACC("u", i)[:, 0:NTOK], ACT.Gelu).then_inc(emptied["s"], 1)
                    for i in range(8):
                        full(act, "vv", i)
                        act.activation(vT[:, i, :], ACC("vv", i)[:, 0:NTOK], ACT.Gelu).then_inc(emptied["s"], 1)
                    for c in range(4):
                        if c < 3:
                            act.wait_ge(cen_v, c + 1)
                        else:
                            evacuated(act, "vmean", 0)
                        act.activation(mixT[:, 2 * c:2 * c + 2, :], vT[:, 2 * c:2 * c + 2, :], ACT.Square).then_inc(sq_v, 1)
                    root(std_v, "vvar")
                    for f in range(8):
                        act.wait_ge(scl_v, f + 1)
                        act.activation(vT[:, f, :], vT[:, f, :], ACT.Identity, bias=parT[:, f, 13:14]).then_inc(vn_ready, 1)
                    cm["vtok"]()
                squares(3 * l)
                evac(act, "s", f"memT{l}", 8, lambda i, a: act.activation(memT[:, i, :], a[:, 0:256], ACT.Copy))
                finish(3 * l)
                cm["mk"](l)
                cm["mv"](l)
                cm["mktok"](l)
                cm["xq"](l)
                nm = 3 + 6 * l
                for h in range(4):
                    act.wait_ge(negmax, nm + h + 1)
                    for t in range(2):
                        ins = act.activation(PX[:, 2 * h + t, :], ACC(f"xs{l}", h)[:, 256 * t:256 * t + 256], ACT.Exp,
                                             bias=st[:, 16 + 2 * h + t:17 + 2 * h + t],
                                             accum_out=st[:, 32 + 2 * h + t:33 + 2 * h + t])
                    ins.then_inc(emptied["s"], 1)
                for b in range(4):
                    cm["xkt"](l, b)

                def mem_softmax(g):
                    act.wait_ge(negmax, nm + 4 + g + 1)
                    act.activation(XP[:, g, :], psS[:, 0, 0:256], ACT.Exp, bias=st[:, 65 + g:66 + g],
                                   accum_out=st[:, 68 + g:69 + g]).then_inc(exp_done, 1)

                ptpo(act, "s", XPTPO, l)
                mem_softmax(0)
                for b in range(4, 8):
                    cm["xkt"](l, b)
                mem_softmax(1)
                squares(3 * l + 1)
                finish(3 * l + 1)
                full(act, f"router{l}", 0)
                act.activation(RT[:, 48:96], ACC(f"router{l}", 0)[:, 0:48], ACT.Sigmoid)\
                    .then_inc(emptied["s"], 1)
                cm["cb"](l)
                t0 = TIDX[f"moe{l}", 0]
                with act.Fori(0, NE // 2) as i:
                    for e in range(2):
                        for j in range(4):
                            n = 16 * e + 2 * j
                            act.wait_ge(acc_full, t0 + n + 1 + 32 * i)
                            act.activation(SG[:, e, j, :], acc[:, (t0 + n) % NACC, 0:NTOK], ACT.Silu).then_inc(emptied["s"], 1)
                squares(3 * l + 2)
                finish(3 * l + 2)
            cm["y"]()

        @block.gpsimd
        def _(pool):
            evacuated(pool, "dbias", 3)
            pool.affine_select(out=BIAS[:, :, 0:128], in_=BIAS[:, :, 0:128], pattern=[[0, 8], [-1, 128]],
                               compare_op=ALU.is_ge, fill=NEG, base=0, channel_multiplier=1).then_inc(bias_masked, 1)
            pool.affine_select(out=BIAS[:, :, 128:384], in_=BIAS[:, :, 128:384], pattern=[[0, 8], [-1, 256]],
                               compare_op=ALU.is_ge, fill=NEG, base=128, channel_multiplier=1).then_inc(bias_masked, 1)
            evacuated(pool, "v", 0), evacuated(pool, "v", 1), evacuated(pool, "v", 2)
            kv = "l (t p) h d -> p (l t) (h d)"
            pool.dma_start(new_v_prompt[0].rearrange(kv, p=P), vtok[:, 0:2, :]).then_inc(out_rest, 16)
            pool.dma_start(new_v_sample[0].rearrange("b s h d -> (b s) (h d)"), vtok[0:32, 2, :]).then_inc(out_rest, 16)
            pool.dma_start(new_conv_sample[0, :, 0:26, :], state_conv[0, :, 4:30, :]).then_inc(out_rest, 16)
            for i in range(3):
                evacuated(pool, "ktok", i)
            pool.dma_start(new_k_prompt[0].rearrange(kv, p=P), ktok[:, 0:2, :]).then_inc(out_even, 16)
            pool.dma_start(new_k_sample[0].rearrange("b s h d -> (b s) (h d)"), ktok[0:32, 2, :]).then_inc(out_even, 16)
            evacuated(pool, "cnew", 0), evacuated(pool, "cnew", 1)
            pool.dma_start(new_conv_prompt[0, 0], cnew[0:30, 0, :]).then_inc(out_rest, 16)
            pool.dma_start(new_conv_sample[0, :, 26:30, :], cnew[0:32, 1, :]).then_inc(out_rest, 16)
            for l in range(DEPTH):
                if l:
                    evacuated(pool, "vtok", 4), evacuated(pool, "vtok", 5)
                    pool.dma_start(new_gmlp_v[0].rearrange("b s d -> (b s) d"), gvtok[0:32, 2, :]).then_inc(out_rest, 16)
                if l:
                    pool.wait_ge(mixed, 8)
                else:
                    pool.wait_ge(smp_out, 2)
                    pool.wait_ge(out_rest, 16 * 5)
                pool.dma_start(memtok, mem_prompt[0].rearrange("(t p) d -> p t d", p=P)).then_inc(mem_in, 16)
                for i in range(4):
                    evacuated(pool, f"mv{l}", i), evacuated(pool, f"mktok{l}", i)
                pool.dma_start(new_mem_v[l, 0].rearrange("(t p) h d -> p t (h d)", p=P), mvtok).then_inc(out_mem, 16)
                pool.dma_start(new_mem_k[l, 0].rearrange("(t p) h d -> p t (h d)", p=P), mktok).then_inc(out_mem, 16)
                pool.wait_ge(smp_read, 3 + l)
                pool.wait_ge(out_mem, 32 * (l + 1))
                pool.dma_start(SEL, selrow.rearrange("a (e m) -> a e m", e=NE)).then_inc(sel_in, 16)
                if l == 0:
                    pool.memset(WBD, 0.0).then_inc(wbd_zero, 1)
                    pool.wait_ge(wbd_zero, 1)
                    pool.dma_start(WLD, sgu_w[0].rearrange("g t s -> t g s")).then_inc(g_in, 16)
                    pool.dma_start(BSG, sgu_b.rearrange("a g t -> a (g t)").to_broadcast([P, D])
                                   .rearrange("p (g t) -> p g t", g=8)).then_inc(g_in, 16)
                    for b in range(DB):
                        for g in range(8):
                            pool.dma_start(WBD[4 * b:4 * b + 4, g, 4 * b:4 * b + 4],
                                           sgu_w[0, g, 0:4, 0:4].rearrange("t s -> s t"),
                                           allow_slow_non_contiguous=True).then_inc(wbd_in, 16)
                    pool.wait_ge(g_in, 32)
                    pool.affine_select(out=WLD, in_=WLD, pattern=[[0, 8], [-1, 128]], compare_op=ALU.is_ge, fill=0.0,
                                       base=0, channel_multiplier=1).then_inc(w_masked, 1)
                    pool.wait_ge(wbd_in, 16 * 64)
                    pool.affine_select(out=WBD, in_=WBD, pattern=[[0, 8], [1, 32]], compare_op=ALU.is_ge, fill=0.0,
                                       base=0, channel_multiplier=-1).then_inc(w_masked, 1)
            for i in range(6):
                evacuated(pool, "y", i)
            pool.dma_start(y_prompt[0].rearrange("(t p) d -> p t d", p=P), ytok[:, 0:2, :]).then_inc(out_rest, 16)
            pool.dma_start(y_sample.rearrange("b s d -> (b s) d"), ytok[0:32, 2, :]).then_inc(out_rest, 16)
            pool.wait_ge(out_rest, 16 * 8)
            pool.wait_ge(out_even, 32)
            pool.wait_ge(out_mem, 32 * DEPTH)


_INS = ['x_prompt', 'x_sample', 'cache_k', 'cache_v', 'state_conv', 'cache_mem_k', 'cache_mem_v', 'page_table',
        'mem_prompt', 'rel_bias', 'w_in_even', 'conv_w', 'conv_b', 'conv_ln_g', 'conv_ln_b', 'w_out_even',
        'w_in_odd', 'sgu_ln_g', 'sgu_ln_b', 'sgu_w', 'sgu_b', 'w_out_odd', 'w_xq', 'w_xkv', 'w_xo',
        'w_router', 'router_bias', 'w_exp_gate', 'w_exp_up', 'w_exp_down', 'ln_g', 'ln_b']
_OUTS = [(1, SEQ, D), (DB, DS, D), (1, 1, SEQ, HA, HD), (1, 1, SEQ, HA, HD), (1, DB, DS, HA, HD), (1, DB, DS, HA, HD),
         (1, 1, CW - 1, CC), (1, DB, CW - 1, CC), (DEPTH, 1, NMEM, HX, HDX), (DEPTH, 1, NMEM, HX, HDX),
         (1, DB, DS, D)]


def kernel(**inputs):
    import numpy as _np
    import concourse.bacc as _bacc
    from concourse import mybir as _mybir
    from concourse.bass_utils import run_bass_kernel_spmd as _run

    nc = _bacc.Bacc("TRN2", target_bir_lowering=False, num_devices=1)
    consts = dict(zip(("const", "table", "selrow"), shape_constants()))
    arrays, args = {}, []
    for name in _INS + list(consts):
        a = _np.ascontiguousarray(inputs[name] if name in inputs else consts[name])
        arrays[f"in_{name}"] = a
        args.append(nc.dram_tensor(f"in_{name}", a.shape, _mybir.dt.from_np(a.dtype), kind="ExternalInput").ap())
    for i, shape in enumerate(_OUTS):
        args.append(nc.dram_tensor(f"out_{i}", shape, _mybir.dt.float32, kind="ExternalOutput").ap())
    build(nc, *args)
    r = _run(nc, [arrays], core_ids=[0])
    return tuple(r.results[0][f"out_{i}"] for i in range(len(_OUTS)))
```

```python
from contextlib import ExitStack

import numpy as np

import concourse.bass as bass
from concourse import mybir

ALU = mybir.AluOpType
ACT = mybir.ActivationFunctionType
X = mybir.AxisListType.X
F32 = mybir.dt.float32
I32 = mybir.dt.int32

P = 128
D = 1024
SEQ = 256
DB, DS = 8, 4
NTOK = SEQ + DB * DS
S0 = SEQ
DEPTH = 2
PAST, PAGE = 1024, 128
NPAGE = PAST // PAGE
NPHYS = DB * NPAGE * 5 // 4
DA, HA, HD = 512, 8, 64
CC, CW = 512, 31
NB_BUCKET, MAXDIST = 32, 128
NMEM, HX, HDX = 256, 4, 256
NE, NG, EPG, DFF = 16, 4, 4, 512
FT = D // P
ALPHA = (2 * DEPTH) ** 0.25
EPS = 1e-5
NEG = -1e30
MOBA = 256
NBLK = PAST // MOBA

SLOTS = 6
UNIT = 8 * 512
NACC = 4

C_ID, C_OWN, C_IDX, C_FIRST, C_TRI = 0, 128, 192, 196, 200
C_BEFORE, C_SLOT, C_ONCE = 216, 344, 632
NCONST = 680
CAP = 128
NROW = 2 * NTOK
SLOTTED = NROW + CAP
NST = -(-NROW // P)
NFURTHER = -(-NTOK // CAP) - 1
T_OH4, T_OHS = 0, 380
NTABLE = 380 + PAST + DB * DS


def bucket(n):
    n = np.maximum(n, 0)
    half = NB_BUCKET // 2
    nf = np.maximum(n, 1).astype(np.float32)
    large = half + (np.log(nf / np.float32(half)) / np.float32(np.log(MAXDIST / half))
                    * np.float32(NB_BUCKET - half)).astype(np.int32)
    return np.where(n < half, n, np.minimum(large, NB_BUCKET - 1))


def shape_constants():
    c = np.zeros((P, NCONST), np.float32)
    c[:, C_ID:C_ID + P] = np.eye(P)
    row = np.arange(P)
    b4, q = row // 32, row % 4
    for g in range(2):
        for b in range(DB):
            for j in range(DS):
                seen = (b == 4 * g + b4) & (j <= q)
                c[:, C_OWN + 32 * g + 4 * b + j] = np.where(seen, 0.0, NEG)
    c[:, C_IDX:C_IDX + 4] = np.arange(1, 5)
    c[:, C_FIRST:C_FIRST + 4] = np.arange(4, 0, -1)
    e = np.arange(4)
    c[:, C_TRI:C_TRI + 16] = (e[None, :] < e[:, None]).astype(np.float32).reshape(-1)
    c[:, C_BEFORE:C_BEFORE + P] = row[:, None] < row[None, :]
    c[:, C_SLOT:C_SLOT + NTOK] = np.arange(1, NTOK + 1)
    c[:, C_ONCE:C_ONCE + 48] = 1
    c[:P - 32, C_ONCE + 32:C_ONCE + 48] = 0
    t = np.zeros((P, NTABLE), np.float32)
    for j in range(4):
        n = np.arange(380) - 252 + 128 - j
        t[32 * j + bucket(n)[n >= 0], T_OH4 + np.arange(380)[n >= 0]] = 1
        k = np.arange(PAST)
        t[32 * j + bucket(PAST + j - k), T_OHS + k] = 1
        for b in range(DB):
            for i in range(j + 1):
                t[32 * j + bucket(np.array(j - i)), T_OHS + PAST + 4 * b + i] = 1
    return c, t


def unit_order():
    u = [("in_even", n) for n in (0, 1, 2, 4, 3)]
    for g in range(2):
        u += [("K", 4 * g + b) for b in range(4)] + [("V", 4 * g + b) for b in range(4)]
    for l in range(DEPTH):
        if l:
            u += [("in_odd", n) for n in range(4)]
        u += [("out", l, n) for n in range(2)]
        u += [("xkv", l, n) for n in range(4)]
        u += [("xq", l, n) for n in range(2)]
        u += [("mem", l, b) for b in range(DB)]
        u += [("xo", l, n) for n in range(2)]
        u += [("moe", l, n) for n in range(3 * NE)]
    return u


def tile_order():
    t = []

    def add(stage, n, owners):
        t.extend((stage, i, owners[i % len(owners)]) for i in range(n))

    add("x", 8, "vs")
    add("q", 4, "vs")
    add("k", 4, "vs")
    add("v", 3, "vs")
    add("g", 4, "s")
    add("a", 4, "v")
    add("par", 1, "v")
    add("cpar", 1, "v")
    add("state", 4, "vs")
    add("dbias", 4, "v")
    add("sbias", 3, "ssv")
    add("ktok", 3, "vs")
    add("ps", 8, "v")
    add("kt0", 8, "s")
    add("cnew", 2, "vs")
    for s, i in PTPO:
        t.append((s, i, "vs"[i % 2]))
    for b in (1, 2, 3):
        add(f"kt{b}", 8, "s")
    add("spt0", 3, "svs")
    add("pvt0", 1, "v")
    for b in (4, 5, 6, 7):
        add(f"kt{b}", 8, "s")
    add("cmean", 1, "v")
    add("cvar", 1, "v")
    add("spt1", 3, "svs")
    add("pvt1", 1, "v")
    for l in range(DEPTH):
        if l:
            add("u", 8, "s")
            add("vv", 8, "s")
            add("vmean", 1, "v")
            add("vvar", 1, "v")
            add("wm", 2, "v")
            add("vtok", 6, "vs")
            add("mix", 8, "v")
        add(f"o{l}", 8, "v")
        add(f"mean{3 * l}", 1, "v")
        add(f"memT{l}", 8, "s")
        add(f"var{3 * l}", 1, "v")
        add(f"mk{l}", 4, "vs")
        add(f"mv{l}", 4, "vs")
        add(f"mktok{l}", 4, "vs")
        add(f"xq{l}", 8, "vs")
        add(f"xs{l}", 4, "s")
        for b in range(4):
            add(f"xkt{l}{b}", 4, "vs")
        for s, i in XPTPO:
            t.append((f"{s}{l}", i, "vs"[i % 2]))
        add(f"xspt{l}0", 1, "v")
        add(f"xpvt{l}0", 2, "v")
        for b in range(4, 8):
            add(f"xkt{l}{b}", 4, "vs")
        add(f"xspt{l}1", 1, "v")
        add(f"xpvt{l}1", 2, "v")
        add(f"xo{l}", 8, "v")
        add(f"mean{3 * l + 1}", 1, "v")
        add(f"var{3 * l + 1}", 1, "v")
        add(f"router{l}", 1, "s")
        add(f"xtok{l}", 6, "vs")
        add(f"rank{l}", 1, "v")
        add(f"xg{l}", 2 * FT, "vs")
        add(f"gt{l}", NST, "vs")
        add(f"yt{l}", 2 * NST, "vs")
        add(f"ms{l}", 8, "v")
        add(f"mean{3 * l + 2}", 1, "v")
        add(f"var{3 * l + 2}", 1, "v")
    add("y", 6, "vs")
    return t


PTPO = [("pt", 0), ("pt", 1), ("pt", 2), ("pt", 3), ("po", 0), ("pt", 4), ("pt", 5), ("po", 1),
        ("pt", 6), ("pt", 7), ("po", 2), ("po", 3)]
XPTPO = [("xpt", 0), ("xpt", 1), ("xpo", 0), ("xpt", 2), ("xpo", 1), ("xpt", 3), ("xpo", 2), ("xpo", 3)]


def build(nc, x_prompt, x_sample, cache_k, cache_v, state_conv, cache_mem_k, cache_mem_v, page_table,
          mem_prompt, rel_bias, w_in_even, conv_w, conv_b, conv_ln_g, conv_ln_b, w_out_even, w_in_odd,
          sgu_ln_g, sgu_ln_b, sgu_w, sgu_b, w_out_odd, w_xq, w_xkv, w_xo, w_router, router_bias,
          w_exp_gate, w_exp_up, w_exp_down, ln_g, ln_b, const, table,
          y_prompt, y_sample, new_k_prompt, new_v_prompt, new_k_sample, new_v_sample,
          new_conv_prompt, new_conv_sample, new_mem_k, new_mem_v, new_gmlp_v):
    units = unit_order()
    UIDX = {u: i for i, u in enumerate(units)}
    tiles = tile_order()
    TIDX = {(s, i): n for n, (s, i, _) in enumerate(tiles)}
    OWNER = [o for _, _, o in tiles]
    CUM = {"v": [0], "s": [0]}
    for o in OWNER:
        for k in "vs":
            CUM[k].append(CUM[k][-1] + (o == k))

    with ExitStack() as ctx:
        def sb(name, shape, dt=F32):
            return ctx.enter_context(nc.sbuf_tensor(name, shape, dt))

        def sem(name):
            return ctx.enter_context(nc.semaphore(name))

        ring = sb("ring", [P, SLOTS, UNIT])
        xT = sb("xT", [P, FT, NTOK])
        zT = sb("zT", [P, FT, NTOK])
        mixT = sb("mixT", [P, FT, NTOK])
        qT = sb("qT", [P, FT, NTOK])
        arena = sb("arena", [P, 17408])
        cst = sb("cst", [P, NCONST])
        ones_d = sb("ones_d", [P, P])
        parT = sb("parT", [P, FT, 14])
        cparT = sb("cparT", [P, 4, 34])
        wrt = sb("wrt", [P, FT, NE])
        rbias = sb("rbias", [P, NE])
        rs = sb("rs", [P, NTOK])
        std = sb("std", [P, NTOK])
        st = sb("st", [P, 112])
        pages = sb("pages", [1, DB * NPAGE], I32)
        acc = ctx.enter_context(nc.psum_tensor("acc", [P, NACC, 512], F32))
        psS = ctx.enter_context(nc.psum_tensor("psS", [P, 2, 512], F32))
        psN = ctx.enter_context(nc.psum_tensor("psN", [P, 512], F32))
        psV = ctx.enter_context(nc.psum_tensor("psV", [P, 512], F32))

        def view(off, *shape):
            n = int(np.prod(shape))
            v = arena[:, off:off + n]
            if len(shape) == 2:
                return v.rearrange("p (a b) -> p a b", b=shape[1])
            if len(shape) == 3:
                return v.rearrange("p (a b c) -> p a b c", b=shape[1], c=shape[2])
            return v

        def flat(t, a, b):
            return t.rearrange("p f m -> p (f m)")[:, 0:a * b].rearrange("p (a b) -> p a b", b=b)

        ident = cst[:, C_ID:C_ID + P]
        KT = view(0, 2, 4, 512)
        tab = view(0, NTABLE)
        prow = view(1536, 1024)
        crow = view(2560, 512)
        strow = view(3072, 2, 512)
        BIAS = view(4096, 8, 384)
        QBD = arena[:, 4096:5120].rearrange("p (b f m) -> p b f m", f=4, m=32)
        cnew = view(5120, 2, 512)
        SALL = view(7168, 8, 384)
        xtok = view(7168, 3, 1024)
        SS = view(7168, 1056)
        PTS = view(8224, 9, 128)
        PV = view(9376, 512)
        UP = view(10240, 4, 286)
        US = view(11384, 4, 8, 34)
        kT = view(12472, 4, NTOK)
        vtok = view(13624, 3, 512)
        SBIAS = view(15160, 1024)
        OBIAS = view(16184, 2, 32)
        PTP = view(16248, 2, 384)
        RB4 = view(17016, 32)
        SBL = view(17048, 128)
        ucmp = std[:, 0:128].rearrange("p (f m) -> p f m", f=4)
        ones_c = view(17176, P)
        ktok = zT[:, 0:6, :].rearrange("p a b -> p (a b)")[:, 0:1536].rearrange("p (a b) -> p a b", b=512)
        memT = view(0, 8, 256)
        XP = view(0, 2, 256)
        XPTS = view(512, 2, 128)
        XPV = view(768, 2, 512)
        mkT = view(2048, 8, 256)
        mvtok = view(4096, 2, 1024)
        mktok = view(6144, 2, 1024)
        PX = view(8192, 8, 256)
        XPT = view(10240, 2, 512)
        QX = arena[:, 11264:13312].rearrange("p (b f m) -> p b f m", f=8, m=32)
        MKT = view(13312, 2, 8, 256)
        memtok = view(13312, 2, 1024)
        XE = view(0, FT, SLOTTED)
        YT = view(5632, FT, SLOTTED)
        XTOK = view(5632, 3, 1024)
        YTOK = view(0, NST, 1024)
        G = flat(zT, 3, NROW)
        GW = flat(mixT, 3, NROW)
        GT = flat(qT, NST, NTOK)
        H = view(16128, 4, CAP)
        SG = view(16640, 4, CAP)
        POS = view(11264, 3, NE)
        COMB = view(11312, 3, NE)
        MASK = view(11360, 3, NE)
        PICK = view(11408, 3, NE)
        CNT = view(11456, NE)
        MORE = view(11472, NE)
        START = view(11488, NE)
        SCAN = view(11504, NE)
        ROW = view(11520, 2, 3)
        ROWB = view(11526, 2, 3)
        WT = view(11532, 2, 3)
        ones = view(11552, P)
        GA = view(11680, NTOK)
        STARTI, MOREI, BEFOREI = (arena[:, 12064 + NE * i:12064 + NE * i + NE].bitcast(I32) for i in range(3))
        RT = arena[:, 12128:12128 + 672]
        vT = view(0, 8, NTOK)
        gvtok = view(2304, 3, 1024)
        WLD = view(12800, 8, 128)
        BSG = view(13824, 8, 128)
        WBD = arena[0:32, 14848:15104].rearrange("p (g t) -> p g t", g=8)
        WMT = view(15104, 8, 128)
        ytok = view(0, 3, 1024)

        unit_in = [sem(f"unit_in{i}") for i in range(SLOTS)]
        values_used = sem("values_used")
        acc_full = sem("acc_full")
        emptied = {"v": sem("emptied_by_dve"), "s": sem("emptied_by_act")}
        in_x = sem("in_x")
        in_const = sem("in_const")
        in_rows = sem("in_rows")
        in_table = sem("in_table")
        in_rb = sem("sample_bias_operand")
        rb_zero = sem("rb_zero")
        rb_in = sem("rb_in")
        in_misc = sem("in_router_bias")
        in_pages = sem("in_pages")
        ones_set = sem("ones_set")
        dve_step = sem("dve_step")
        conv_step = sem("conv_step")
        bias_masked = sem("bias_masked")
        u_pads = sem("u_pads")
        qbd_ready = sem("qbd_ready")
        scores_full = sem("scores_full")
        scores_read = sem("scores_read")
        negmax = sem("negmax")
        exp_done = sem("exp_done")
        probs = sem("probs")
        smp_out = sem("smp_out")
        smp_read = sem("smp_read")
        centered = sem("centered")
        squared = sem("squared")
        std_ready = sem("std_ready")
        scaled = sem("scaled")
        x_ready = sem("x_ready")
        cen_c = None
        sq_c = sem("conv_squared")
        std_c = sem("conv_std")
        scl_c = sem("conv_scaled")
        cv_ready = sem("conv_ready")
        cen_v = sem("v_centered")
        sq_v = sem("v_squared")
        std_v = sem("v_std")
        scl_v = sem("v_scaled")
        vn_ready = sem("v_ready")
        mem_in = sem("mem_in")
        qx_ready = sem("qx_ready")
        comb_ready = sem("comb_ready")
        ranks_ready = sem("ranks_ready")
        rows_ready = sem("rows_ready")
        weights_ready = sem("weights_ready")
        expert_used = sem("expert_used")

        class Item:

            def __init__(self, tag):
                self.gate_up = sem(f"{tag}_gate_up")
                self.silu = sem(f"{tag}_silu")
                self.h = sem(f"{tag}_h")
                self.down = sem(f"{tag}_down")
                self.y_act = sem(f"{tag}_y_act")
                self.y_dve = sem(f"{tag}_y_dve")

        first = Item("first")
        more = [Item(f"more{l}") for l in range(DEPTH)]
        g_in = sem("gmlp_in")
        wbd_zero = sem("wbd_zero")
        wbd_in = sem("wbd_in")
        w_masked = sem("w_masked")
        mixed = sem("mixed")
        out_even = sem("out_even")
        out_mem = sem("out_mem")
        out_rest = sem("out_rest")

        kt_read = sem("kt_read")
        xk_read = sem("xk_read")
        xpv_ready = sem("xpv_ready")

        def further(start, c):
            return bass.ds(nc.s_assert_within(start + CAP + CAP * c, 0, NROW, skip_runtime_bounds_check_because="the chunk holds a row of its expert"), CAP)

        def ACC(stage, i):
            return acc[:, TIDX[stage, i] % NACC, :]

        def full(eng, stage, i):
            eng.wait_ge(acc_full, TIDX[stage, i] + 1)

        def bank_free(pe, stage, i):
            n = TIDX[stage, i] - NACC
            if n >= 0:
                o = OWNER[n]
                pe.wait_ge(emptied[o], CUM[o][n + 1])

        def evacuated(eng, stage, i):
            n = TIDX[stage, i]
            eng.wait_ge(emptied[OWNER[n]], CUM[OWNER[n]][n + 1])

        def owned(who, stage, n):
            return [i for i in range(n) if OWNER[TIDX[stage, i]] == who]

        def slot(u):
            return ring[:, u % SLOTS, :]

        LANDED = []
        total = [0] * SLOTS
        for n, k in enumerate(units):
            total[n % SLOTS] += 16 * (8 if k[0] in "KV" else 2 if k[0] == "mem" else 1)
            LANDED.append(total[n % SLOTS])

        def arrived(eng, u, more=0):
            eng.wait_ge(unit_in[u % SLOTS], LANDED[u] + more)

        def xr(nth):
            return 8 * (nth + 1)

        READER = {("in_even", 0): ("q", 3), ("in_even", 1): ("k", 3), ("in_even", 2): ("v", 2),
                  ("in_even", 4): ("g", 3), ("in_even", 3): ("a", 3)}
        for b in range(DB):
            READER["K", b] = (f"kt{b}", 7)
        for n in range(4):
            READER["in_odd", n] = (("u", "vv")[n // 2], 4 * (n % 2) + 3)
        for l in range(DEPTH):
            for n in range(2):
                READER["out", l, n] = (f"o{l}", 4 * n + 3)
                READER["xq", l, n] = (f"xq{l}", 4 * n + 3)
                READER["xo", l, n] = (f"xo{l}", 4 * n + 3)
                READER["xkv", l, n] = (f"mk{l}", 2 * n + 1)
                READER["xkv", l, 2 + n] = (f"mv{l}", 2 * n + 1)
            for n in range(3):
                READER["moe", l, 3 * (NE - 1) + n] = (f"gt{l}", 0)

        def slot_free(sp, u):
            if u < SLOTS:
                return
            k = units[u - SLOTS]
            if k[0] == "moe" and k[2] < 3 * (NE - 1):
                sp.wait_ge(expert_used, NE * k[1] + k[2] // 3 + 2)
            elif k[0] in ("V", "mem"):
                sp.wait_ge(values_used, 1 + (k[1] if k[0] == "V" else DB * (1 + k[1]) + k[2]))
            else:
                sp.wait_ge(acc_full, TIDX[READER[k]] + 1)

        block = ctx.enter_context(nc.Block())

        @block.sync
        def _(sp):
            sp.dma_start(xtok[:, 0:2, :], x_prompt[0].rearrange("(t p) d -> p t d", p=P)).then_inc(in_x, 16)
            sp.dma_start(xtok[0:32, 2, :], x_sample.rearrange("b s d -> (b s) d")).then_inc(in_x, 16)
            sp.dma_start(pages[:, :], page_table.rearrange("(a b) n -> a (b n)", a=1)).then_inc(in_pages, 16)

            def mat(w, n):
                return w[:, 512 * n:512 * n + 512].rearrange("(k p) n -> p k n", p=P)

            def load(u, dst8):
                kind = units[u]
                s = unit_in[u % SLOTS]
                if kind[0] in "KV":
                    cache = cache_k if kind[0] == "K" else cache_v
                    for p in range(NPAGE):
                        at = kind[1] * NPAGE + p
                        page = sp.value_load(pages[0:1, at:at + 1], min_val=0, max_val=NPHYS - 1)
                        sp.dma_start(dst8[:, p, :],
                                     cache[0, bass.ds(page, 1)].rearrange("a t h d -> (a t) (h d)")).then_inc(s, 16)
                    return
                if kind[0] == "mem":
                    _, l, b = kind
                    d2 = slot(u).rearrange("p (c t n) -> p c t n", c=2, n=1024)
                    for i, m in enumerate((cache_mem_k, cache_mem_v)):
                        sp.dma_start(d2[:, i], m[l, b].rearrange("(t p) h d -> p t (h d)", p=P)).then_inc(s, 16)
                    return
                if kind[0] == "in_even":
                    src = mat(w_in_even[0], kind[1])
                elif kind[0] == "in_odd":
                    src = mat(w_in_odd[0], kind[1])
                else:
                    _, l, n = kind
                    src = mat({"out": (w_out_even, w_out_odd)[l][0], "xkv": w_xkv[l], "xq": w_xq[l],
                               "xo": w_xo[l]}[kind[0]], n)
                sp.dma_start(dst8, src).then_inc(s, 16)

            u = 0
            while u < len(units):
                if units[u][0] == "K" and units[u][1] == 0:
                    sp.wait_ge(in_pages, 16)
                if units[u][0] != "moe":
                    slot_free(sp, u)
                    load(u, slot(u).rearrange("p (k n) -> p k n", k=8))
                    u += 1
                    continue
                l = units[u][1]

                def expert_pair(i, first):
                    for j in range(6):
                        if first:
                            slot_free(sp, u + j)
                        else:
                            sp.wait_ge(expert_used, NE * l + j // 3 + 2 * i)
                        e = 2 * i + j // 3
                        w = (w_exp_gate, w_exp_up, w_exp_down)[j % 3]
                        k = 8 if j % 3 < 2 else 4
                        sp.dma_start(slot(u + j).rearrange("p (k n) -> p k n", k=k),
                                     w[l, bass.ds(e, 1)].rearrange("a (k p) n -> p (a k) n", p=P))\
                          .then_inc(unit_in[(u + j) % SLOTS], 16)

                expert_pair(0, True)
                with sp.Fori(1, NE // 2) as i:
                    expert_pair(i, False)
                u += 3 * NE

        @block.tensor
        def _(pe):
            def mm(out, lhsT, rhs, first, last):
                return pe.matmul(out, lhsT, rhs, start=first, stop=last)

            def project(stage, u, rhs, j0, ready=None, cols=NTOK):
                W = slot(u).rearrange("p (k n) -> p k n", k=8)
                arrived(pe, u)
                for j in range(4):
                    bank_free(pe, stage, j0 + j)
                    for k in range(8):
                        if ready and j == 0:
                            ready(k)
                        last = mm(ACC(stage, j0 + j)[:, 0:cols], W[:, k, P * j:P * j + P], rhs[:, k, :], k == 0, k == 7)
                    last.then_inc(acc_full, 1)

            def mean_tile(stage, zz, w1, n, ready):
                bank_free(pe, stage, 0)
                for k in range(n):
                    ready(k)
                    last = mm(ACC(stage, 0)[:, 0:NTOK], w1, zz[:, k, :], k == 0, k == n - 1)
                last.then_inc(acc_full, 1)

            pe.wait_ge(in_const, 16)
            pe.wait_ge(in_x, 32)
            for i in range(8):
                bank_free(pe, "x", i)
                for t in range(3):
                    n = P if t < 2 else 32
                    last = pe.transpose(ACC("x", i)[:, P * t:P * t + n], xtok[0:n, t, P * i:P * i + P], ident[0:n, 0:n])
                last.then_inc(acc_full, 1)
            for i in range(8):
                evacuated(pe, "x", i)
            project("q", 0, xT, 0)
            project("k", 1, xT, 0)
            arrived(pe, 2)
            W = slot(2).rearrange("p (k n) -> p k n", k=8)
            for t in range(3):
                n = P if t < 2 else 32
                bank_free(pe, "v", t)
                for k in range(8):
                    last = mm(ACC("v", t)[0:n, :], xT[:, k, P * t:P * t + n], W[:, k, :], k == 0, k == 7)
                last.then_inc(acc_full, 1)
            project("g", 3, xT, 0)
            project("a", 4, xT, 0)
            pe.wait_ge(in_rows, 16 * 11)
            bank_free(pe, "par", 0)
            for i in range(8):
                last = pe.transpose(ACC("par", 0)[:, 14 * i:14 * i + 14], prow[0:14, P * i:P * i + P], ident[0:14, 0:14])
            last.then_inc(acc_full, 1)
            bank_free(pe, "cpar", 0)
            for i in range(4):
                last = pe.transpose(ACC("cpar", 0)[:, 34 * i:34 * i + 34], crow[0:34, P * i:P * i + P], ident[0:34, 0:34])
            last.then_inc(acc_full, 1)
            for i in range(4):
                bank_free(pe, "state", i)
                for t in range(2):
                    last = pe.transpose(ACC("state", i)[:, 120 * t:120 * t + 120], strow[0:120, t, P * i:P * i + P],
                                        ident[0:120, 0:120])
                last.then_inc(acc_full, 1)
            pe.wait_ge(in_table, 16)
            pe.wait_ge(rb_in, 64)
            for i in range(4):
                bank_free(pe, "dbias", i)
                for t in range(16):
                    w = 252 - 4 * (16 * i + t)
                    last = mm(ACC("dbias", i)[:, 32 * t:32 * t + 32], tab[:, T_OH4 + w:T_OH4 + w + P], RB4, True, True)
                last.then_inc(acc_full, 1)
            pe.wait_ge(in_rb, 1)
            for i in range(3):
                n = 512 if i < 2 else 32
                bank_free(pe, "sbias", i)
                mm(ACC("sbias", i)[:, 0:n], SBL, tab[:, T_OHS + 512 * i:T_OHS + 512 * i + n], True, True)\
                    .then_inc(acc_full, 1)

            for t in range(3):
                n = P if t < 2 else 32
                bank_free(pe, "ktok", t)
                for f in range(4):
                    evacuated(pe, "k", f)
                    last = pe.transpose(ACC("ktok", t)[0:n, P * f:P * f + P], kT[:, f, P * t:P * t + n], ident)
                last.then_inc(acc_full, 1)

            for h in range(8):
                r = slice(64 * (h % 2), 64 * (h % 2) + 64)
                evacuated(pe, "q", h // 2)
                bank_free(pe, "ps", h)
                mm(ACC("ps", h)[:, 0:128], qT[r, h // 2, 0:128], kT[r, h // 2, 0:128], True, True)
                mm(ACC("ps", h)[:, 128:384], qT[r, h // 2, 128:256], kT[r, h // 2, 0:256], True, True)\
                    .then_inc(acc_full, 1)

            def sample_keys(b):
                u = UIDX["K", b]
                K = slot(u).rearrange("p (k n) -> p k n", k=8)
                arrived(pe, u)
                g, b4 = b // 4, b % 4
                rows = slice(32 * b4, 32 * b4 + 32)
                if b4 == 0 and g:
                    pe.wait_ge(scores_read, 1)
                if b == 0:
                    pe.wait_ge(qbd_ready, 1)
                for half in range(2):
                    for f in range(4):
                        i = 4 * half + f
                        bank_free(pe, f"kt{b}", i)
                        for p in range(4):
                            last = pe.transpose(ACC(f"kt{b}", i)[:, P * p:P * p + P],
                                                K[:, 4 * half + p, P * f:P * f + P], ident)
                        last.then_inc(acc_full, 1)
                    for f in range(4):
                        evacuated(pe, f"kt{b}", 4 * half + f)
                        mm(psS[rows, half, :], QBD[:, b, f, :], KT[:, half, f, :], f == 0, f == 3)\
                            .then_inc(kt_read, 1)
                for f in range(4):
                    last = mm(psN[rows, 0:32], QBD[:, b, f, :], kT[:, f, S0:NTOK], f == 0, f == 3)
                if b4 == 3:
                    last.then_inc(scores_full, 1)

            def sample_values(g):
                pe.wait_ge(probs, 1 + 1 + g)
                for i in range(3):
                    bank_free(pe, f"spt{g}", i)
                    if i < 2:
                        for c in range(4):
                            k = 4 * i + c
                            last = pe.transpose(ACC(f"spt{g}", i)[:, P * c:P * c + P], SS[:, P * k:P * k + P], ident)
                    else:
                        last = pe.transpose(ACC(f"spt{g}", i)[0:32, 0:P], SS[:, PAST:PAST + 32], ident)
                    last.then_inc(acc_full, 1)
                for i in range(3):
                    evacuated(pe, f"spt{g}", i)
                for b4 in range(4):
                    b = 4 * g + b4
                    u = UIDX["V", b]
                    V = slot(u).rearrange("p (k n) -> p k n", k=8)
                    arrived(pe, u)
                    rows, c = psV[32 * b4:32 * b4 + 32, :], 32 * b4
                    for k in range(8):
                        last = mm(rows, PTS[:, k, c:c + 32], V[:, k, :], k == 0, False)
                    last.then_inc(values_used, 1)
                    last = mm(rows, PTS[0:32, 8, c:c + 32], vtok[0:32, 2, :], False, True)
                last.then_inc(smp_out, 1)

            def turn_rows(g):
                pe.wait_ge(smp_read, g + 1)
                bank_free(pe, f"pvt{g}", 0)
                for f in range(4):
                    last = pe.transpose(ACC(f"pvt{g}", 0)[:, P * f:P * f + P], PV[:, P * f:P * f + P], ident)
                last.then_inc(acc_full, 1)

            sample_keys(0)
            evacuated(pe, "a", 3)
            for i in range(2):
                n = 30 if i == 0 else 32
                bank_free(pe, "cnew", i)
                for f in range(4):
                    src = UP[:, f, 256:286] if i == 0 else ucmp[:, f, :]
                    last = pe.transpose(ACC("cnew", i)[0:n, P * f:P * f + P], src, ident)
                last.then_inc(acc_full, 1)
            pe.wait_ge(probs, 1)
            for s, i in PTPO:
                bank_free(pe, s, i)
                if s == "pt":
                    for c in range(3):
                        last = pe.transpose(ACC(s, i)[:, P * c:P * c + P], SALL[:, i, P * c:P * c + P], ident)
                else:
                    for h in (2 * i, 2 * i + 1):
                        evacuated(pe, "pt", h)
                        if i == 0:
                            evacuated(pe, "v", 0), evacuated(pe, "v", 1), evacuated(pe, "v", 2)
                        o = ACC(s, i)[64 * (h % 2):64 * (h % 2) + 64, :]
                        mm(o[:, 0:256], vtok[:, 0, 64 * h:64 * h + 64], PTP[:, h % 2, 0:256], True, False)
                        last = mm(o[:, 128:256], vtok[:, 1, 64 * h:64 * h + 64], PTP[:, h % 2, 256:384], False, True)
                last.then_inc(acc_full, 1)
            for b in (1, 2, 3):
                sample_keys(b)
            sample_values(0)
            turn_rows(0)
            for b in (4, 5, 6, 7):
                sample_keys(b)
            mean_tile("cmean", mixT[:, 4:8, :], ones_c, 4, lambda k: pe.wait_ge(conv_step, 8 * (CW - 1) + 2 * k + 2))
            mean_tile("cvar", zT, ones_c, 4, lambda k: pe.wait_ge(sq_c, 1))
            sample_values(1)
            turn_rows(1)

            def cross(l):
                nth = 3 * l + 1
                u0 = UIDX["xkv", l, 0]
                def mem_keys(i):
                    u = u0 + i // 2
                    W = slot(u).rearrange("p (k n) -> p k n", k=8)
                    arrived(pe, u)
                    bank_free(pe, f"mk{l}", i)
                    for c in range(2):
                        j = 2 * (i % 2) + c
                        for k in range(8):
                            last = mm(ACC(f"mk{l}", i)[:, 256 * c:256 * c + 256], W[:, k, P * j:P * j + P],
                                      memT[:, k, :], k == 0, k == 7)
                    last.then_inc(acc_full, 1)

                mean_tile(f"mean{3 * l}", zT, ones_d[:, :], 8, lambda k: evacuated(pe, f"o{l}", k))
                pe.wait_ge(mem_in, 16 * (l + 1))
                for i in range(8):
                    bank_free(pe, f"memT{l}", i)
                    for t in range(2):
                        last = pe.transpose(ACC(f"memT{l}", i)[:, P * t:P * t + P], memtok[:, t, P * i:P * i + P], ident)
                    last.then_inc(acc_full, 1)
                mean_tile(f"var{3 * l}", mixT, ones_d[:, :], 8, lambda k: pe.wait_ge(squared, 4 * 3 * l + k // 2 + 1))
                for i in range(8):
                    evacuated(pe, f"memT{l}", i)
                for i in range(4):
                    mem_keys(i)
                for i in range(4):
                    n, t = i // 2, i % 2
                    u = u0 + 2 + n
                    W = slot(u).rearrange("p (k n) -> p k n", k=8)
                    arrived(pe, u)
                    bank_free(pe, f"mv{l}", i)
                    for k in range(8):
                        last = mm(ACC(f"mv{l}", i), memT[:, k, P * t:P * t + P], W[:, k, :], k == 0, k == 7)
                    last.then_inc(acc_full, 1)
                for i in range(4):
                    t, n = i // 2, i % 2
                    bank_free(pe, f"mktok{l}", i)
                    for f in range(4):
                        evacuated(pe, f"mk{l}", (4 * n + f) // 2)
                        last = pe.transpose(ACC(f"mktok{l}", i)[:, P * f:P * f + P],
                                            mkT[:, 4 * n + f, P * t:P * t + P], ident)
                    last.then_inc(acc_full, 1)
                for n in range(2):
                    project(f"xq{l}", UIDX["xq", l, n], xT, 4 * n,
                            lambda k: pe.wait_ge(x_ready, xr(3 * l - 1) + k + 1))
                for h in range(4):
                    evacuated(pe, f"xq{l}", 2 * h), evacuated(pe, f"xq{l}", 2 * h + 1)
                    bank_free(pe, f"xs{l}", h)
                    for t in range(2):
                        for c in range(2):
                            last = mm(ACC(f"xs{l}", h)[:, 256 * t:256 * t + 256], qT[:, 2 * h + c, P * t:P * t + P],
                                      mkT[:, 2 * h + c, :], c == 0, c == 1)
                    last.then_inc(acc_full, 1)

                def keys(b):
                    u = UIDX["mem", l, b]
                    K = slot(u).rearrange("p (c t n) -> p c t n", c=2, n=1024)[:, 0]
                    arrived(pe, u)
                    b4 = b % 4
                    if b == 0:
                        pe.wait_ge(qx_ready, l + 1)
                    if b == 4:
                        pe.wait_ge(exp_done, 26 + 2 * l + 1)
                    for i in range(4):
                        bank_free(pe, f"xkt{l}{b}", i)
                        for c in range(4):
                            f, t = 2 * i + c // 2, c % 2
                            last = pe.transpose(ACC(f"xkt{l}{b}", i)[:, P * c:P * c + P], K[:, t, P * f:P * f + P], ident)
                        last.then_inc(acc_full, 1)
                    for f in range(8):
                        evacuated(pe, f"xkt{l}{b}", f // 2)
                        last = mm(psS[32 * b4:32 * b4 + 32, 0, 0:256], QX[:, b, f, :], MKT[:, b % 2, f, :], f == 0, f == 7)
                    last.then_inc(xk_read, 1)

                def values(g):
                    bank_free(pe, f"xspt{l}{g}", 0)
                    pe.wait_ge(probs, 3 + (DEPTH + 1) * l + 1 + g + 1)
                    for t in range(2):
                        last = pe.transpose(ACC(f"xspt{l}{g}", 0)[:, P * t:P * t + P], XP[:, g, P * t:P * t + P], ident)
                    last.then_inc(acc_full, 1)
                    evacuated(pe, f"xspt{l}{g}", 0)
                    for b4 in range(4):
                        b = 4 * g + b4
                        u = UIDX["mem", l, b]
                        V = slot(u).rearrange("p (c t n) -> p c t n", c=2, n=1024)[:, 1]
                        for half in range(2):
                            for t in range(2):
                                last = mm((psV, psN)[half][32 * b4:32 * b4 + 32, :], XPTS[:, t, 32 * b4:32 * b4 + 32],
                                          V[:, t, 512 * half:512 * half + 512], t == 0, t == 1)
                        last.then_inc(values_used, 1)
                    pe.wait_ge(xpv_ready, 2 * (2 * l + g) + 2)
                    for half in range(2):
                        bank_free(pe, f"xpvt{l}{g}", half)
                        for f in range(4):
                            last = pe.transpose(ACC(f"xpvt{l}{g}", half)[:, P * f:P * f + P], XPV[:, half, P * f:P * f + P], ident)
                        last.then_inc(acc_full, 1)

                for b in range(4):
                    keys(b)
                pe.wait_ge(probs, 3 + (DEPTH + 1) * l + 1)
                for s, i in XPTPO:
                    bank_free(pe, f"{s}{l}", i)
                    if s == "xpt":
                        for c in range(4):
                            kt, t = c // 2, c % 2
                            last = pe.transpose(ACC(f"xpt{l}", i)[:, P * c:P * c + P], PX[:, 2 * i + t, P * kt:P * kt + P], ident)
                    else:
                        evacuated(pe, f"xpt{l}", i)
                        if i == 0:
                            for n in range(4):
                                evacuated(pe, f"mv{l}", n)
                        for c in range(2):
                            for kt in range(2):
                                w = 256 * i + P * c
                                last = mm(ACC(f"xpo{l}", i)[:, 256 * c:256 * c + 256], mvtok[:, kt, w:w + P],
                                          XPT[:, i % 2, 256 * kt:256 * kt + 256], kt == 0, kt == 1)
                    last.then_inc(acc_full, 1)
                values(0)
                for b in range(4, 8):
                    keys(b)
                values(1)
                for i in range(2):
                    evacuated(pe, f"xpvt{l}0", i), evacuated(pe, f"xpvt{l}1", i)
                for i in range(4):
                    evacuated(pe, f"xpo{l}", i)
                for n in range(2):
                    project(f"xo{l}", UIDX["xo", l, n], mixT, 4 * n)
                mean_tile(f"mean{nth}", zT, ones_d[:, :], 8, lambda k: evacuated(pe, f"xo{l}", k))
                mean_tile(f"var{nth}", mixT, ones_d[:, :], 8, lambda k: pe.wait_ge(squared, 4 * nth + k // 2 + 1))

            def expert_chunk(S, n, W, at, banks, free, started=None):
                Wg, Wu, Wd, ug, uu, ud = W
                ug()
                for j in range(4):
                    if j >= 2:
                        pe.wait_ge(S.h, 4 * n + j - 1)
                    for c, w in enumerate((Wg, Wu)):
                        if j == 0 and c == 1:
                            uu()
                        for k in range(8):
                            last = mm(psS[:, j % 2, CAP * c:CAP * c + CAP], w[:, k, P * j:P * j + P], XE[:, k, at], k == 0, k == 7)
                            if started and j == 0 and c == 0 and k == 0:
                                last.then_inc(started, 1)
                    last.then_inc(S.gate_up, 1)
                ud()
                free()
                order = [(0, (0, 1, 2)), (4, (0, 1, 2)), (0, (3,)), (4, (3,))] + [(f, range(4)) for f in (1, 2, 3, 5, 6, 7)]
                for f, ks in order:
                    for k in ks:
                        if f == 0:
                            pe.wait_ge(S.h, 4 * n + k + 1)
                        last = mm(banks[f // 4][:, CAP * (f % 4):CAP * (f % 4) + CAP], Wd[:, k, P * f:P * f + P], H[:, k, :],
                                  k == 0, k == 3)
                    if f in (3, 7):
                        last.then_inc(S.down, 1)

            def experts(l):
                bank_free(pe, f"router{l}", 0)
                for t in range(3):
                    a = min(P * t, NTOK - P)
                    for k in range(8):
                        if t == 0:
                            pe.wait_ge(x_ready, xr(3 * l) + k + 1)
                        last = mm(ACC(f"router{l}", 0)[:, NE * t:NE * t + NE], xT[:, k, a:a + P], wrt[:, k, :], k == 0, k == 7)
                last.then_inc(acc_full, 1)
                for i in range(6):
                    t, half = i // 2, i % 2
                    a = min(P * t, NTOK - P)
                    bank_free(pe, f"xtok{l}", i)
                    for f in range(4):
                        last = pe.transpose(ACC(f"xtok{l}", i)[:, P * f:P * f + P], xT[:, 4 * half + f, a:a + P], ident)
                    last.then_inc(acc_full, 1)
                pe.wait_ge(comb_ready, l + 1)
                bank_free(pe, f"rank{l}", 0)
                R = ACC(f"rank{l}", 0)
                for t in (3, 0, 1, 2):
                    for s_ in range(min(t + 1, 3)):
                        last = mm(R[:, NE * t:NE * t + NE], cst[:, C_BEFORE:C_BEFORE + P] if s_ == t else ones,
                                  MASK[:, s_, :], s_ == 0, s_ == min(t, 2))
                last.then_inc(acc_full, 1)
                for i in range(6):
                    evacuated(pe, f"xtok{l}", i)
                pe.wait_ge(rows_ready, l + 1)
                for i in range(2 * FT):
                    f, half = i // 2, i % 2
                    bank_free(pe, f"xg{l}", i)
                    for t in range(3):
                        last = mm(ACC(f"xg{l}", i)[:, 0:NTOK], XTOK[:, t, P * f:P * f + P], G[:, t, NTOK * half:NTOK * half + NTOK],
                                  t == 0, t == 2)
                    last.then_inc(acc_full, 1)
                for i in range(2 * FT):
                    evacuated(pe, f"xg{l}", i)
                pe.wait_ge(ranks_ready, l + 1)
                u0 = UIDX["moe", l, 0]
                Y = (NE + 1) * l + 1
                with pe.Fori(0, NE // 2) as i:
                    for e in range(2):
                        n = 2 * i + e
                        u = u0 + 3 * e
                        W = [slot(u + j).rearrange("p (k n) -> p k n", k=(8, 8, 4)[j]) for j in range(3)]
                        here = [lambda j=j: arrived(pe, u + j, 16 * i) for j in range(3)]
                        start = pe.value_load(STARTI[0:1, bass.ds(n, 1)], min_val=0, max_val=NROW)
                        expert_chunk(first, NE * l + n, W + here, bass.ds(start, CAP), (acc[:, 0, :], acc[:, 1, :]),
                                     lambda: (pe.wait_ge(first.y_act, Y + n), pe.wait_ge(first.y_dve, Y + n)), expert_used)
                        extra = pe.value_load(MOREI[0:1, bass.ds(n, 1)], min_val=0, max_val=NFURTHER)
                        with pe.If(extra > 0):
                            before = pe.value_load(BEFOREI[0:1, bass.ds(n, 1)], min_val=0, max_val=NROW // CAP)
                            with pe.Fori(0, extra) as c:
                                k = before + c
                                expert_chunk(more[l], k, W + [lambda: None] * 3, further(start, c),
                                             (psN[:, :], psV[:, :]), lambda: None)
                                pe.wait_ge(more[l].y_act, k + 1)
                                pe.wait_ge(more[l].y_dve, k + 1)
                pe.wait_ge(weights_ready, l + 1)
                pe.wait_ge(first.y_act, (NE + 1) * (l + 1))
                pe.wait_ge(first.y_dve, (NE + 1) * (l + 1))
                for i in range(NST):
                    r = min(P, NROW - P * i)
                    bank_free(pe, f"gt{l}", i)
                    for t in (2, 0, 1):
                        a = min(P * t, NTOK - P)
                        last = pe.transpose(ACC(f"gt{l}", i)[0:r, a:a + P], GW[:, t, P * i:P * i + r], ident)
                    last.then_inc(acc_full, 1)
                for i in range(2 * NST):
                    half, s_ = i // NST, i % NST
                    r = min(P, NROW - P * s_)
                    bank_free(pe, f"yt{l}", i)
                    for f in range(4):
                        last = pe.transpose(ACC(f"yt{l}", i)[0:r, P * f:P * f + P], YT[:, 4 * half + f, P * s_:P * s_ + r], ident)
                    last.then_inc(acc_full, 1)
                for i in range(NST):
                    evacuated(pe, f"gt{l}", i)
                for f in range(8):
                    for s_ in range(NST):
                        if f % 4 == 0:
                            evacuated(pe, f"yt{l}", NST * (f // 4) + s_)
                        if s_ == 0:
                            bank_free(pe, f"ms{l}", f)
                        r = min(P, NROW - P * s_)
                        last = mm(ACC(f"ms{l}", f)[:, 0:NTOK], YTOK[0:r, s_, P * f:P * f + P], GT[0:r, s_, :], s_ == 0, s_ == NST - 1)
                    last.then_inc(acc_full, 1)
                nth = 3 * l + 2
                mean_tile(f"mean{nth}", zT, ones_d[:, :], 8, lambda k: evacuated(pe, f"ms{l}", k))
                mean_tile(f"var{nth}", mixT, ones_d[:, :], 8, lambda k: pe.wait_ge(squared, 4 * nth + k // 2 + 1))

            for l in range(DEPTH):
                if l:
                    for n in range(2):
                        project("u", UIDX["in_odd", n], xT, 4 * n, lambda k: pe.wait_ge(x_ready, xr(2)))
                    for n in range(2):
                        project("vv", UIDX["in_odd", 2 + n], xT, 4 * n)
                    mean_tile("vmean", vT, ones_d[:, :], 8, lambda k: evacuated(pe, "vv", k))
                    mean_tile("vvar", mixT, ones_d[:, :], 8, lambda k: pe.wait_ge(sq_v, k // 2 + 1))
                    pe.wait_ge(w_masked, 1)
                    for i in range(2):
                        bank_free(pe, "wm", i)
                        for g in range(4):
                            last = pe.transpose(ACC("wm", i)[:, P * g:P * g + P], WLD[:, 4 * i + g, :], ident)
                        last.then_inc(acc_full, 1)
                    for i in range(6):
                        t, half = i // 2, i % 2
                        n = P if t < 2 else 32
                        bank_free(pe, "vtok", i)
                        for f in range(4):
                            if i < 2:
                                pe.wait_ge(vn_ready, 4 * half + f + 1)
                            last = pe.transpose(ACC("vtok", i)[0:n, P * f:P * f + P],
                                                vT[:, 4 * half + f, P * t:P * t + n], ident)
                        last.then_inc(acc_full, 1)
                    for i in range(6):
                        evacuated(pe, "vtok", i)
                    evacuated(pe, "wm", 1)
                    pe.wait_ge(w_masked, 2)
                    for g in range(8):
                        bank_free(pe, "mix", g)
                        for t in range(2):
                            mm(ACC("mix", g)[:, P * t:P * t + P], gvtok[:, t, P * g:P * g + P], WMT[:, g, :], True, True)
                        mm(ACC("mix", g)[:, S0:NTOK], gvtok[0:32, 2, P * g:P * g + P], WBD[:, g, :], True, True)\
                            .then_inc(acc_full, 1)
                if l:
                    pe.wait_ge(mixed, 8)
                else:
                    evacuated(pe, "pvt0", 0), evacuated(pe, "pvt1", 0)
                    pe.wait_ge(cv_ready, 4)
                    for i in range(4):
                        evacuated(pe, "po", i)
                for n in range(2):
                    project(f"o{l}", UIDX["out", l, n], mixT, 4 * n)
                cross(l)
                experts(l)
            pe.wait_ge(x_ready, xr(5))
            for i in range(6):
                t, half = i // 2, i % 2
                n = P if t < 2 else 32
                bank_free(pe, "y", i)
                for f in range(4):
                    last = pe.transpose(ACC("y", i)[0:n, P * f:P * f + P], xT[:, 4 * half + f, P * t:P * t + n], ident)
                last.then_inc(acc_full, 1)

        def evac(eng, who, stage, n, body):
            for i in owned(who, stage, n):
                full(eng, stage, i)
                body(i, ACC(stage, i)).then_inc(emptied[who], 1)

        def copier(eng, who):
            if who == "v":
                return eng.tensor_copy
            return lambda out, in_: eng.activation(out, in_, ACT.Copy)

        def scaler(eng, who):
            if who == "v":
                return lambda out, in_, c: eng.tensor_scalar(out, in_, c, None, ALU.mult)
            return lambda out, in_, c: eng.activation(out, in_, ACT.Copy, scale=c)

        def common(eng, who):
            copy, scale = copier(eng, who), scaler(eng, who)

            def rows(i):
                return P if i < 2 else 32

            def xkt(l, b):
                def body(i, a):
                    if b >= 2:
                        eng.wait_ge(xk_read, 8 * l + b - 1)
                    elif l and b < 2:
                        eng.wait_ge(xk_read, 8 * l)
                    return copy(MKT[:, b % 2, 2 * i:2 * i + 2, :], a.rearrange("p (f m) -> p f m", f=2))
                evac(eng, who, f"xkt{l}{b}", 4, body)

            def kt(b):
                def body(i, a):
                    if b:
                        eng.wait_ge(kt_read, 8 * (b - 1) + i + 1)
                    return copy(KT[:, i // 4, i % 4, :], a)
                evac(eng, who, f"kt{b}", 8, body)

            return dict(
                x=lambda: evac(eng, who, "x", 8, lambda i, a: copy(xT[:, i, :], a[:, 0:NTOK])),
                state=lambda: evac(eng, who, "state", 4, lambda i, a: copy(
                    US[:, i, :, 0:30], a[:, 0:240].rearrange("p (b t) -> p b t", b=8))),
                q=lambda: evac(eng, who, "q", 4, lambda i, a: scale(qT[:, i, :], a[:, 0:NTOK], HD ** -0.5)),
                k=lambda: evac(eng, who, "k", 4, lambda i, a: copy(kT[:, i, :], a[:, 0:NTOK])),
                v=lambda: evac(eng, who, "v", 3, lambda i, a: copy(vtok[0:rows(i), i, :], a[0:rows(i), :])),
                ktok=lambda: evac(eng, who, "ktok", 3, lambda i, a: copy(ktok[0:rows(i), i, :], a[0:rows(i), :])),
                cnew=lambda: evac(eng, who, "cnew", 2, lambda i, a: copy(
                    cnew[0:30 + 2 * i, i, :], a[0:30 + 2 * i, :])),
                kt=kt,
                spt=lambda g: evac(eng, who, f"spt{g}", 3, lambda i, a: (
                    copy(PTS[:, 4 * i:4 * i + 4, :], a.rearrange("p (k m) -> p k m", k=4)) if i < 2 else
                    copy(PTS[0:32, 8, :], a[0:32, 0:P]))),
                mk=lambda l: evac(eng, who, f"mk{l}", 4, lambda i, a: copy(
                    mkT[:, 2 * i:2 * i + 2, :], a.rearrange("p (f m) -> p f m", f=2))),
                mv=lambda l: evac(eng, who, f"mv{l}", 4, lambda i, a: copy(
                    mvtok[:, i % 2, 512 * (i // 2):512 * (i // 2) + 512], a)),
                mktok=lambda l: evac(eng, who, f"mktok{l}", 4, lambda i, a: copy(
                    mktok[:, i // 2, 512 * (i % 2):512 * (i % 2) + 512], a)),
                xq=lambda l: evac(eng, who, f"xq{l}", 8, lambda i, a: scale(qT[:, i, :], a[:, 0:NTOK], HDX ** -0.5)),
                xkt=xkt,
                xtok=lambda l: evac(eng, who, f"xtok{l}", 6, lambda i, a: copy(
                    XTOK[:, i // 2, 512 * (i % 2):512 * (i % 2) + 512], a)),
                xg=lambda l: evac(eng, who, f"xg{l}", 2 * FT, lambda i, a: copy(
                    XE[:, i // 2, NTOK * (i % 2):NTOK * (i % 2) + NTOK], a[:, 0:NTOK])),
                gt=lambda l: evac(eng, who, f"gt{l}", NST, lambda i, a: copy(
                    GT[0:min(P, NROW - P * i), i, :], a[0:min(P, NROW - P * i), 0:NTOK])),
                yt=lambda l: evac(eng, who, f"yt{l}", 2 * NST, lambda i, a: copy(
                    YTOK[0:min(P, NROW - P * (i % NST)), i % NST, 512 * (i // NST):512 * (i // NST) + 512],
                    a[0:min(P, NROW - P * (i % NST)), :])),
                vtok=lambda: evac(eng, who, "vtok", 6, lambda i, a: copy(
                    gvtok[0:rows(i // 2), i // 2, 512 * (i % 2):512 * (i % 2) + 512], a[0:rows(i // 2), :])),
                y=lambda: evac(eng, who, "y", 6, lambda i, a: copy(
                    ytok[0:rows(i // 2), i // 2, 512 * (i % 2):512 * (i % 2) + 512], a[0:rows(i // 2), :])),
            )

        def ptpo(eng, who, table, l=None):
            copy = copier(eng, who)
            for s, i in table:
                stage = s if l is None else f"{s}{l}"
                if OWNER[TIDX[stage, i]] != who:
                    continue
                full(eng, stage, i)
                a = ACC(stage, i)
                if s == "pt":
                    if i >= 2:
                        full(eng, "po", i // 2 - 1)
                    ins = copy(PTP[:, i % 2, :], a[:, 0:384])
                elif s == "po":
                    ins = copy(mixT[:, i, 0:SEQ], a[:, 0:SEQ])
                elif s == "xpt":
                    if i >= 2:
                        full(eng, f"xpo{l}", i - 2)
                    ins = copy(XPT[:, i % 2, :], a)
                else:
                    ins = copy(mixT[:, 2 * i:2 * i + 2, 0:SEQ], a.rearrange("p (f q) -> p f q", f=2))
                ins.then_inc(emptied[who], 1)

        @block.vector
        def _(dve):
            steps = [0]

            def link(ins):
                steps[0] += 1
                ins.then_inc(dve_step, 1)
                dve.wait_ge(dve_step, steps[0])

            taps = [(w, f, part) for w in range(CW) for f in range(4) for part in range(2)]

            def conv_taps(n):
                for _ in range(min(n, len(taps) - done[0])):
                    w, f, part = taps[done[0]]
                    y = mixT[:, 4 + f, 0:SEQ] if part == 0 else mixT[:, 4 + f, S0:NTOK].rearrange("p (b s) -> p b s", b=8)
                    u = UP[:, f, w:w + SEQ] if part == 0 else US[:, f, :, w:w + DS]
                    tap = cparT[:, f, w:w + 1]
                    if w:
                        dve.wait_ge(conv_step, done[0] - 7)
                        ins = dve.scalar_tensor_tensor(out=y, in0=u, scalar=tap, in1=y, op0=ALU.mult, op1=ALU.add)
                    else:
                        ins = dve.tensor_scalar(y, u, tap, cparT[:, f, 31:32], ALU.mult, ALU.add)
                    ins.then_inc(conv_step, 1)
                    done[0] += 1

            done = [0]
            cm = common(dve, "v")
            dve.memset(ones_d[:, :], 1.0 / D).then_inc(ones_set, 1)
            dve.memset(ones_c, 1.0 / CC).then_inc(ones_set, 1)
            dve.memset(RB4, 0.0).then_inc(rb_zero, 1)
            cm["x"]()
            cm["q"]()
            cm["k"]()
            cm["v"]()
            dve.memset(UP[:, :, 0:30], 0.0).then_inc(u_pads, 1)
            for i in range(4):
                evacuated(dve, "g", i)
                full(dve, "a", i)
                a = ACC("a", i)
                dve.tensor_tensor(UP[:, i, 30:286], a[:, 0:SEQ], zT[:, i, 0:SEQ], ALU.mult)
                dve.tensor_tensor(ucmp[:, i, :], a[:, S0:NTOK], zT[:, i, S0:NTOK], ALU.mult)
                dve.tensor_tensor(US[:, i, :, 30:34], a[:, S0:NTOK].rearrange("p (b s) -> p b s", b=8),
                                  zT[:, i, S0:NTOK].rearrange("p (b s) -> p b s", b=8), ALU.mult)\
                    .then_inc(emptied["v"], 1)
            full(dve, "par", 0)
            dve.tensor_copy(parT[:, :, :], ACC("par", 0)[:, 0:112].rearrange("p (f c) -> p f c", f=8)).then_inc(emptied["v"], 1)
            full(dve, "cpar", 0)
            dve.tensor_copy(cparT[:, :, :], ACC("cpar", 0)[:, 0:136].rearrange("p (f c) -> p f c", f=4)).then_inc(emptied["v"], 1)
            dve.wait_ge(rb_in, 64)
            src = RB4.rearrange("p (q h) -> p h q", q=4)
            for b in range(4):
                last = dve.tensor_copy(SBL[:, 32 * b:32 * b + 32].rearrange("p (h q) -> p h q", q=4), src)
            last.then_inc(in_rb, 1)
            cm["state"]()
            for i in range(4):
                full(dve, "dbias", i)
                a = ACC("dbias", i).rearrange("p (m h) -> p h m", h=8)
                ins = dve.tensor_copy(BIAS[:, :, 128 + 64 * i:192 + 64 * i], a)
                if i >= 2:
                    ins = dve.tensor_copy(BIAS[:, :, 64 * i - 128:64 * i - 64], a)
                ins.then_inc(emptied["v"], 1)
            full(dve, "sbias", 2)
            for g in range(2):
                last = dve.tensor_tensor(OBIAS[:, g, :], ACC("sbias", 2)[:, 0:32],
                                         cst[:, C_OWN + 32 * g:C_OWN + 32 * g + 32], ALU.add)
            last.then_inc(emptied["v"], 1)
            cm["ktok"]()
            for i in range(4):
                evacuated(dve, "state", i)
            dve.wait_ge(bias_masked, 2)
            for h in range(8):
                full(dve, "ps", h)
                last = dve.tensor_tensor(SALL[:, h, :], ACC("ps", h)[:, 0:384], BIAS[:, h, :], ALU.add)
                last.then_inc(emptied["v"], 1)
            evacuated(dve, "ps", 7)
            dve.tensor_reduce(st[:, 0:8], SALL[:, :, 0:128], X, ALU.max)
            link(dve.tensor_reduce(st[:, 8:16], SALL[:, :, 128:384], X, ALU.max))
            dve.tensor_scalar(st[:, 16:32], st[:, 0:16], -1.0, None, ALU.mult).then_inc(negmax, 1)
            link(dve.memset(QBD, 0.0))
            for f in range(4):
                for r in range(2):
                    h = 2 * f + r
                    last = dve.tensor_copy(QBD[64 * r:64 * r + 64, :, f, 4 * h:4 * h + 4],
                                           qT[64 * r:64 * r + 64, f, S0:NTOK].rearrange("p (b q) -> p b q", q=4))
            last.then_inc(qbd_ready, 1)
            cm["cnew"]()
            dve.wait_ge(exp_done, 16)
            link(dve.reciprocal(st[:, 48:64], st[:, 32:48]))
            dve.tensor_tensor(SALL[:, :, 0:128], SALL[:, :, 0:128], st[:, 48:56].unsqueeze(2).to_broadcast([P, 8, 128]), ALU.mult)
            dve.tensor_tensor(SALL[:, :, 128:384], SALL[:, :, 128:384],
                              st[:, 56:64].unsqueeze(2).to_broadcast([P, 8, 256]), ALU.mult).then_inc(probs, 1)
            ptpo(dve, "v", PTPO)

            def sample_rows(g):
                full(dve, f"pvt{g}", 0)
                a = ACC(f"pvt{g}", 0).rearrange("p (f b c) -> p f b c", f=4, b=4)
                for f in range(4):
                    for r in range(2):
                        rr = slice(64 * r, 64 * r + 64)
                        h = 2 * f + r
                        ins = dve.tensor_copy(mixT[rr, f, S0 + 16 * g:S0 + 16 * g + 16].rearrange("p (b q) -> p b q", b=4),
                                              a[rr, f, :, 4 * h:4 * h + 4])
                ins.then_inc(emptied["v"], 1)

            def sample_softmax(g):
                dve.wait_ge(scores_full, g + 1)
                gs, v, bm, pen = st[:, 64:68], st[:, 68:72], st[:, 72:77], st[:, 80:85]
                mn, mx, sm, rc, nb = st[:, 77:78], st[:, 78:79], st[:, 79:80], st[:, 85:86], st[:, 88:93]
                dve.tensor_reduce(gs, psS[:, :, :].rearrange("p a (c k) -> p (a c) k", k=MOBA), X, ALU.add)
                dve.tensor_tensor(SS[:, 0:PAST], psS[:, :, :].rearrange("p a k -> p (a k)"), SBIAS, ALU.add)
                dve.tensor_tensor(SS[:, PAST:PAST + 32], psN[:, 0:32], OBIAS[:, g, :], ALU.add).then_inc(scores_read, 1)
                dve.wait_ge(scores_read, g + 1)
                dve.tensor_reduce(bm[:, 0:4], SS[:, 0:PAST].rearrange("p (c k) -> p c k", k=MOBA), X, ALU.max)
                dve.tensor_reduce(bm[:, 4:5], SS[:, PAST:PAST + 32], X, ALU.max)
                link(dve.tensor_reduce(mn, gs, X, ALU.min))
                link(dve.scalar_tensor_tensor(out=v, in0=gs, scalar=mn, in1=cst[:, C_IDX:C_IDX + 4],
                                              op0=ALU.is_equal, op1=ALU.mult))
                link(dve.tensor_reduce(mx, v, X, ALU.max))
                dve.memset(pen[:, 4:5], 0.0)
                link(dve.tensor_scalar(pen[:, 0:4], v, mx, NEG, ALU.is_equal, ALU.mult))
                link(dve.tensor_tensor(bm[:, 0:4], bm[:, 0:4], pen[:, 0:4], ALU.add))
                link(dve.tensor_reduce(sm, bm, X, ALU.max))
                dve.tensor_scalar(nb, pen, sm, None, ALU.subtract).then_inc(negmax, 1)
                dve.wait_ge(exp_done, 16 + 5 * (g + 1))
                link(dve.tensor_reduce(rc, st[:, 96:101], X, ALU.add))
                link(dve.reciprocal(rc, rc))
                dve.tensor_scalar(SS, SS, rc, None, ALU.mult).then_inc(probs, 1)

            conv_taps(len(taps) // 3)
            sample_softmax(0)
            cm["spt"](0)
            conv_taps(len(taps) // 4)
            sample_rows(0)
            conv_taps(len(taps))

            def center(stage, zz, n, done, step):
                full(dve, stage, 0)
                m = ACC(stage, 0)[:, 0:NTOK].unsqueeze(1).to_broadcast([P, step, NTOK])
                for c in range(0, n, step):
                    ins = dve.tensor_tensor(zz[:, c:c + step, :], zz[:, c:c + step, :], m, ALU.subtract)
                    ins.then_inc(done if c + step < n else emptied["v"], 1)

            def rstd(stage, signal_std, count):
                full(dve, stage, 0)
                dve.tensor_scalar(rs[:, :], ACC(stage, 0)[:, 0:NTOK], EPS, None, ALU.add)\
                    .then_inc(emptied["v"], 1)
                dve.wait_ge(signal_std, count)
                link(dve.reciprocal(rs[:, :], std[:, :]))

            center("cmean", mixT[:, 4:8, :], 4, cen_c, 4)
            rstd("cvar", std_c, 1)
            for f in range(4):
                dve.tensor_tensor(mixT[:, 4 + f, :], mixT[:, 4 + f, :], rs[:, :], ALU.mult).then_inc(scl_c, 1)
            sample_softmax(1)
            cm["spt"](1)
            sample_rows(1)

            def residual(stage):
                for i in range(8):
                    full(dve, stage, i)
                    dve.scalar_tensor_tensor(out=zT[:, i, :], in0=xT[:, i, :], scalar=ALPHA, in1=ACC(stage, i)[:, 0:NTOK],
                                             op0=ALU.mult, op1=ALU.add).then_inc(emptied["v"], 1)

            def normalise(nth):
                rstd(f"var{nth}", std_ready, nth + 1)
                for f in range(8):
                    dve.scalar_tensor_tensor(out=zT[:, f, :], in0=zT[:, f, :], scalar=parT[:, f, nth:nth + 1],
                                             in1=rs[:, :], op0=ALU.mult, op1=ALU.mult).then_inc(scaled, 1)

            for l in range(DEPTH):
                if l:
                    center("vmean", vT, 8, cen_v, 2)
                    rstd("vvar", std_v, 1)
                    for f in range(8):
                        dve.scalar_tensor_tensor(out=vT[:, f, :], in0=vT[:, f, :], scalar=parT[:, f, 12:13],
                                                 in1=rs[:, :], op0=ALU.mult, op1=ALU.mult).then_inc(scl_v, 1)
                    evac(dve, "v", "wm", 2, lambda i, a: dve.tensor_copy(
                        WMT[:, 4 * i:4 * i + 4, :], a.rearrange("p (g t) -> p g t", g=4)))
                    cm["vtok"]()
                    for i in range(8):
                        evacuated(dve, "u", i)
                    for g in range(8):
                        full(dve, "mix", g)
                        a = ACC("mix", g)
                        dve.tensor_tensor(mixT[:, g, 0:SEQ].rearrange("p (n t) -> p n t", n=2),
                                          a[:, 0:SEQ].rearrange("p (n t) -> p n t", n=2),
                                          BSG[:, g, :].unsqueeze(1).to_broadcast([P, 2, P]), ALU.add)
                        dve.tensor_tensor(mixT[:, g, S0:NTOK].rearrange("p (b s) -> p b s", b=8),
                                          a[:, S0:NTOK].rearrange("p (b s) -> p b s", b=8),
                                          BSG[:, g, 0:DS].unsqueeze(1).to_broadcast([P, DB, DS]), ALU.add)\
                            .then_inc(emptied["v"], 1)
                        evacuated(dve, "mix", g)
                        dve.tensor_tensor(mixT[:, g, :], mixT[:, g, :], qT[:, g, :], ALU.mult).then_inc(mixed, 1)
                residual(f"o{l}")
                evacuated(dve, f"o{l}", 7)
                center(f"mean{3 * l}", zT, 8, centered, 2)
                normalise(3 * l)
                cm["mk"](l)
                cm["mv"](l)
                cm["mktok"](l)
                link(dve.memset(QX, 0.0))
                cm["xq"](l)
                for i in range(8):
                    evacuated(dve, f"xq{l}", i)
                for f in range(8):
                    h = f // 2
                    last = dve.tensor_copy(QX[:, :, f, 4 * h:4 * h + 4],
                                           qT[:, f, S0:NTOK].rearrange("p (b q) -> p b q", q=4))
                last.then_inc(qx_ready, 1)
                for h in range(4):
                    full(dve, f"xs{l}", h)
                    link(dve.tensor_reduce(st[:, 2 * h:2 * h + 2], ACC(f"xs{l}", h).rearrange("p (t k) -> p t k", t=2),
                                           X, ALU.max))
                    dve.tensor_scalar(st[:, 16 + 2 * h:18 + 2 * h], st[:, 2 * h:2 * h + 2], -1.0, None, ALU.mult)\
                        .then_inc(negmax, 1)
                for b in range(4):
                    cm["xkt"](l, b)
                ex = 26 + 2 * l
                evacuated(dve, f"xs{l}", 3)
                link(dve.reciprocal(st[:, 48:56], st[:, 32:40]))
                dve.tensor_tensor(PX, PX, st[:, 48:56].unsqueeze(2).to_broadcast([P, 8, 256]), ALU.mult).then_inc(probs, 1)

                def mem_softmax(g):
                    dve.wait_ge(xk_read, 8 * l + 4 * g + 4)
                    link(dve.tensor_reduce(st[:, 64:65], psS[:, 0, 0:256], X, ALU.max))
                    dve.tensor_scalar(st[:, 65 + g:66 + g], st[:, 64:65], -1.0, None, ALU.mult).then_inc(negmax, 1)
                    dve.wait_ge(exp_done, ex + g + 1)
                    link(dve.reciprocal(st[:, 70:71], st[:, 68 + g:69 + g]))
                    dve.tensor_scalar(XP[:, g, :], XP[:, g, :], st[:, 70:71], None, ALU.mult).then_inc(probs, 1)
                    evac(dve, "v", f"xspt{l}{g}", 1, lambda i, a: dve.tensor_copy(
                        XPTS, a[:, 0:256].rearrange("p (t m) -> p t m", t=2)))

                def mem_rows(g):
                    dve.wait_ge(values_used, DB * (1 + l) + 4 * g + 4)
                    dve.tensor_copy(XPV[:, 1, :], psN[:, :]).then_inc(xpv_ready, 1)
                    for half in range(2):
                        full(dve, f"xpvt{l}{g}", half)
                        a = ACC(f"xpvt{l}{g}", half).rearrange("p (f b c) -> p f b c", f=4, b=4)
                        for f in range(4):
                            h = 2 * half + f // 2
                            ins = dve.tensor_copy(mixT[:, 4 * half + f, S0 + 16 * g:S0 + 16 * g + 16].rearrange("p (b q) -> p b q", b=4),
                                                  a[:, f, :, 4 * h:4 * h + 4])
                        ins.then_inc(emptied["v"], 1)

                ptpo(dve, "v", XPTPO, l)
                mem_softmax(0)
                mem_rows(0)
                for b in range(4, 8):
                    cm["xkt"](l, b)
                mem_softmax(1)
                mem_rows(1)
                residual(f"xo{l}")
                evacuated(dve, f"xo{l}", 7)
                center(f"mean{3 * l + 1}", zT, 8, centered, 2)
                normalise(3 * l + 1)

                evacuated(dve, f"router{l}", 0)
                dve.wait_ge(in_misc, 16)
                sc, sel, cmp_ = RT[:, 48:96], RT[:, 96:144], RT[:, 144:336]
                eq = RT[:, 336:528]
                top, gsc, v, best = RT[:, 528:576], RT[:, 576:588], RT[:, 588:600], RT[:, 600:612]
                mx, tmp = RT[:, 612:615], RT[:, 616:664]
                link(dve.tensor_tensor(sel.rearrange("p (t e) -> p t e", t=3), sc.rearrange("p (t e) -> p t e", t=3),
                                       rbias[:, :].unsqueeze(1).to_broadcast([P, 3, NE]), ALU.add))
                s3 = sel.rearrange("p (g e) -> p g e", e=4)
                other = s3.unsqueeze(2).to_broadcast([P, 12, 4, 4])
                self_ = s3.unsqueeze(3).to_broadcast([P, 12, 4, 4])
                c4 = cmp_.rearrange("p (g e o) -> p g e o", e=4, o=4)
                e4 = eq.rearrange("p (g e o) -> p g e o", e=4, o=4)
                dve.tensor_tensor(c4, other, self_, ALU.is_gt)
                link(dve.tensor_tensor(e4, other, self_, ALU.is_equal))
                link(dve.tensor_tensor(eq.rearrange("p (g c) -> p g c", c=16), eq.rearrange("p (g c) -> p g c", c=16),
                                       cst[:, C_TRI:C_TRI + 16].unsqueeze(1).to_broadcast([P, 12, 16]), ALU.mult))
                link(dve.tensor_tensor(cmp_, cmp_, eq, ALU.add))
                link(dve.tensor_reduce(top, cmp_.rearrange("p (g o) -> p g o", o=4), X, ALU.add))
                link(dve.tensor_scalar(top, top, 1.5, None, ALU.is_lt))
                link(dve.tensor_tensor(tmp, sel, top, ALU.mult))
                link(dve.tensor_reduce(gsc, tmp.rearrange("p (g e) -> p g e", e=4), X, ALU.add))
                g3 = gsc.rearrange("p (t g) -> p t g", g=4)
                v3 = v.rearrange("p (t g) -> p t g", g=4)
                b3 = best.rearrange("p (t g) -> p t g", g=4)
                link(dve.tensor_reduce(mx, g3, X, ALU.max))
                link(dve.tensor_tensor(v3, g3, mx.unsqueeze(2).to_broadcast([P, 3, 4]), ALU.is_equal))
                link(dve.tensor_tensor(v3, v3, cst[:, C_FIRST:C_FIRST + 4].unsqueeze(1).to_broadcast([P, 3, 4]), ALU.mult))
                link(dve.tensor_reduce(mx, v3, X, ALU.max))
                link(dve.tensor_tensor(b3, v3, mx.unsqueeze(2).to_broadcast([P, 3, 4]), ALU.is_equal))
                link(dve.tensor_tensor(top.rearrange("p (g e) -> p g e", e=4), top.rearrange("p (g e) -> p g e", e=4),
                                       best.unsqueeze(2).to_broadcast([P, 12, 4]), ALU.mult))
                link(dve.tensor_tensor(tmp, sc, top, ALU.mult))
                link(dve.tensor_reduce(mx, tmp.rearrange("p (t e) -> p t e", t=3), X, ALU.add))
                link(dve.reciprocal(mx, mx))
                dve.wait_ge(out_mem, 32 * (l + 1))
                once = cst[:, C_ONCE:C_ONCE + 48].rearrange("p (t e) -> p t e", t=3)
                link(dve.memset(ones, 1.0))
                dve.tensor_tensor(MASK, top.rearrange("p (t e) -> p t e", t=3), once, ALU.mult).then_inc(comb_ready, 1)
                link(dve.tensor_tensor(COMB, tmp.rearrange("p (t e) -> p t e", t=3),
                                       mx.unsqueeze(2).to_broadcast([P, 3, NE]), ALU.mult))
                cm["xtok"](l)
                full(dve, f"rank{l}", 0)
                R = ACC(f"rank{l}", 0)
                dve.wait_ge(comb_ready, l + 1)
                link(dve.tensor_copy(CNT, R[:, 48:64]))
                link(dve.tensor_tensor_scan(START, ones[:, 0:NE], CNT, 0.0, ALU.mult, ALU.add))
                link(dve.tensor_tensor(START, START, CNT, ALU.subtract))
                dve.tensor_tensor(POS, R[:, 0:48].rearrange("p (t e) -> p t e", t=3),
                                  START.unsqueeze(1).to_broadcast([P, 3, NE]), ALU.add).then_inc(emptied["v"], 1)
                evacuated(dve, f"rank{l}", 0)
                link(dve.scalar_tensor_tensor(out=POS, in0=POS, scalar=1.0, in1=MASK, op0=ALU.add, op1=ALU.mult))
                dve.tensor_reduce(ROW[:, 0, :], POS, X, ALU.max)
                link(dve.tensor_reduce(ROW[:, 1, :], POS, X, ALU.add))
                link(dve.tensor_tensor(ROW[:, 1, :], ROW[:, 1, :], ROW[:, 0, :], ALU.subtract))
                link(dve.tensor_scalar(ROWB, ROW, -float(NTOK), None, ALU.add))
                seq = cst[:, C_SLOT:C_SLOT + NTOK]
                for half, at in ((0, ROW), (1, ROWB)):
                    for t in range(3):
                        g = G[:, t, NTOK * half:NTOK * half + NTOK]
                        link(dve.tensor_scalar(GA, seq, at[:, 0, t:t + 1], None, ALU.is_equal))
                        ins = dve.scalar_tensor_tensor(out=g, in0=seq, scalar=at[:, 1, t:t + 1], in1=GA,
                                                       op0=ALU.is_equal, op1=ALU.add)
                        link(ins)
                dve.memset(XE[:, :, NROW:], 0.0).then_inc(rows_ready, 1)
                link(dve.tensor_scalar(MORE, CNT, CAP + 0.5, None, ALU.is_gt))
                for c in range(2, NFURTHER + 1):
                    link(dve.scalar_tensor_tensor(out=MORE, in0=CNT, scalar=c * CAP + 0.5, in1=MORE, op0=ALU.is_gt, op1=ALU.add))
                link(dve.tensor_tensor_scan(SCAN, ones[:, 0:NE], MORE, 0.0, ALU.mult, ALU.add))
                link(dve.tensor_tensor(SCAN, SCAN, MORE, ALU.subtract))
                dve.tensor_copy(STARTI, START)
                dve.tensor_copy(MOREI, MORE)
                dve.tensor_copy(BEFOREI, SCAN).then_inc(ranks_ready, 1)
                cm["xg"](l)
                for pick in range(2):
                    link(dve.tensor_tensor(PICK, POS, ROW[:, pick, :].unsqueeze(2).to_broadcast([P, 3, NE]), ALU.is_equal))
                    link(dve.tensor_tensor(PICK, PICK, COMB, ALU.mult))
                    link(dve.tensor_reduce(WT[:, pick, :], PICK, X, ALU.add))
                for half, at in ((0, ROW), (1, ROWB)):
                    for t in range(3):
                        g = GW[:, t, NTOK * half:NTOK * half + NTOK]
                        dve.tensor_scalar(g, seq, at[:, 0, t:t + 1], WT[:, 0, t:t + 1], ALU.is_equal, ALU.mult)
                        link(dve.tensor_scalar(GA, seq, at[:, 1, t:t + 1], WT[:, 1, t:t + 1], ALU.is_equal, ALU.mult))
                        ins = dve.tensor_tensor(g, g, GA, ALU.add)
                        if (half, t) == (1, 2):
                            ins.then_inc(weights_ready, 1)
                        else:
                            link(ins)
                dve.wait_ge(weights_ready, l + 1)
                dve.memset(GA[:, 0:1], 0.0).then_inc(first.y_dve, 1)

                dve.wait_ge(ranks_ready, l + 1)

                def chunk(S, n, at, bank):
                    for j in range(4):
                        dve.wait_ge(S.gate_up, 4 * n + j + 1)
                        dve.wait_ge(S.silu, 4 * n + j + 1)
                        dve.tensor_tensor(H[:, j, :], SG[:, j, :], psS[:, j % 2, CAP:2 * CAP], ALU.mult).then_inc(S.h, 1)
                    dve.wait_ge(S.down, 2 * n + 2)
                    dve.tensor_copy(YT[:, 4:8, at], bank[:, 0:4 * CAP].rearrange("p (f m) -> p f m", f=4)).then_inc(S.y_dve, 1)

                with dve.Fori(0, NE // 2) as i:
                    for e in range(2):
                        n = 2 * i + e
                        start = dve.value_load(STARTI[0:1, bass.ds(n, 1)], min_val=0, max_val=NROW)
                        chunk(first, NE * l + n, bass.ds(start, CAP), acc[:, 1, :])
                        extra = dve.value_load(MOREI[0:1, bass.ds(n, 1)], min_val=0, max_val=NFURTHER)
                        with dve.If(extra > 0):
                            before = dve.value_load(BEFOREI[0:1, bass.ds(n, 1)], min_val=0, max_val=NROW // CAP)
                            with dve.Fori(0, extra) as c:
                                chunk(more[l], before + c, further(start, c), psV[:, :])
                cm["gt"](l)
                cm["yt"](l)
                residual(f"ms{l}")
                evacuated(dve, f"ms{l}", 7)
                center(f"mean{3 * l + 2}", zT, 8, centered, 2)
                normalise(3 * l + 2)
            cm["y"]()

        @block.scalar
        def _(act):
            cm = common(act, "s")
            act.dma_start(cst[:, :], const).then_inc(in_const, 16)
            act.dma_start(prow[0:6, :], ln_g.rearrange("l k d -> (l k) d")).then_inc(in_rows, 16)
            act.dma_start(prow[6:12, :], ln_b.rearrange("l k d -> (l k) d")).then_inc(in_rows, 16)
            act.dma_start(prow[12:13, :], sgu_ln_g).then_inc(in_rows, 16)
            act.dma_start(prow[13:14, :], sgu_ln_b).then_inc(in_rows, 16)
            act.dma_start(crow[0:31, :], conv_w[0]).then_inc(in_rows, 16)
            for i, w in enumerate((conv_b, conv_ln_g, conv_ln_b)):
                act.dma_start(crow[31 + i:32 + i, :], w).then_inc(in_rows, 16)
            for t in range(2):
                act.dma_start(strow[0:120, t, :], state_conv[0, 4 * t:4 * t + 4].rearrange("b t c -> (b t) c")).then_inc(in_rows, 16)
            act.dma_start(wrt[:, :, :], w_router.rearrange("(k p) e -> p k e", p=P)).then_inc(in_rows, 16)
            act.dma_start(rbias[:, :], router_bias.rearrange("(a e) -> a e", a=1).to_broadcast([P, NE])).then_inc(in_misc, 16)
            act.dma_start(tab, table).then_inc(in_table, 16)
            act.wait_ge(rb_zero, 1)
            for j in range(4):
                act.dma_start(RB4[32 * j:32 * j + 32, 8 * j:8 * j + 8], rel_bias).then_inc(rb_in, 16)
            cm["x"]()
            cm["q"]()
            cm["k"]()
            cm["v"]()
            for i in range(4):
                full(act, "g", i)
                act.activation(zT[:, i, :], ACC("g", i)[:, 0:NTOK], ACT.Sigmoid).then_inc(emptied["s"], 1)
            cm["state"]()
            for i in range(2):
                full(act, "sbias", i)
                act.activation(SBIAS[:, 512 * i:512 * i + 512], ACC("sbias", i), ACT.Copy).then_inc(emptied["s"], 1)
            evacuated(act, "a", 3)
            cm["ktok"]()
            act.wait_ge(negmax, 1)
            for h in range(8):
                for t in range(2):
                    r = slice(0, 128) if t == 0 else slice(128, 384)
                    act.activation(SALL[:, h, r], SALL[:, h, r], ACT.Exp, bias=st[:, 16 + 8 * t + h:17 + 8 * t + h],
                                   accum_out=st[:, 32 + 8 * t + h:33 + 8 * t + h]).then_inc(exp_done, 1)
            cm["kt"](0)
            cm["cnew"]()
            ptpo(act, "s", PTPO)

            def sample_softmax(g):
                act.wait_ge(negmax, 2 + g)
                for j in range(5):
                    r = slice(MOBA * j, MOBA * j + MOBA) if j < 4 else slice(PAST, PAST + 32)
                    act.activation(SS[:, r], SS[:, r], ACT.Exp, bias=st[:, 88 + j:89 + j],
                                   accum_out=st[:, 96 + j:97 + j]).then_inc(exp_done, 1)

            def weighted_values(g):
                act.wait_ge(smp_out, g + 1)
                act.activation(PV, psV[:, :], ACT.Copy).then_inc(smp_read, 1)

            for b in (1, 2, 3):
                cm["kt"](b)
            sample_softmax(0)
            cm["spt"](0)
            weighted_values(0)
            for b in (4, 5, 6, 7):
                cm["kt"](b)

            def root(signal, stage):
                evacuated(act, stage, 0)
                act.activation(std[:, :], rs[:, :], ACT.Sqrt).then_inc(signal, 1)

            evacuated(act, "cmean", 0)
            act.wait_ge(out_even, 16 * 2)
            act.activation(zT[:, 0:4, :], mixT[:, 4:8, :], ACT.Square).then_inc(sq_c, 1)
            root(std_c, "cvar")
            for f in range(4):
                act.wait_ge(scl_c, f + 1)
                act.activation(mixT[:, 4 + f, :], mixT[:, 4 + f, :], ACT.Silu, bias=cparT[:, f, 33:34],
                               scale=cparT[:, f, 32:33]).then_inc(cv_ready, 1)
            sample_softmax(1)
            cm["spt"](1)
            weighted_values(1)

            def squares(nth):
                for c in range(4):
                    if c < 3:
                        act.wait_ge(centered, 3 * nth + c + 1)
                    else:
                        evacuated(act, f"mean{nth}", 0)
                    act.activation(mixT[:, 2 * c:2 * c + 2, :], zT[:, 2 * c:2 * c + 2, :], ACT.Square).then_inc(squared, 1)

            def finish(nth):
                root(std_ready, f"var{nth}")
                for f in range(8):
                    act.wait_ge(scaled, 8 * nth + f + 1)
                    act.activation(xT[:, f, :], zT[:, f, :], ACT.Identity, bias=parT[:, f, 6 + nth:7 + nth]).then_inc(x_ready, 1)

            for l in range(DEPTH):
                if l:
                    for i in range(8):
                        full(act, "u", i)
                        act.activation(qT[:, i, :], ACC("u", i)[:, 0:NTOK], ACT.Gelu).then_inc(emptied["s"], 1)
                    for i in range(8):
                        full(act, "vv", i)
                        act.activation(vT[:, i, :], ACC("vv", i)[:, 0:NTOK], ACT.Gelu).then_inc(emptied["s"], 1)
                    for c in range(4):
                        if c < 3:
                            act.wait_ge(cen_v, c + 1)
                        else:
                            evacuated(act, "vmean", 0)
                        act.activation(mixT[:, 2 * c:2 * c + 2, :], vT[:, 2 * c:2 * c + 2, :], ACT.Square).then_inc(sq_v, 1)
                    root(std_v, "vvar")
                    for f in range(8):
                        act.wait_ge(scl_v, f + 1)
                        act.activation(vT[:, f, :], vT[:, f, :], ACT.Identity, bias=parT[:, f, 13:14]).then_inc(vn_ready, 1)
                    cm["vtok"]()
                squares(3 * l)
                evac(act, "s", f"memT{l}", 8, lambda i, a: act.activation(memT[:, i, :], a[:, 0:256], ACT.Copy))
                finish(3 * l)
                cm["mk"](l)
                cm["mv"](l)
                cm["mktok"](l)
                cm["xq"](l)
                nm = 3 + 6 * l
                for h in range(4):
                    act.wait_ge(negmax, nm + h + 1)
                    for t in range(2):
                        ins = act.activation(PX[:, 2 * h + t, :], ACC(f"xs{l}", h)[:, 256 * t:256 * t + 256], ACT.Exp,
                                             bias=st[:, 16 + 2 * h + t:17 + 2 * h + t],
                                             accum_out=st[:, 32 + 2 * h + t:33 + 2 * h + t])
                    ins.then_inc(emptied["s"], 1)
                for b in range(4):
                    cm["xkt"](l, b)

                def mem_softmax(g):
                    act.wait_ge(negmax, nm + 4 + g + 1)
                    act.activation(XP[:, g, :], psS[:, 0, 0:256], ACT.Exp, bias=st[:, 65 + g:66 + g],
                                   accum_out=st[:, 68 + g:69 + g]).then_inc(exp_done, 1)

                def mem_rows(g):
                    act.wait_ge(values_used, DB * (1 + l) + 4 * g + 4)
                    act.activation(XPV[:, 0, :], psV[:, :], ACT.Copy).then_inc(xpv_ready, 1)

                ptpo(act, "s", XPTPO, l)
                mem_softmax(0)
                mem_rows(0)
                for b in range(4, 8):
                    cm["xkt"](l, b)
                mem_softmax(1)
                mem_rows(1)
                squares(3 * l + 1)
                finish(3 * l + 1)
                full(act, f"router{l}", 0)
                act.activation(RT[:, 48:96], ACC(f"router{l}", 0)[:, 0:48], ACT.Sigmoid)\
                    .then_inc(emptied["s"], 1)
                act.wait_ge(out_mem, 32 * (l + 1))
                cm["xtok"](l)
                cm["xg"](l)

                def chunk(S, n, at, bank):
                    for j in range(4):
                        act.wait_ge(S.gate_up, 4 * n + j + 1)
                        act.activation(SG[:, j, :], psS[:, j % 2, 0:CAP], ACT.Silu).then_inc(S.silu, 1)
                    act.wait_ge(S.down, 2 * n + 1)
                    act.activation(YT[:, 0:4, at], bank[:, 0:4 * CAP].rearrange("p (f m) -> p f m", f=4), ACT.Copy).then_inc(S.y_act, 1)

                act.wait_ge(ranks_ready, l + 1)
                act.activation(SG[:, 0, 0:1], cst[:, 0:1], ACT.Copy).then_inc(first.y_act, 1)
                act.wait_ge(first.y_act, (NE + 1) * l + 1)
                with act.Fori(0, NE // 2) as i:
                    for e in range(2):
                        n = 2 * i + e
                        start = act.value_load(STARTI[0:1, bass.ds(n, 1)], min_val=0, max_val=NROW)
                        chunk(first, NE * l + n, bass.ds(start, CAP), acc[:, 0, :])
                        extra = act.value_load(MOREI[0:1, bass.ds(n, 1)], min_val=0, max_val=NFURTHER)
                        with act.If(extra > 0):
                            before = act.value_load(BEFOREI[0:1, bass.ds(n, 1)], min_val=0, max_val=NROW // CAP)
                            with act.Fori(0, extra) as c:
                                chunk(more[l], before + c, further(start, c), psN[:, :])
                cm["gt"](l)
                cm["yt"](l)
                squares(3 * l + 2)
                finish(3 * l + 2)
            cm["y"]()

        @block.gpsimd
        def _(pool):
            evacuated(pool, "dbias", 3)
            pool.affine_select(out=BIAS[:, :, 0:128], in_=BIAS[:, :, 0:128], pattern=[[0, 8], [-1, 128]],
                               compare_op=ALU.is_ge, fill=NEG, base=0, channel_multiplier=1).then_inc(bias_masked, 1)
            pool.affine_select(out=BIAS[:, :, 128:384], in_=BIAS[:, :, 128:384], pattern=[[0, 8], [-1, 256]],
                               compare_op=ALU.is_ge, fill=NEG, base=128, channel_multiplier=1).then_inc(bias_masked, 1)
            evacuated(pool, "v", 0), evacuated(pool, "v", 1), evacuated(pool, "v", 2)
            kv = "l (t p) h d -> p (l t) (h d)"
            pool.dma_start(new_v_prompt[0].rearrange(kv, p=P), vtok[:, 0:2, :]).then_inc(out_rest, 16)
            pool.dma_start(new_v_sample[0].rearrange("b s h d -> (b s) (h d)"), vtok[0:32, 2, :]).then_inc(out_rest, 16)
            pool.dma_start(new_conv_sample[0, :, 0:26, :], state_conv[0, :, 4:30, :]).then_inc(out_rest, 16)
            for i in range(3):
                evacuated(pool, "ktok", i)
            pool.dma_start(new_k_prompt[0].rearrange(kv, p=P), ktok[:, 0:2, :]).then_inc(out_even, 16)
            pool.dma_start(new_k_sample[0].rearrange("b s h d -> (b s) (h d)"), ktok[0:32, 2, :]).then_inc(out_even, 16)
            evacuated(pool, "cnew", 0), evacuated(pool, "cnew", 1)
            pool.dma_start(new_conv_prompt[0, 0], cnew[0:30, 0, :]).then_inc(out_rest, 16)
            pool.dma_start(new_conv_sample[0, :, 26:30, :], cnew[0:32, 1, :]).then_inc(out_rest, 16)
            for l in range(DEPTH):
                if l:
                    evacuated(pool, "vtok", 4), evacuated(pool, "vtok", 5)
                    pool.dma_start(new_gmlp_v[0].rearrange("b s d -> (b s) d"), gvtok[0:32, 2, :]).then_inc(out_rest, 16)
                if l:
                    pool.wait_ge(mixed, 8)
                else:
                    pool.wait_ge(smp_out, 2)
                    pool.wait_ge(out_rest, 16 * 5)
                pool.dma_start(memtok, mem_prompt[0].rearrange("(t p) d -> p t d", p=P)).then_inc(mem_in, 16)
                for i in range(4):
                    evacuated(pool, f"mv{l}", i), evacuated(pool, f"mktok{l}", i)
                pool.dma_start(new_mem_v[l, 0].rearrange("(t p) h d -> p t (h d)", p=P), mvtok).then_inc(out_mem, 16)
                pool.dma_start(new_mem_k[l, 0].rearrange("(t p) h d -> p t (h d)", p=P), mktok).then_inc(out_mem, 16)
                evacuated(pool, f"xpvt{l}1", 1)
                if l == 0:
                    pool.memset(WBD, 0.0).then_inc(wbd_zero, 1)
                    pool.wait_ge(wbd_zero, 1)
                    pool.dma_start(WLD, sgu_w[0].rearrange("g t s -> t g s")).then_inc(g_in, 16)
                    pool.dma_start(BSG, sgu_b.rearrange("a g t -> a (g t)").to_broadcast([P, D])
                                   .rearrange("p (g t) -> p g t", g=8)).then_inc(g_in, 16)
                    for b in range(DB):
                        for g in range(8):
                            pool.dma_start(WBD[4 * b:4 * b + 4, g, 4 * b:4 * b + 4],
                                           sgu_w[0, g, 0:4, 0:4].rearrange("t s -> s t"),
                                           allow_slow_non_contiguous=True).then_inc(wbd_in, 16)
                    pool.wait_ge(g_in, 32)
                    pool.affine_select(out=WLD, in_=WLD, pattern=[[0, 8], [-1, 128]], compare_op=ALU.is_ge, fill=0.0,
                                       base=0, channel_multiplier=1).then_inc(w_masked, 1)
                    pool.wait_ge(wbd_in, 16 * 64)
                    pool.affine_select(out=WBD, in_=WBD, pattern=[[0, 8], [1, 32]], compare_op=ALU.is_ge, fill=0.0,
                                       base=0, channel_multiplier=-1).then_inc(w_masked, 1)
            for i in range(6):
                evacuated(pool, "y", i)
            pool.dma_start(y_prompt[0].rearrange("(t p) d -> p t d", p=P), ytok[:, 0:2, :]).then_inc(out_rest, 16)
            pool.dma_start(y_sample.rearrange("b s d -> (b s) d"), ytok[0:32, 2, :]).then_inc(out_rest, 16)
            pool.wait_ge(out_rest, 16 * 8)
            pool.wait_ge(out_even, 32)
            pool.wait_ge(out_mem, 32 * DEPTH)


_INS = ['x_prompt', 'x_sample', 'cache_k', 'cache_v', 'state_conv', 'cache_mem_k', 'cache_mem_v', 'page_table',
        'mem_prompt', 'rel_bias', 'w_in_even', 'conv_w', 'conv_b', 'conv_ln_g', 'conv_ln_b', 'w_out_even',
        'w_in_odd', 'sgu_ln_g', 'sgu_ln_b', 'sgu_w', 'sgu_b', 'w_out_odd', 'w_xq', 'w_xkv', 'w_xo',
        'w_router', 'router_bias', 'w_exp_gate', 'w_exp_up', 'w_exp_down', 'ln_g', 'ln_b']
_OUTS = [(1, SEQ, D), (DB, DS, D), (1, 1, SEQ, HA, HD), (1, 1, SEQ, HA, HD), (1, DB, DS, HA, HD), (1, DB, DS, HA, HD),
         (1, 1, CW - 1, CC), (1, DB, CW - 1, CC), (DEPTH, 1, NMEM, HX, HDX), (DEPTH, 1, NMEM, HX, HDX),
         (1, DB, DS, D)]


def kernel(**inputs):
    import numpy as _np
    import concourse.bacc as _bacc
    from concourse import mybir as _mybir
    from concourse.bass_utils import run_bass_kernel_spmd as _run

    nc = _bacc.Bacc("TRN2", target_bir_lowering=False, num_devices=1)
    consts = dict(zip(("const", "table"), shape_constants()))
    arrays, args = {}, []
    for name in _INS + list(consts):
        a = _np.ascontiguousarray(inputs[name] if name in inputs else consts[name])
        arrays[f"in_{name}"] = a
        args.append(nc.dram_tensor(f"in_{name}", a.shape, _mybir.dt.from_np(a.dtype), kind="ExternalInput").ap())
    for i, shape in enumerate(_OUTS):
        args.append(nc.dram_tensor(f"out_{i}", shape, _mybir.dt.float32, kind="ExternalOutput").ap())
    build(nc, *args)
    r = _run(nc, [arrays], core_ids=[0])
    return tuple(r.results[0][f"out_{i}"] for i in range(len(_OUTS)))
```

```python
from contextlib import ExitStack

import numpy as np

import concourse.bass as bass
from concourse import mybir

ALU = mybir.AluOpType
ACT = mybir.ActivationFunctionType
X = mybir.AxisListType.X
F32 = mybir.dt.float32
I32 = mybir.dt.int32
BF16 = mybir.dt.bfloat16

P = 128
D = 1024
SEQ = 256
DB, DS = 8, 4
NTOK = SEQ + DB * DS
S0 = SEQ
DEPTH = 2
PAST, PAGE = 1024, 128
NPAGE = PAST // PAGE
NPHYS = DB * NPAGE * 5 // 4
HA, HD = 8, 64
CC, CW = 512, 31
NB_BUCKET, MAXDIST = 32, 128
NMEM, HX, HDX = 256, 4, 256
NE, NG, EPG, DFF = 16, 4, 4, 512
FT = D // P
ALPHA = (2 * DEPTH) ** 0.25
EPS = 1e-5
NEG = -1e30
MOBA = 256

SLOTS = 6
UNIT = 8 * 512
NACC = 4

C_ID, C_OWN, C_IDX, C_FIRST, C_TRI = 0, 128, 192, 196, 200
C_BEFORE, C_SLOT, C_ONCE = 216, 344, 632
NCONST = 680
CAP = 64
NROW = 2 * NTOK
SLOTTED = NROW + CAP
NST = -(-NROW // P)
NFURTHER = -(-NTOK // CAP) - 1
T_OH4, T_OHS = 0, 380
NTABLE = 380 + PAST + DB * DS


def bucket(n):
    n = np.maximum(n, 0)
    half = NB_BUCKET // 2
    nf = np.maximum(n, 1).astype(np.float32)
    large = half + (np.log(nf / np.float32(half)) / np.float32(np.log(MAXDIST / half))
                    * np.float32(NB_BUCKET - half)).astype(np.int32)
    return np.where(n < half, n, np.minimum(large, NB_BUCKET - 1))


def shape_constants():
    c = np.zeros((P, NCONST), np.float32)
    c[:, C_ID:C_ID + P] = np.eye(P)
    row = np.arange(P)
    b4, q = row // 32, row % 4
    for g in range(2):
        for b in range(DB):
            for j in range(DS):
                seen = (b == 4 * g + b4) & (j <= q)
                c[:, C_OWN + 32 * g + 4 * b + j] = np.where(seen, 0.0, NEG)
    c[:, C_IDX:C_IDX + 4] = np.arange(1, 5)
    c[:, C_FIRST:C_FIRST + 4] = np.arange(4, 0, -1)
    e = np.arange(4)
    c[:, C_TRI:C_TRI + 16] = (e[None, :] < e[:, None]).astype(np.float32).reshape(-1)
    c[:, C_BEFORE:C_BEFORE + P] = row[:, None] < row[None, :]
    c[:, C_SLOT:C_SLOT + NTOK] = np.arange(1, NTOK + 1)
    c[:, C_ONCE:C_ONCE + 48] = 1
    c[:P - 32, C_ONCE + 32:C_ONCE + 48] = 0
    t = np.zeros((P, NTABLE), np.float32)
    for j in range(4):
        n = np.arange(380) - 252 + 128 - j
        t[32 * j + bucket(n)[n >= 0], T_OH4 + np.arange(380)[n >= 0]] = 1
        k = np.arange(PAST)
        t[32 * j + bucket(PAST + j - k), T_OHS + k] = 1
        for b in range(DB):
            for i in range(j + 1):
                t[32 * j + bucket(np.array(j - i)), T_OHS + PAST + 4 * b + i] = 1
    return c, t


def unit_order():
    u = [("in_even", n) for n in (0, 1, 2, 4, 3)]
    u += [("K", b) for b in range(6)] + [("V", b) for b in range(4)]
    u += [("K", b) for b in (6, 7)] + [("xkv", 0, 0)] + [("V", b) for b in range(4, 8)] + [("xkv", 0, 1)]
    for l in range(DEPTH):
        if l:
            u += [("in_odd", n) for n in range(4)]
        u += [("out", l, n) for n in range(2)]
        u += [("xkv", l, n) for n in range(4) if l or n > 1]
        u += [("xq", l, n) for n in range(2)]
        u += [("memK", l, 0), ("memK", l, 1), ("memK", l, 2), ("memV", l, 0), ("memV", l, 1), ("memK", l, 3),
              ("memV", l, 2), ("memV", l, 3)]
        u += [("xo", l, n) for n in range(2)]
        u += [("moe", l, n) for n in range(3 * NE)]
    return u


def tile_order():
    t = []

    def add(stage, n, owners):
        t.extend((stage, i, owners[i % len(owners)]) for i in range(n))

    add("x", 8, "vs")
    add("q", 4, "vs")
    add("k", 4, "vs")
    add("v", 3, "vs")
    add("g", 4, "s")
    add("a", 4, "v")
    add("par", 1, "v")
    add("cpar", 1, "v")
    add("state", 4, "vs")
    add("dbias", 4, "v")
    add("sbias", 3, "ssv")
    add("ktok", 3, "vs")
    add("kt0", 8, "s")
    add("ps", 8, "v")
    add("cnew", 2, "vs")
    add("kt1", 8, "s")
    add("kt2", 8, "s")
    for s, i in PTPO:
        t.append((s, i, "vs"[i % 2]))
    for b in (3, 4, 5):
        add(f"kt{b}", 8, "s")
    add("spt0", 3, "svs")
    add("pvt0", 1, "s")
    for b in (6, 7):
        add(f"kt{b}", 8, "s")
    add("memT0", 8, "s")
    add("mk0", 2, "s")
    add("spt1", 3, "svs")
    add("pvt1", 1, "s")
    add("cmean", 1, "v")
    t.append(("mk0", 2, "s"))
    add("cvar", 1, "v")
    t.append(("mk0", 3, "s"))
    for l in range(DEPTH):
        if l:
            add("u", 8, "s")
            add("vv", 8, "s")
            add("vmean", 1, "v")
            add("vvar", 1, "v")
            add("wm", 2, "v")
            add("vtok", 6, "vs")
            add("mix", 8, "v")
        add(f"o{l}", 8, "v")
        add(f"mean{3 * l}", 1, "v")
        if l:
            add(f"memT{l}", 8, "s")
        else:
            t += [(f"mv{l}", i, "s") for i in range(2)]
        add(f"var{3 * l}", 1, "v")
        if l == 0:
            t += [(f"mv{l}", i, "s") for i in (2, 3)]
        else:
            add(f"mk{l}", 4, "vs")
            add(f"mv{l}", 4, "vs")
        add(f"xq{l}", 8, "vs")
        add(f"xs{l}", 4, "s")
        for b in range(4):
            add(f"xkt{l}{b}", 4, "vs")
        for s, i in XPTPO:
            t.append((f"{s}{l}", i, "vs"[i % 2]))
        for b in (4, 5):
            add(f"xkt{l}{b}", 4, "vs")
        add(f"xspt{l}0", 1, "v")
        add(f"xpvt{l}0", 2, "v")
        for b in (6, 7):
            add(f"xkt{l}{b}", 4, "vs")
        add(f"xspt{l}1", 1, "v")
        add(f"xpvt{l}1", 2, "v")
        add(f"xo{l}", 8, "v")
        add(f"mean{3 * l + 1}", 1, "v")
        add(f"mktok{l}", 4, "vvss")
        add(f"var{3 * l + 1}", 1, "v")
        add(f"router{l}", 1, "s")
        add(f"xtok{l}", 6, "s")
        add(f"rank{l}", 1, "v")
        add(f"xg{l}", 2 * FT, "vs")
        add(f"gt{l}", NST, "vs")
        add(f"yt{l}", 2 * NST, "vs")
        add(f"ms{l}", 8, "v")
        add(f"mean{3 * l + 2}", 1, "v")
        add(f"var{3 * l + 2}", 1, "v")
    add("y", 6, "vs")
    return t


PTPO = [("pt", 0), ("pt", 1), ("pt", 2), ("pt", 3), ("po", 0), ("pt", 4), ("pt", 5), ("po", 1),
        ("pt", 6), ("pt", 7), ("po", 2), ("po", 3)]
XPTPO = [("xpt", 0), ("xpt", 1), ("xpo", 0), ("xpt", 2), ("xpo", 1), ("xpt", 3), ("xpo", 2), ("xpo", 3)]


def build(nc, x_prompt, x_sample, cache_k, cache_v, state_conv, cache_mem_k, cache_mem_v, page_table,
          mem_prompt, rel_bias, w_in_even, conv_w, conv_b, conv_ln_g, conv_ln_b, w_out_even, w_in_odd,
          sgu_ln_g, sgu_ln_b, sgu_w, sgu_b, w_out_odd, w_xq, w_xkv, w_xo, w_router, router_bias,
          w_exp_gate, w_exp_up, w_exp_down, ln_g, ln_b, const, table,
          y_prompt, y_sample, new_k_prompt, new_v_prompt, new_k_sample, new_v_sample,
          new_conv_prompt, new_conv_sample, new_mem_k, new_mem_v, new_gmlp_v):
    units = unit_order()
    UIDX = {u: i for i, u in enumerate(units)}
    tiles = tile_order()
    TIDX = {(s, i): n for n, (s, i, _) in enumerate(tiles)}
    OWNER = [o for _, _, o in tiles]
    CUM = {"v": [0], "s": [0]}
    for o in OWNER:
        for k in "vs":
            CUM[k].append(CUM[k][-1] + (o == k))

    with ExitStack() as ctx:
        def sb(name, shape, dt=F32):
            return ctx.enter_context(nc.sbuf_tensor(name, shape, dt))

        def sem(name):
            return ctx.enter_context(nc.semaphore(name))

        ring = sb("ring", [P, SLOTS, UNIT])
        xT = sb("xT", [P, FT, NTOK])
        zT = sb("zT", [P, FT, NTOK])
        mixT = sb("mixT", [P, FT, NTOK])
        qT = sb("qT", [P, FT, NTOK])
        arena = sb("arena", [P, 17408])
        cst = sb("cst", [P, NCONST])
        ones_d = sb("ones_d", [P, P])
        parT = sb("parT", [P, FT, 14])
        cparT = sb("cparT", [P, 4, 34])
        wrt = sb("wrt", [P, FT, NE])
        rbias = sb("rbias", [P, NE])
        rs = sb("rs", [P, NTOK])
        std = sb("std", [P, NTOK])
        st = sb("st", [P, 112])
        pages = sb("pages", [1, DB * NPAGE], I32)
        acc = ctx.enter_context(nc.psum_tensor("acc", [P, NACC, 512], F32))
        psS = ctx.enter_context(nc.psum_tensor("psS", [P, 2, 512], F32))
        psN = ctx.enter_context(nc.psum_tensor("psN", [P, 512], F32))
        psV = ctx.enter_context(nc.psum_tensor("psV", [P, 512], F32))

        def view(off, *shape):
            n = int(np.prod(shape))
            v = arena[:, off:off + n]
            if len(shape) == 2:
                return v.rearrange("p (a b) -> p a b", b=shape[1])
            if len(shape) == 3:
                return v.rearrange("p (a b c) -> p a b c", b=shape[1], c=shape[2])
            return v

        def flat(t, a, b):
            return t.rearrange("p f m -> p (f m)")[:, 0:a * b].rearrange("p (a b) -> p a b", b=b)

        ident = cst[:, C_ID:C_ID + P]
        KT = view(0, 2, 4, 512)
        tab = view(0, NTABLE)
        prow = view(1536, 1024)
        crow = view(2560, 512)
        strow = view(3072, 2, 512)
        BIAS = view(4096, 8, 384)
        QBD = qT[:, 4:8, :].rearrange("p f m -> p (f m)")[:, 0:1024].rearrange("p (b f m) -> p b f m", f=4, m=32)
        cnew = view(6144, 2, 512)
        SALL = view(7168, 8, 384)
        xtok = view(7168, 3, 1024)
        SS = view(7168, 1056)
        PTS = view(8224, 9, 128)
        PV = view(9376, 512)
        UP = view(10240, 4, 286)
        US = view(11384, 4, 8, 34)
        kT = view(12472, 4, NTOK)
        vtok = view(13624, 3, 512)
        SBIAS = view(15160, 1024)
        OBIAS = view(16184, 2, 32)
        PTP = view(16248, 2, 384)
        RB4 = view(17016, 32)
        SBL = view(17048, 128)
        ucmp = std[:, 0:128].rearrange("p (f m) -> p f m", f=4)
        tab16 = rs[:, 0:190].bitcast(BF16)
        RB16 = rs[:, 190:238].bitcast(BF16).rearrange("p (c m) -> p c m", c=3)
        rb_rest = rs[:, 238:270]
        ones_c = view(17176, P)
        ktok = zT[:, 0:6, :].rearrange("p a b -> p (a b)")[:, 0:1536].rearrange("p (a b) -> p a b", b=512)
        memT = view(0, 8, 256)
        XP = view(0, 2, 256)
        XPTS = view(512, 2, 128)
        XPV = view(768, 2, 512)
        mkT = view(2048, 8, 256)
        mvtok = view(4096, 2, 1024)
        mktok = view(6144, 2, 1024)
        PX = view(8192, 8, 256)
        XPT = view(10240, 2, 512)
        QX = arena[:, 11264:13312].rearrange("p (b f m) -> p b f m", f=8, m=32)
        MKT = view(13312, 2, 8, 256)
        memtok = view(4096, 2, 1024)
        XE = view(0, FT, SLOTTED + CAP)
        YT = view(5632, FT, SLOTTED)
        XTOK = view(5632, 3, 1024)
        YTOK = view(0, NST, 1024)
        G = flat(zT, 3, NROW)
        GW = flat(mixT, 3, NROW)
        GT = flat(qT, NST, NTOK)
        XS = view(10752, FT, CAP)
        XSM = view(15104, FT, CAP)
        SG = view(16128, DFF // 2)
        H = view(16384, DFF // 2)
        HT = view(16640, 2, 2 * CAP)
        YS = view(16896, 512)
        POS = view(11264, 3, NE)
        COMB = view(11312, 3, NE)
        MASK = view(11360, 3, NE)
        PICK = view(11408, 3, NE)
        CNT = view(11456, NE)
        MORE = view(11472, NE)
        START = view(11488, NE)
        SCAN = view(11504, NE)
        ROW = view(11520, 2, 3)
        ROWB = view(11526, 2, 3)
        WT = view(11532, 2, 3)
        ones = view(11552, P)
        GA = view(8704, 3, NTOK)
        START17 = view(12064, 2 * NE)
        STARTI, MOREI, BEFOREI = (arena[:, a:b].bitcast(I32) for a, b in ((12064, 12096), (12096, 12112), (12112, 12128)))
        RT = arena[:, 12128:12128 + 672]
        vT = view(0, 8, NTOK)
        gvtok = view(2304, 3, 1024)
        WLD = view(12800, 8, 128)
        BSG = view(13824, 8, 128)
        WBD = arena[0:32, 14848:15104].rearrange("p (g t) -> p g t", g=8)
        WMT = view(15104, 8, 128)
        ytok = view(0, 3, 1024)

        unit_in = [sem(f"unit_in{i}") for i in range(SLOTS)]
        values_used = sem("values_used")
        acc_full = sem("acc_full")
        emptied = {"v": sem("emptied_by_dve"), "s": sem("emptied_by_act")}
        in_x = sem("in_x")
        in_const = sem("in_const")
        in_rows = sem("in_rows")
        in_table = sem("in_table")
        in_rb = sem("sample_bias_operand")
        rb_zero = sem("rb_zero")
        rb_split = sem("rb_split")
        rb_in = sem("rb_in")
        in_misc = sem("in_router_bias")
        in_pages = sem("in_pages")
        ones_set = sem("ones_set")
        dve_step = sem("dve_step")
        conv_step = sem("conv_step")
        conv_pool = sem("conv_pool")
        bias_masked = sem("bias_masked")
        qbd_ready = sem("qbd_ready")
        scores_full = sem("scores_full")
        scores_read = sem("scores_read")
        negmax = sem("negmax")
        exp_done = sem("exp_done")
        probs = sem("probs")
        smp_out = sem("smp_out")
        smp_read = sem("smp_read")
        centered = sem("centered")
        squared = sem("squared")
        std_ready = sem("std_ready")
        scaled = sem("scaled")
        x_ready = sem("x_ready")
        sq_c = sem("conv_squared")
        std_c = sem("conv_std")
        scl_c = sem("conv_scaled")
        cv_ready = sem("conv_ready")
        cen_v = sem("v_centered")
        sq_v = sem("v_squared")
        std_v = sem("v_std")
        scl_v = sem("v_scaled")
        vn_ready = sem("v_ready")
        mem_in = sem("mem_in")
        qx_ready = sem("qx_ready")
        comb_ready = sem("comb_ready")
        ranks_ready = sem("ranks_ready")
        rows_ready = sem("rows_ready")
        weights_ready = sem("weights_ready")

        class Item:

            def __init__(self, tag):
                self.xs = sem(f"{tag}_x_rows")
                self.gate = sem(f"{tag}_gate")
                self.parts = sem(f"{tag}_parts")
                self.silu = sem(f"{tag}_silu")
                self.h = sem(f"{tag}_h")
                self.turned = sem(f"{tag}_h_turned")
                self.ht = sem(f"{tag}_ht")
                self.down = sem(f"{tag}_down")
                self.y = sem(f"{tag}_y")
                self.y_turned = sem(f"{tag}_y_turned")
                self.yt = sem(f"{tag}_yt")

        first = Item("first")

        def matrix_done(sp, j, n):
            sp.wait_ge((first.gate, first.parts, first.down)[j], 2 * n if j == 1 else n)

        more = [Item(f"more{l}") for l in range(DEPTH)]
        g_in = sem("gmlp_in")
        wbd_zero = sem("wbd_zero")
        wbd_in = sem("wbd_in")
        w_masked = sem("w_masked")
        mixed = sem("mixed")
        out_even = sem("out_even")
        out_mem = sem("out_mem")
        out_rest = sem("out_rest")

        kt_read = sem("kt_read")
        xk_read = sem("xk_read")
        xpv_ready = sem("xpv_ready")

        def further(start, c):
            return bass.ds(nc.s_assert_within(start + CAP + CAP * c, 0, NROW,
                                              skip_runtime_bounds_check_because="the chunk holds a row of its expert"), CAP)

        def after_further(start, c):
            return bass.ds(nc.s_assert_within(start + 2 * CAP + CAP * c, 0, NROW + CAP,
                                              skip_runtime_bounds_check_because="the chunk before holds a row of its expert"), CAP)

        def ACC(stage, i):
            return acc[:, TIDX[stage, i] % NACC, :]

        def full(eng, stage, i):
            eng.wait_ge(acc_full, TIDX[stage, i] + 1)

        def bank_free(pe, stage, i):
            n = TIDX[stage, i] - NACC
            if n >= 0:
                o = OWNER[n]
                pe.wait_ge(emptied[o], CUM[o][n + 1])

        def evacuated(eng, stage, i):
            n = TIDX[stage, i]
            eng.wait_ge(emptied[OWNER[n]], CUM[OWNER[n]][n + 1])

        def owned(who, stage, n):
            return [i for i in range(n) if OWNER[TIDX[stage, i]] == who]

        def slot(u):
            return ring[:, u % SLOTS, :]

        LANDED = []
        total = [0] * SLOTS
        for n, k in enumerate(units):
            total[n % SLOTS] += 16 * (8 if k[0] in "KV" else 2 if k[0][:3] == "mem" else 1)
            LANDED.append(total[n % SLOTS])

        def arrived(eng, u, more=0):
            eng.wait_ge(unit_in[u % SLOTS], LANDED[u] + more)

        def xr(nth):
            return 8 * (nth + 1)

        READER = {("in_even", 0): ("q", 3), ("in_even", 1): ("k", 3), ("in_even", 2): ("v", 2),
                  ("in_even", 4): ("g", 3), ("in_even", 3): ("a", 3)}
        for b in range(DB):
            READER["K", b] = (f"kt{b}", 7)
        for n in range(4):
            READER["in_odd", n] = (("u", "vv")[n // 2], 4 * (n % 2) + 3)
        for l in range(DEPTH):
            for n in range(4):
                READER["memK", l, n] = (f"xkt{l}{2 * n + 1}", 3)
            for n in range(2):
                READER["out", l, n] = (f"o{l}", 4 * n + 3)
                READER["xq", l, n] = (f"xq{l}", 4 * n + 3)
                READER["xo", l, n] = (f"xo{l}", 4 * n + 3)
                READER["xkv", l, n] = (f"mk{l}", 2 * n + 1)
                READER["xkv", l, 2 + n] = (f"mv{l}", 2 * n + 1)

        def slot_free(sp, u):
            if u < SLOTS:
                return
            k = units[u - SLOTS]
            if k[0] == "moe":
                matrix_done(sp, k[2] % 3, NE * k[1] + k[2] // 3 + 1)
            elif k[0] in ("V", "memV"):
                sp.wait_ge(values_used, 1 + k[1] if k[0] == "V" else DB * (1 + k[1]) + 2 * k[2] + 2)
            else:
                sp.wait_ge(acc_full, TIDX[READER[k]] + 1)

        block = ctx.enter_context(nc.Block())

        @block.sync
        def _(sp):
            sp.dma_start(xtok[:, 0:2, :], x_prompt[0].rearrange("(t p) d -> p t d", p=P)).then_inc(in_x, 16)
            sp.dma_start(xtok[0:32, 2, :], x_sample.rearrange("b s d -> (b s) d")).then_inc(in_x, 16)
            sp.dma_start(pages[:, :], page_table.rearrange("(a b) n -> a (b n)", a=1)).then_inc(in_pages, 16)

            def mat(w, n):
                return w[:, 512 * n:512 * n + 512].rearrange("(k p) n -> p k n", p=P)

            def load(u, dst8):
                kind = units[u]
                s = unit_in[u % SLOTS]
                if kind[0] in "KV":
                    cache = cache_k if kind[0] == "K" else cache_v
                    for p in range(NPAGE):
                        at = kind[1] * NPAGE + p
                        page = sp.value_load(pages[0:1, at:at + 1], min_val=0, max_val=NPHYS - 1)
                        sp.dma_start(dst8[:, p, :],
                                     cache[0, bass.ds(page, 1)].rearrange("a t h d -> (a t) (h d)")).then_inc(s, 16)
                    return
                if kind[0][:3] == "mem":
                    _, l, i = kind
                    m = cache_mem_k if kind[0] == "memK" else cache_mem_v
                    d2 = slot(u).rearrange("p (c t n) -> p c t n", c=2, n=1024)
                    for c in range(2):
                        sp.dma_start(d2[:, c], m[l, 2 * i + c].rearrange("(t p) h d -> p t (h d)", p=P)).then_inc(s, 16)
                    return
                if kind[0] == "in_even":
                    src = mat(w_in_even[0], kind[1])
                elif kind[0] == "in_odd":
                    src = mat(w_in_odd[0], kind[1])
                else:
                    _, l, n = kind
                    src = mat({"out": (w_out_even, w_out_odd)[l][0], "xkv": w_xkv[l], "xq": w_xq[l],
                               "xo": w_xo[l]}[kind[0]], n)
                sp.dma_start(dst8, src).then_inc(s, 16)

            u = 0
            while u < len(units):
                if units[u][0] == "K" and units[u][1] == 0:
                    sp.wait_ge(in_pages, 16)
                if units[u][0] != "moe":
                    slot_free(sp, u)
                    load(u, slot(u).rearrange("p (k n) -> p k n", k=8))
                    u += 1
                    continue
                l = units[u][1]

                def expert_pair(i, first):
                    for j in range(6):
                        if first:
                            slot_free(sp, u + j)
                        else:
                            matrix_done(sp, j % 3, NE * l + j // 3 - 1 + 2 * i)
                        e = 2 * i + j // 3
                        w = (w_exp_gate, w_exp_up, w_exp_down)[j % 3]
                        k = 8 if j % 3 < 2 else 4
                        sp.dma_start(slot(u + j).rearrange("p (k n) -> p k n", k=k),
                                     w[l, bass.ds(e, 1)].rearrange("a (k p) n -> p (a k) n", p=P))\
                          .then_inc(unit_in[(u + j) % SLOTS], 16)

                expert_pair(0, True)
                with sp.Fori(1, NE // 2) as i:
                    expert_pair(i, False)
                u += 3 * NE

        @block.tensor
        def _(pe):
            def mm(out, lhsT, rhs, first, last):
                return pe.matmul(out, lhsT, rhs, start=first, stop=last)

            def project(stage, u, rhs, j0, ready=None, cols=NTOK, order=tuple(range(8))):
                W = slot(u).rearrange("p (k n) -> p k n", k=8)
                arrived(pe, u)
                for j in range(4):
                    bank_free(pe, stage, j0 + j)
                    for k in order:
                        if ready and j == 0:
                            ready(k)
                        last = mm(ACC(stage, j0 + j)[:, 0:cols], W[:, k, P * j:P * j + P], rhs[:, k, :],
                                  k == order[0], k == order[-1])
                    last.then_inc(acc_full, 1)

            def mean_tile(stage, zz, w1, n, ready):
                bank_free(pe, stage, 0)
                for k in range(n):
                    ready(k)
                    last = mm(ACC(stage, 0)[:, 0:NTOK], w1, zz[:, k, :], k == 0, k == n - 1)
                last.then_inc(acc_full, 1)

            pe.wait_ge(in_const, 16)
            pe.wait_ge(in_x, 32)
            for i in range(8):
                bank_free(pe, "x", i)
                for t in range(3):
                    n = P if t < 2 else 32
                    last = pe.transpose(ACC("x", i)[:, P * t:P * t + n], xtok[0:n, t, P * i:P * i + P], ident[0:n, 0:n])
                last.then_inc(acc_full, 1)
            for i in range(8):
                evacuated(pe, "x", i)
            project("q", 0, xT, 0)
            project("k", 1, xT, 0)
            arrived(pe, 2)
            W = slot(2).rearrange("p (k n) -> p k n", k=8)
            for t in range(3):
                n = P if t < 2 else 32
                bank_free(pe, "v", t)
                for k in range(8):
                    last = mm(ACC("v", t)[0:n, :], xT[:, k, P * t:P * t + n], W[:, k, :], k == 0, k == 7)
                last.then_inc(acc_full, 1)
            project("g", 3, xT, 0)
            project("a", 4, xT, 0)
            pe.wait_ge(in_rows, 16 * 11)
            bank_free(pe, "par", 0)
            for i in range(8):
                last = pe.transpose(ACC("par", 0)[:, 14 * i:14 * i + 14], prow[0:14, P * i:P * i + P], ident[0:14, 0:14])
            last.then_inc(acc_full, 1)
            bank_free(pe, "cpar", 0)
            for i in range(4):
                last = pe.transpose(ACC("cpar", 0)[:, 34 * i:34 * i + 34], crow[0:34, P * i:P * i + P], ident[0:34, 0:34])
            last.then_inc(acc_full, 1)
            for i in range(4):
                bank_free(pe, "state", i)
                for t in range(2):
                    last = pe.transpose(ACC("state", i)[:, 120 * t:120 * t + 120], strow[0:120, t, P * i:P * i + P],
                                        ident[0:120, 0:120])
                last.then_inc(acc_full, 1)
            pe.wait_ge(rb_split, 1)
            for i in range(4):
                bank_free(pe, "dbias", i)
                for t in range(16):
                    w = 252 - 4 * (16 * i + t)
                    for c in range(3):
                        last = mm(ACC("dbias", i)[:, 32 * t:32 * t + 32], tab16[:, w:w + P], RB16[:, c, :], c == 0, c == 2)
                last.then_inc(acc_full, 1)
            pe.wait_ge(in_rb, 1)
            for i in range(3):
                n = 512 if i < 2 else 32
                bank_free(pe, "sbias", i)
                mm(ACC("sbias", i)[:, 0:n], SBL, tab[:, T_OHS + 512 * i:T_OHS + 512 * i + n], True, True)\
                    .then_inc(acc_full, 1)

            for t in range(3):
                n = P if t < 2 else 32
                bank_free(pe, "ktok", t)
                for f in range(4):
                    evacuated(pe, "k", f)
                    last = pe.transpose(ACC("ktok", t)[0:n, P * f:P * f + P], kT[:, f, P * t:P * t + n], ident)
                last.then_inc(acc_full, 1)

            def turn_keys(b, half):
                u = UIDX["K", b]
                K = slot(u).rearrange("p (k n) -> p k n", k=8)
                arrived(pe, u)
                for f in range(4):
                    i = 4 * half + f
                    bank_free(pe, f"kt{b}", i)
                    for p in range(4):
                        last = pe.transpose(ACC(f"kt{b}", i)[:, P * p:P * p + P], K[:, 4 * half + p, P * f:P * f + P], ident)
                    last.then_inc(acc_full, 1)

            def key_scores(b, half):
                rows = slice(32 * (b % 4), 32 * (b % 4) + 32)
                if b == 4 and half == 0:
                    pe.wait_ge(scores_read, 1)
                if b == 0:
                    pe.wait_ge(qbd_ready, 1)
                for f in range(4):
                    evacuated(pe, f"kt{b}", 4 * half + f)
                    mm(psS[rows, half, :], QBD[:, b, f, :], KT[:, half, f, :], f == 0, f == 3).then_inc(kt_read, 1)
                if half:
                    for f in range(4):
                        last = mm(psN[rows, 0:32], QBD[:, b, f, :], kT[:, f, S0:NTOK], f == 0, f == 3)
                    if b % 4 == 3:
                        last.then_inc(scores_full, 1)

            def sample_keys(*seqs):
                todo = [(b, half) for b in seqs for half in range(2)]
                turn_keys(*todo[0])
                for i, (b, half) in enumerate(todo):
                    if i + 1 < len(todo):
                        turn_keys(*todo[i + 1])
                    key_scores(b, half)

            def sample_values(g):
                pe.wait_ge(probs, 1 + 1 + g)
                for i in range(3):
                    bank_free(pe, f"spt{g}", i)
                    if i < 2:
                        for c in range(4):
                            k = 4 * i + c
                            last = pe.transpose(ACC(f"spt{g}", i)[:, P * c:P * c + P], SS[:, P * k:P * k + P], ident)
                    else:
                        last = pe.transpose(ACC(f"spt{g}", i)[0:32, 0:P], SS[:, PAST:PAST + 32], ident)
                    last.then_inc(acc_full, 1)
                for i in range(3):
                    evacuated(pe, f"spt{g}", i)
                for b4 in range(4):
                    arrived(pe, UIDX["V", 4 * g + b4])
                for k in range(9):
                    for b4 in range(4):
                        V = slot(UIDX["V", 4 * g + b4]).rearrange("p (k n) -> p k n", k=8)
                        rows, c = psV[32 * b4:32 * b4 + 32, :], 32 * b4
                        if k < 8:
                            last = mm(rows, PTS[:, k, c:c + 32], V[:, k, :], k == 0, False)
                        else:
                            last = mm(rows, PTS[0:32, 8, c:c + 32], vtok[0:32, 2, :], False, True)
                        if k == 7:
                            last.then_inc(values_used, 1)
                last.then_inc(smp_out, 1)

            def turn_rows(g):
                pe.wait_ge(smp_read, g + 1)
                bank_free(pe, f"pvt{g}", 0)
                for f in range(4):
                    last = pe.transpose(ACC(f"pvt{g}", 0)[:, P * f:P * f + P], PV[:, P * f:P * f + P], ident)
                last.then_inc(acc_full, 1)

            sample_keys(0)
            for h in range(8):
                r = slice(64 * (h % 2), 64 * (h % 2) + 64)
                evacuated(pe, "q", h // 2)
                bank_free(pe, "ps", h)
                mm(ACC("ps", h)[:, 0:128], qT[r, h // 2, 0:128], kT[r, h // 2, 0:128], True, True)
                mm(ACC("ps", h)[:, 128:384], qT[r, h // 2, 128:256], kT[r, h // 2, 0:256], True, True)\
                    .then_inc(acc_full, 1)

            evacuated(pe, "a", 3)
            for i in range(2):
                n = 30 if i == 0 else 32
                bank_free(pe, "cnew", i)
                for f in range(4):
                    src = UP[:, f, 256:286] if i == 0 else ucmp[:, f, :]
                    last = pe.transpose(ACC("cnew", i)[0:n, P * f:P * f + P], src, ident)
                last.then_inc(acc_full, 1)
            sample_keys(1, 2)
            pe.wait_ge(probs, 1)
            for s, i in PTPO:
                bank_free(pe, s, i)
                if s == "pt":
                    for c in range(3):
                        last = pe.transpose(ACC(s, i)[:, P * c:P * c + P], SALL[:, i, P * c:P * c + P], ident)
                else:
                    for h in (2 * i, 2 * i + 1):
                        evacuated(pe, "pt", h)
                        if i == 0:
                            evacuated(pe, "v", 0), evacuated(pe, "v", 1), evacuated(pe, "v", 2)
                        o = ACC(s, i)[64 * (h % 2):64 * (h % 2) + 64, :]
                        mm(o[:, 0:256], vtok[:, 0, 64 * h:64 * h + 64], PTP[:, h % 2, 0:256], True, False)
                        last = mm(o[:, 128:256], vtok[:, 1, 64 * h:64 * h + 64], PTP[:, h % 2, 256:384], False, True)
                last.then_inc(acc_full, 1)
            sample_keys(3, 4, 5)
            sample_values(0)
            turn_rows(0)
            sample_keys(6, 7)

            def memory_turned(l):
                pe.wait_ge(mem_in, 16 * (l + 1))
                for i in range(8):
                    bank_free(pe, f"memT{l}", i)
                    for t in range(2):
                        last = pe.transpose(ACC(f"memT{l}", i)[:, P * t:P * t + P], memtok[:, t, P * i:P * i + P], ident)
                    last.then_inc(acc_full, 1)

            def memory_keys(l, tiles=range(4)):
                for i in range(8):
                    evacuated(pe, f"memT{l}", i)
                for i in tiles:
                    u = UIDX["xkv", l, i // 2]
                    W = slot(u).rearrange("p (k n) -> p k n", k=8)
                    arrived(pe, u)
                    bank_free(pe, f"mk{l}", i)
                    for c in range(2):
                        j = 2 * (i % 2) + c
                        for k in range(8):
                            last = mm(ACC(f"mk{l}", i)[:, 256 * c:256 * c + 256], W[:, k, P * j:P * j + P],
                                      memT[:, k, :], k == 0, k == 7)
                    last.then_inc(acc_full, 1)

            def memory_values(l, tiles=range(4)):
                for i in tiles:
                    n, t = i // 2, i % 2
                    u = UIDX["xkv", l, 2 + n]
                    W = slot(u).rearrange("p (k n) -> p k n", k=8)
                    arrived(pe, u)
                    bank_free(pe, f"mv{l}", i)
                    for k in range(8):
                        last = mm(ACC(f"mv{l}", i), memT[:, k, P * t:P * t + P], W[:, k, :], k == 0, k == 7)
                    last.then_inc(acc_full, 1)

            memory_turned(0)
            pe.wait_ge(ones_set, 2)
            memory_keys(0, (0, 1))
            sample_values(1)
            turn_rows(1)
            mean_tile("cmean", mixT[:, 4:8, :], ones_c, 4, lambda k:
                      pe.wait_ge(conv_step, 6 * (CW - 1) + 2 * k + 2) if k < 3 else pe.wait_ge(conv_pool, 2 * CW - 1))
            memory_keys(0, (2,))
            mean_tile("cvar", zT, ones_c, 4, lambda k: pe.wait_ge(sq_c, 1))
            memory_keys(0, (3,))

            def cross(l):
                nth = 3 * l + 1
                mean_tile(f"mean{3 * l}", zT, ones_d[:, :], 8, lambda k: evacuated(pe, f"o{l}", k))
                if l:
                    memory_turned(l)
                else:
                    memory_values(l, (0, 1))
                mean_tile(f"var{3 * l}", mixT, ones_d[:, :], 8, lambda k: pe.wait_ge(squared, 4 * 3 * l + k // 2 + 1))
                if l:
                    memory_keys(l)
                    memory_values(l)
                else:
                    memory_values(l, (2, 3))
                for n in range(2):
                    project(f"xq{l}", UIDX["xq", l, n], xT, 4 * n,
                            lambda k: pe.wait_ge(x_ready, xr(3 * l - 1) + k + 1))
                for h in range(4):
                    evacuated(pe, f"xq{l}", 2 * h), evacuated(pe, f"xq{l}", 2 * h + 1)
                    bank_free(pe, f"xs{l}", h)
                    for t in range(2):
                        for c in range(2):
                            last = mm(ACC(f"xs{l}", h)[:, 256 * t:256 * t + 256], qT[:, 2 * h + c, P * t:P * t + P],
                                      mkT[:, 2 * h + c, :], c == 0, c == 1)
                    last.then_inc(acc_full, 1)

                def keys(b):
                    u = UIDX["memK", l, b // 2]
                    K = slot(u).rearrange("p (c t n) -> p c t n", c=2, n=1024)[:, b % 2]
                    arrived(pe, u)
                    b4 = b % 4
                    if b == 0:
                        pe.wait_ge(qx_ready, l + 1)
                    for i in range(4):
                        bank_free(pe, f"xkt{l}{b}", i)
                        for c in range(4):
                            f, t = 2 * i + c // 2, c % 2
                            last = pe.transpose(ACC(f"xkt{l}{b}", i)[:, P * c:P * c + P], K[:, t, P * f:P * f + P], ident)
                        last.then_inc(acc_full, 1)
                    for f in range(8):
                        evacuated(pe, f"xkt{l}{b}", f // 2)
                        last = mm(psS[32 * b4:32 * b4 + 32, b // 4, 0:256], QX[:, b, f, :], MKT[:, b % 2, f, :], f == 0, f == 7)
                    last.then_inc(xk_read, 1)

                def values(g):
                    bank_free(pe, f"xspt{l}{g}", 0)
                    pe.wait_ge(probs, 3 + (DEPTH + 1) * l + 1 + g + 1)
                    for t in range(2):
                        last = pe.transpose(ACC(f"xspt{l}{g}", 0)[:, P * t:P * t + P], XP[:, g, P * t:P * t + P], ident)
                    last.then_inc(acc_full, 1)
                    evacuated(pe, f"xspt{l}{g}", 0)
                    for b4 in range(4):
                        b = 4 * g + b4
                        u = UIDX["memV", l, b // 2]
                        V = slot(u).rearrange("p (c t n) -> p c t n", c=2, n=1024)[:, b % 2]
                        arrived(pe, u)
                        for half in range(2):
                            for t in range(2):
                                last = mm((psV, psN)[half][32 * b4:32 * b4 + 32, :], XPTS[:, t, 32 * b4:32 * b4 + 32],
                                          V[:, t, 512 * half:512 * half + 512], t == 0, t == 1)
                        last.then_inc(values_used, 1)
                    pe.wait_ge(xpv_ready, 2 * (2 * l + g) + 2)
                    for half in range(2):
                        bank_free(pe, f"xpvt{l}{g}", half)
                        for f in range(4):
                            last = pe.transpose(ACC(f"xpvt{l}{g}", half)[:, P * f:P * f + P], XPV[:, half, P * f:P * f + P], ident)
                        last.then_inc(acc_full, 1)

                for b in range(4):
                    keys(b)
                pe.wait_ge(probs, 3 + (DEPTH + 1) * l + 1)
                for s, i in XPTPO:
                    bank_free(pe, f"{s}{l}", i)
                    if s == "xpt":
                        for c in range(4):
                            kt, t = c // 2, c % 2
                            last = pe.transpose(ACC(f"xpt{l}", i)[:, P * c:P * c + P], PX[:, 2 * i + t, P * kt:P * kt + P], ident)
                    else:
                        evacuated(pe, f"xpt{l}", i)
                        if i == 0:
                            for n in range(4):
                                evacuated(pe, f"mv{l}", n)
                        for c in range(2):
                            for kt in range(2):
                                w = 256 * i + P * c
                                last = mm(ACC(f"xpo{l}", i)[:, 256 * c:256 * c + 256], mvtok[:, kt, w:w + P],
                                          XPT[:, i % 2, 256 * kt:256 * kt + 256], kt == 0, kt == 1)
                    last.then_inc(acc_full, 1)
                for b in (4, 5):
                    keys(b)
                values(0)
                for b in (6, 7):
                    keys(b)
                values(1)
                for i in range(2):
                    evacuated(pe, f"xpvt{l}0", i), evacuated(pe, f"xpvt{l}1", i)
                for i in range(4):
                    evacuated(pe, f"xpo{l}", i)
                for n in range(2):
                    project(f"xo{l}", UIDX["xo", l, n], mixT, 4 * n)
                mean_tile(f"mean{nth}", zT, ones_d[:, :], 8, lambda k: evacuated(pe, f"xo{l}", k))
                for i in range(4):
                    t, n = i // 2, i % 2
                    bank_free(pe, f"mktok{l}", i)
                    for f in range(4):
                        evacuated(pe, f"mk{l}", (4 * n + f) // 2)
                        last = pe.transpose(ACC(f"mktok{l}", i)[:, P * f:P * f + P],
                                            mkT[:, 4 * n + f, P * t:P * t + P], ident)
                    last.then_inc(acc_full, 1)
                mean_tile(f"var{nth}", mixT, ones_d[:, :], 8, lambda k: pe.wait_ge(squared, 4 * nth + k // 2 + 1))

            def expert_chunk(S, n, W, xs, xs_count, free):
                Wg, Wu, Wd, ug, uu, ud = W
                pe.wait_ge(S.xs, xs_count)
                ug()

                def product(w, j, c):
                    for k in range(8):
                        for half in range(2):
                            at = 256 * half + P * j
                            last = mm(psS[CAP * half:CAP * half + CAP, j, P * c:P * c + P], xs[:, k, :], w[:, k, at:at + P],
                                      k == 0, k == 7)
                    return last

                def turn(j):
                    pe.wait_ge(S.h, 2 * n + j + 1)
                    pe.transpose((psN, acc[:, 1, :])[j][:, 0:P], H[:, P * j:P * j + P], ident).then_inc(S.turned, 1)

                def down(k):
                    for half in range(2):
                        last = mm(psV[CAP * half:CAP * half + CAP, :], HT[:, k % 2, CAP * (k // 2):CAP * (k // 2) + CAP],
                                  Wd[:, k, 512 * half:512 * half + 512], k == 0, k == 3)
                    return last

                product(Wg, 0, 0)
                uu()
                product(Wu, 0, 1).then_inc(S.parts, 1)
                product(Wg, 1, 0).then_inc(S.gate, 1)
                turn(0)
                product(Wu, 1, 1).then_inc(S.parts, 1)
                ud()
                pe.wait_ge(S.ht, 2 * n + 1)
                down(0)
                turn(1)
                down(2)
                pe.wait_ge(S.ht, 2 * n + 2)
                down(1)
                down(3).then_inc(S.down, 1)
                for j in range(4):
                    if j % 2 == 0:
                        pe.wait_ge(S.y, 2 * n + j // 2 + 1)
                    if j == 0:
                        free()
                    last = pe.transpose(acc[:, 0, P * j:P * j + P], YS[:, P * j:P * j + P], ident)
                last.then_inc(S.y_turned, 1)

            def experts(l):
                bank_free(pe, f"router{l}", 0)
                for t in range(3):
                    a = min(P * t, NTOK - P)
                    for k in range(8):
                        if t == 0:
                            pe.wait_ge(x_ready, xr(3 * l) + k + 1)
                        last = mm(ACC(f"router{l}", 0)[:, NE * t:NE * t + NE], xT[:, k, a:a + P], wrt[:, k, :], k == 0, k == 7)
                last.then_inc(acc_full, 1)
                for i in range(6):
                    t, half = i // 2, i % 2
                    a = min(P * t, NTOK - P)
                    bank_free(pe, f"xtok{l}", i)
                    for f in range(4):
                        last = pe.transpose(ACC(f"xtok{l}", i)[:, P * f:P * f + P], xT[:, 4 * half + f, a:a + P], ident)
                    last.then_inc(acc_full, 1)
                pe.wait_ge(comb_ready, l + 1)
                bank_free(pe, f"rank{l}", 0)
                R = ACC(f"rank{l}", 0)
                for t in (3, 0, 1, 2):
                    for s_ in range(min(t + 1, 3)):
                        last = mm(R[:, NE * t:NE * t + NE], cst[:, C_BEFORE:C_BEFORE + P] if s_ == t else ones,
                                  MASK[:, s_, :], s_ == 0, s_ == min(t, 2))
                last.then_inc(acc_full, 1)
                for i in range(6):
                    evacuated(pe, f"xtok{l}", i)
                for i in range(2 * FT):
                    half, f = i // FT, i % FT
                    pe.wait_ge(rows_ready, 2 * l + half + 1)
                    bank_free(pe, f"xg{l}", i)
                    for t in range(3):
                        last = mm(ACC(f"xg{l}", i)[:, 0:NTOK], XTOK[:, t, P * f:P * f + P], G[:, t, NTOK * half:NTOK * half + NTOK],
                                  t == 0, t == 2)
                    last.then_inc(acc_full, 1)
                for i in range(2 * FT):
                    evacuated(pe, f"xg{l}", i)
                pe.wait_ge(ranks_ready, l + 1)
                u0 = UIDX["moe", l, 0]
                Y = (NE + 1) * l + 1
                with pe.Fori(0, NE // 2) as i:
                    for e in range(2):
                        n = 2 * i + e
                        u = u0 + 3 * e
                        W = [slot(u + j).rearrange("p (k n) -> p k n", k=(8, 8, 4)[j]) for j in range(3)]
                        here = [lambda j=j: arrived(pe, u + j, 16 * i) for j in range(3)]
                        extra = pe.value_load(MOREI[0:1, bass.ds(n, 1)], min_val=0, max_val=NFURTHER)
                        with pe.If(extra > 0):
                            before = pe.value_load(BEFOREI[0:1, bass.ds(n, 1)], min_val=0, max_val=NROW // CAP)
                            with pe.Fori(0, extra) as c:
                                k = before + c
                                expert_chunk(more[l], k, W + here, XSM, k + n + 1, lambda: pe.wait_ge(first.yt, Y + n))
                                pe.wait_ge(more[l].yt, k + 1)
                        expert_chunk(first, NE * l + n, W + here, XS, Y + n, lambda: pe.wait_ge(first.yt, Y + n))
                pe.wait_ge(weights_ready, l + 1)
                pe.wait_ge(first.yt, (NE + 1) * (l + 1))
                for i in range(NST):
                    r = min(P, NROW - P * i)
                    bank_free(pe, f"gt{l}", i)
                    for t in (2, 0, 1):
                        a = min(P * t, NTOK - P)
                        last = pe.transpose(ACC(f"gt{l}", i)[0:r, a:a + P], GW[:, t, P * i:P * i + r], ident)
                    last.then_inc(acc_full, 1)
                for i in range(2 * NST):
                    half, s_ = i // NST, i % NST
                    r = min(P, NROW - P * s_)
                    bank_free(pe, f"yt{l}", i)
                    for f in range(4):
                        last = pe.transpose(ACC(f"yt{l}", i)[0:r, P * f:P * f + P], YT[:, 4 * half + f, P * s_:P * s_ + r], ident)
                    last.then_inc(acc_full, 1)
                for i in range(NST):
                    evacuated(pe, f"gt{l}", i)
                for f in range(8):
                    for s_ in range(NST):
                        if f % 4 == 0:
                            evacuated(pe, f"yt{l}", NST * (f // 4) + s_)
                        if s_ == 0:
                            bank_free(pe, f"ms{l}", f)
                        r = min(P, NROW - P * s_)
                        last = mm(ACC(f"ms{l}", f)[:, 0:NTOK], YTOK[0:r, s_, P * f:P * f + P], GT[0:r, s_, :], s_ == 0, s_ == NST - 1)
                    last.then_inc(acc_full, 1)
                nth = 3 * l + 2
                mean_tile(f"mean{nth}", zT, ones_d[:, :], 8, lambda k: evacuated(pe, f"ms{l}", k))
                mean_tile(f"var{nth}", mixT, ones_d[:, :], 8, lambda k: pe.wait_ge(squared, 4 * nth + k // 2 + 1))

            for l in range(DEPTH):
                if l:
                    for n in range(2):
                        project("u", UIDX["in_odd", n], xT, 4 * n, lambda k: pe.wait_ge(x_ready, xr(1) + k + 1))
                    for n in range(2):
                        project("vv", UIDX["in_odd", 2 + n], xT, 4 * n)
                    mean_tile("vmean", vT, ones_d[:, :], 8, lambda k: evacuated(pe, "vv", k))
                    mean_tile("vvar", mixT, ones_d[:, :], 8, lambda k: pe.wait_ge(sq_v, k // 2 + 1))
                    pe.wait_ge(w_masked, 1)
                    for i in range(2):
                        bank_free(pe, "wm", i)
                        for g in range(4):
                            last = pe.transpose(ACC("wm", i)[:, P * g:P * g + P], WLD[:, 4 * i + g, :], ident)
                        last.then_inc(acc_full, 1)
                    for i in range(6):
                        t, half = i // 2, i % 2
                        n = P if t < 2 else 32
                        bank_free(pe, "vtok", i)
                        for f in range(4):
                            if i < 2:
                                pe.wait_ge(vn_ready, 4 * half + f + 1)
                            last = pe.transpose(ACC("vtok", i)[0:n, P * f:P * f + P],
                                                vT[:, 4 * half + f, P * t:P * t + n], ident)
                        last.then_inc(acc_full, 1)
                    for i in range(6):
                        evacuated(pe, "vtok", i)
                    evacuated(pe, "wm", 1)
                    pe.wait_ge(w_masked, 2)
                    for g in range(8):
                        bank_free(pe, "mix", g)
                        for t in range(2):
                            mm(ACC("mix", g)[:, P * t:P * t + P], gvtok[:, t, P * g:P * g + P], WMT[:, g, :], True, True)
                        mm(ACC("mix", g)[:, S0:NTOK], gvtok[0:32, 2, P * g:P * g + P], WBD[:, g, :], True, True)\
                            .then_inc(acc_full, 1)
                if l:
                    pe.wait_ge(mixed, 8)
                else:
                    for i in range(4):
                        evacuated(pe, "po", i)
                if l:
                    for n in range(2):
                        project(f"o{l}", UIDX["out", l, n], mixT, 4 * n)
                else:
                    for n in range(2):
                        project(f"o{l}", UIDX["out", l, n], mixT, 4 * n,
                                lambda k: pe.wait_ge(cv_ready, k - 3) if k >= 4 else evacuated(pe, "pvt1", 0),
                                order=(4, 5, 6, 7, 0, 1, 2, 3))
                cross(l)
                experts(l)
            for i in range(6):
                half, t = i // 3, i % 3
                pe.wait_ge(x_ready, xr(4) + 4 * half + 4)
                n = P if t < 2 else 32
                bank_free(pe, "y", i)
                for f in range(4):
                    last = pe.transpose(ACC("y", i)[0:n, P * f:P * f + P], xT[:, 4 * half + f, P * t:P * t + n], ident)
                last.then_inc(acc_full, 1)

        def evac(eng, who, stage, n, body):
            for i in owned(who, stage, n):
                full(eng, stage, i)
                body(i, ACC(stage, i)).then_inc(emptied[who], 1)

        def copier(eng, who):
            if who == "v":
                return eng.tensor_copy
            return lambda out, in_: eng.activation(out, in_, ACT.Copy)

        def scaler(eng, who):
            if who == "v":
                return lambda out, in_, c: eng.tensor_scalar(out, in_, c, None, ALU.mult)
            return lambda out, in_, c: eng.activation(out, in_, ACT.Copy, scale=c)

        def common(eng, who):
            copy, scale = copier(eng, who), scaler(eng, who)

            def rows(i):
                return P if i < 2 else 32

            def xkt(l, b):
                def body(i, a):
                    if b >= 2:
                        eng.wait_ge(xk_read, 8 * l + b - 1)
                    elif l and b < 2:
                        eng.wait_ge(xk_read, 8 * l)
                    return copy(MKT[:, b % 2, 2 * i:2 * i + 2, :], a.rearrange("p (f m) -> p f m", f=2))
                evac(eng, who, f"xkt{l}{b}", 4, body)

            def kt(b, between=lambda i: None):
                def body(i, a):
                    between(i)
                    if b:
                        eng.wait_ge(kt_read, 8 * (b - 1) + i + 1)
                    return copy(KT[:, i // 4, i % 4, :], a)
                evac(eng, who, f"kt{b}", 8, body)

            def cnew_left(l):
                if l == 0:
                    eng.wait_ge(out_rest, 16 * 5)

            return dict(
                x=lambda: evac(eng, who, "x", 8, lambda i, a: copy(xT[:, i, :], a[:, 0:NTOK])),
                state=lambda: evac(eng, who, "state", 4, lambda i, a: copy(
                    US[:, i, :, 0:30], a[:, 0:240].rearrange("p (b t) -> p b t", b=8))),
                q=lambda: evac(eng, who, "q", 4, lambda i, a: scale(qT[:, i, :], a[:, 0:NTOK], HD ** -0.5)),
                k=lambda: evac(eng, who, "k", 4, lambda i, a: copy(kT[:, i, :], a[:, 0:NTOK])),
                v=lambda: evac(eng, who, "v", 3, lambda i, a: copy(vtok[0:rows(i), i, :], a[0:rows(i), :])),
                ktok=lambda: evac(eng, who, "ktok", 3, lambda i, a: copy(ktok[0:rows(i), i, :], a[0:rows(i), :])),
                cnew=lambda: evacuated(eng, "ps", 7) or evac(eng, who, "cnew", 2, lambda i, a: copy(
                    cnew[0:30 + 2 * i, i, :], a[0:30 + 2 * i, :])),
                kt=kt,
                spt=lambda g: evac(eng, who, f"spt{g}", 3, lambda i, a: (
                    copy(PTS[:, 4 * i:4 * i + 4, :], a.rearrange("p (k m) -> p k m", k=4)) if i < 2 else
                    copy(PTS[0:32, 8, :], a[0:32, 0:P]))),
                mk=lambda l: evac(eng, who, f"mk{l}", 4, lambda i, a: copy(
                    mkT[:, 2 * i:2 * i + 2, :], a.rearrange("p (f m) -> p f m", f=2))),
                mv=lambda l: evac(eng, who, f"mv{l}", 4, lambda i, a: copy(
                    mvtok[:, i % 2, 512 * (i // 2):512 * (i // 2) + 512], a)),
                mktok=lambda l: cnew_left(l) or evac(eng, who, f"mktok{l}", 4, lambda i, a: copy(
                    mktok[:, i // 2, 512 * (i % 2):512 * (i % 2) + 512], a)),
                xq=lambda l: evac(eng, who, f"xq{l}", 8, lambda i, a: scale(qT[:, i, :], a[:, 0:NTOK], HDX ** -0.5)),
                xkt=xkt,
                xtok=lambda l: evac(eng, who, f"xtok{l}", 6, lambda i, a: copy(
                    XTOK[:, i // 2, 512 * (i % 2):512 * (i % 2) + 512], a)),
                xg=lambda l: evac(eng, who, f"xg{l}", 2 * FT, lambda i, a: copy(
                    XE[:, i % FT, NTOK * (i // FT):NTOK * (i // FT) + NTOK], a[:, 0:NTOK])),
                gt=lambda l: evac(eng, who, f"gt{l}", NST, lambda i, a: copy(
                    GT[0:min(P, NROW - P * i), i, :], a[0:min(P, NROW - P * i), 0:NTOK])),
                yt=lambda l: evac(eng, who, f"yt{l}", 2 * NST, lambda i, a: copy(
                    YTOK[0:min(P, NROW - P * (i % NST)), i % NST, 512 * (i // NST):512 * (i // NST) + 512],
                    a[0:min(P, NROW - P * (i % NST)), :])),
                vtok=lambda: evac(eng, who, "vtok", 6, lambda i, a: copy(
                    gvtok[0:rows(i // 2), i // 2, 512 * (i % 2):512 * (i % 2) + 512], a[0:rows(i // 2), :])),
                y=lambda: evac(eng, who, "y", 6, lambda i, a: copy(
                    ytok[0:rows(i % 3), i % 3, 512 * (i // 3):512 * (i // 3) + 512], a[0:rows(i % 3), :])),
            )

        def sample_rows(eng, who, g):
            copy = copier(eng, who)
            full(eng, f"pvt{g}", 0)
            a = ACC(f"pvt{g}", 0).rearrange("p (f b c) -> p f b c", f=4, b=4)
            for f in range(4):
                for r in range(2):
                    rr = slice(64 * r, 64 * r + 64)
                    h = 2 * f + r
                    ins = copy(mixT[rr, f, S0 + 16 * g:S0 + 16 * g + 16].rearrange("p (b q) -> p b q", b=4),
                               a[rr, f, :, 4 * h:4 * h + 4])
            ins.then_inc(emptied[who], 1)

        def ptpo(eng, who, table, l=None):
            copy = copier(eng, who)
            for s, i in table:
                stage = s if l is None else f"{s}{l}"
                if OWNER[TIDX[stage, i]] != who:
                    continue
                full(eng, stage, i)
                a = ACC(stage, i)
                if s == "pt":
                    if i >= 2:
                        full(eng, "po", i // 2 - 1)
                    ins = copy(PTP[:, i % 2, :], a[:, 0:384])
                elif s == "po":
                    ins = copy(mixT[:, i, 0:SEQ], a[:, 0:SEQ])
                elif s == "xpt":
                    if i >= 2:
                        full(eng, f"xpo{l}", i - 2)
                    ins = copy(XPT[:, i % 2, :], a)
                else:
                    ins = copy(mixT[:, 2 * i:2 * i + 2, 0:SEQ], a.rearrange("p (f q) -> p f q", f=2))
                ins.then_inc(emptied[who], 1)

        @block.vector
        def _(dve):
            steps = [0]

            def link(ins):
                steps[0] += 1
                ins.then_inc(dve_step, 1)
                dve.wait_ge(dve_step, steps[0])

            taps = [(w, f, part) for w in range(CW) for f in range(3) for part in range(2)]

            def conv_taps(n):
                for _ in range(min(n, len(taps) - done[0])):
                    w, f, part = taps[done[0]]
                    y = mixT[:, 4 + f, 0:SEQ] if part == 0 else mixT[:, 4 + f, S0:NTOK].rearrange("p (b s) -> p b s", b=8)
                    u = UP[:, f, w:w + SEQ] if part == 0 else US[:, f, :, w:w + DS]
                    tap = cparT[:, f, w:w + 1]
                    if w:
                        dve.wait_ge(conv_step, done[0] - 5)
                        ins = dve.scalar_tensor_tensor(out=y, in0=u, scalar=tap, in1=y, op0=ALU.mult, op1=ALU.add)
                    else:
                        ins = dve.tensor_scalar(y, u, tap, cparT[:, f, 31:32], ALU.mult, ALU.add)
                    ins.then_inc(conv_step, 1)
                    done[0] += 1

            done = [0]
            cm = common(dve, "v")
            dve.memset(ones_d[:, :], 1.0 / D).then_inc(ones_set, 1)
            dve.memset(ones_c, 1.0 / CC).then_inc(ones_set, 1)
            dve.memset(RB4, 0.0).then_inc(rb_zero, 1)
            cm["x"]()
            cm["q"]()
            cm["k"]()
            cm["v"]()
            link(dve.memset(QBD, 0.0))
            evacuated(dve, "q", 2), evacuated(dve, "q", 3)
            for f in range(4):
                for r in range(2):
                    h = 2 * f + r
                    last = dve.tensor_copy(QBD[64 * r:64 * r + 64, :, f, 4 * h:4 * h + 4],
                                           qT[64 * r:64 * r + 64, f, S0:NTOK].rearrange("p (b q) -> p b q", q=4))
            last.then_inc(qbd_ready, 1)
            dve.wait_ge(in_table, 16)
            dve.wait_ge(rb_in, 64)
            dve.tensor_copy(tab16, tab[:, T_OH4:T_OH4 + 380])
            link(dve.tensor_copy(RB16[:, 0, :], RB4))
            link(dve.tensor_tensor(rb_rest, RB4, RB16[:, 0, :], ALU.subtract))
            link(dve.tensor_copy(RB16[:, 1, :], rb_rest))
            link(dve.tensor_tensor(rb_rest, rb_rest, RB16[:, 1, :], ALU.subtract))
            dve.tensor_copy(RB16[:, 2, :], rb_rest).then_inc(rb_split, 1)
            dve.memset(UP[:, :, 0:30], 0.0)
            for i in range(4):
                evacuated(dve, "g", i)
                full(dve, "a", i)
                a = ACC("a", i)
                dve.tensor_tensor(UP[:, i, 30:286], a[:, 0:SEQ], zT[:, i, 0:SEQ], ALU.mult)
                dve.tensor_tensor(ucmp[:, i, :], a[:, S0:NTOK], zT[:, i, S0:NTOK], ALU.mult)
                dve.tensor_tensor(US[:, i, :, 30:34], a[:, S0:NTOK].rearrange("p (b s) -> p b s", b=8),
                                  zT[:, i, S0:NTOK].rearrange("p (b s) -> p b s", b=8), ALU.mult)\
                    .then_inc(emptied["v"], 1)
            full(dve, "par", 0)
            dve.tensor_copy(parT[:, :, :], ACC("par", 0)[:, 0:112].rearrange("p (f c) -> p f c", f=8)).then_inc(emptied["v"], 1)
            full(dve, "cpar", 0)
            dve.tensor_copy(cparT[:, :, :], ACC("cpar", 0)[:, 0:136].rearrange("p (f c) -> p f c", f=4)).then_inc(emptied["v"], 1)
            src = RB4.rearrange("p (q h) -> p h q", q=4)
            for b in range(4):
                last = dve.tensor_copy(SBL[:, 32 * b:32 * b + 32].rearrange("p (h q) -> p h q", q=4), src)
            last.then_inc(in_rb, 1)
            cm["state"]()
            for i in range(4):
                full(dve, "dbias", i)
                a = ACC("dbias", i).rearrange("p (m h) -> p h m", h=8)
                ins = dve.tensor_copy(BIAS[:, :, 128 + 64 * i:192 + 64 * i], a)
                if i >= 2:
                    ins = dve.tensor_copy(BIAS[:, :, 64 * i - 128:64 * i - 64], a)
                ins.then_inc(emptied["v"], 1)
            full(dve, "sbias", 2)
            for g in range(2):
                last = dve.tensor_tensor(OBIAS[:, g, :], ACC("sbias", 2)[:, 0:32],
                                         cst[:, C_OWN + 32 * g:C_OWN + 32 * g + 32], ALU.add)
            last.then_inc(emptied["v"], 1)
            cm["ktok"]()
            for i in range(4):
                evacuated(dve, "state", i)
            dve.wait_ge(bias_masked, 2)
            for h in range(8):
                full(dve, "ps", h)
                last = dve.tensor_tensor(SALL[:, h, :], ACC("ps", h)[:, 0:384], BIAS[:, h, :], ALU.add)
                last.then_inc(emptied["v"], 1)
            evacuated(dve, "ps", 7)
            dve.tensor_reduce(st[:, 0:8], SALL[:, :, 0:128], X, ALU.max)
            link(dve.tensor_reduce(st[:, 8:16], SALL[:, :, 128:384], X, ALU.max))
            dve.tensor_scalar(st[:, 16:32], st[:, 0:16], -1.0, None, ALU.mult).then_inc(negmax, 1)
            cm["cnew"]()
            conv_taps(len(taps) // 4)
            dve.wait_ge(exp_done, 16)
            link(dve.reciprocal(st[:, 48:64], st[:, 32:48]))
            dve.tensor_tensor(SALL[:, :, 0:128], SALL[:, :, 0:128], st[:, 48:56].unsqueeze(2).to_broadcast([P, 8, 128]), ALU.mult)
            dve.tensor_tensor(SALL[:, :, 128:384], SALL[:, :, 128:384],
                              st[:, 56:64].unsqueeze(2).to_broadcast([P, 8, 256]), ALU.mult).then_inc(probs, 1)
            ptpo(dve, "v", PTPO)

            def sample_softmax(g):
                dve.wait_ge(scores_full, g + 1)
                gs, v, bm, pen = st[:, 64:68], st[:, 68:72], st[:, 72:77], st[:, 80:85]
                mn, mx, sm, rc, nb = st[:, 77:78], st[:, 78:79], st[:, 79:80], st[:, 85:86], st[:, 88:93]
                dve.tensor_reduce(gs, psS[:, :, :].rearrange("p a (c k) -> p (a c) k", k=MOBA), X, ALU.add)
                dve.tensor_tensor(SS[:, 0:PAST], psS[:, :, :].rearrange("p a k -> p (a k)"), SBIAS, ALU.add)
                dve.tensor_tensor(SS[:, PAST:PAST + 32], psN[:, 0:32], OBIAS[:, g, :], ALU.add).then_inc(scores_read, 1)
                dve.wait_ge(scores_read, g + 1)
                dve.tensor_reduce(bm[:, 0:4], SS[:, 0:PAST].rearrange("p (c k) -> p c k", k=MOBA), X, ALU.max)
                dve.tensor_reduce(bm[:, 4:5], SS[:, PAST:PAST + 32], X, ALU.max)
                link(dve.tensor_reduce(mn, gs, X, ALU.min))
                link(dve.scalar_tensor_tensor(out=v, in0=gs, scalar=mn, in1=cst[:, C_IDX:C_IDX + 4],
                                              op0=ALU.is_equal, op1=ALU.mult))
                link(dve.tensor_reduce(mx, v, X, ALU.max))
                dve.memset(pen[:, 4:5], 0.0)
                link(dve.tensor_scalar(pen[:, 0:4], v, mx, NEG, ALU.is_equal, ALU.mult))
                link(dve.tensor_tensor(bm[:, 0:4], bm[:, 0:4], pen[:, 0:4], ALU.add))
                link(dve.tensor_reduce(sm, bm, X, ALU.max))
                dve.tensor_scalar(nb, pen, sm, None, ALU.subtract).then_inc(negmax, 1)
                dve.wait_ge(exp_done, 16 + 5 * (g + 1))
                link(dve.tensor_reduce(rc, st[:, 96:101], X, ALU.add))
                link(dve.reciprocal(rc, rc))
                dve.tensor_scalar(SS, SS, rc, None, ALU.mult).then_inc(probs, 1)

            conv_taps(len(taps) // 16)
            sample_softmax(0)
            cm["spt"](0)
            conv_taps(len(taps) // 2)
            sample_softmax(1)
            cm["spt"](1)
            conv_taps(len(taps))

            def center(stage, zz, n, done, step):
                full(dve, stage, 0)
                m = ACC(stage, 0)[:, 0:NTOK].unsqueeze(1).to_broadcast([P, step, NTOK])
                for c in range(0, n, step):
                    ins = dve.tensor_tensor(zz[:, c:c + step, :], zz[:, c:c + step, :], m, ALU.subtract)
                    ins.then_inc(done if c + step < n else emptied["v"], 1)

            def rstd(stage, signal_std, count):
                full(dve, stage, 0)
                dve.tensor_scalar(rs[:, :], ACC(stage, 0)[:, 0:NTOK], EPS, None, ALU.add)\
                    .then_inc(emptied["v"], 1)
                dve.wait_ge(signal_std, count)
                link(dve.reciprocal(rs[:, :], std[:, :]))

            dve.wait_ge(conv_pool, 2 * CW - 1)
            center("cmean", mixT[:, 4:8, :], 4, None, 4)
            rstd("cvar", std_c, 1)
            for f in range(4):
                dve.tensor_tensor(mixT[:, 4 + f, :], mixT[:, 4 + f, :], rs[:, :], ALU.mult).then_inc(scl_c, 1)

            def residual(stage):
                for i in range(8):
                    full(dve, stage, i)
                    dve.scalar_tensor_tensor(out=zT[:, i, :], in0=xT[:, i, :], scalar=ALPHA, in1=ACC(stage, i)[:, 0:NTOK],
                                             op0=ALU.mult, op1=ALU.add).then_inc(emptied["v"], 1)

            def normalise(nth):
                rstd(f"var{nth}", std_ready, nth + 1)
                for f in range(8):
                    dve.scalar_tensor_tensor(out=zT[:, f, :], in0=zT[:, f, :], scalar=parT[:, f, nth:nth + 1],
                                             in1=rs[:, :], op0=ALU.mult, op1=ALU.mult).then_inc(scaled, 1)

            for l in range(DEPTH):
                if l:
                    center("vmean", vT, 8, cen_v, 2)
                    rstd("vvar", std_v, 1)
                    for f in range(8):
                        dve.scalar_tensor_tensor(out=vT[:, f, :], in0=vT[:, f, :], scalar=parT[:, f, 12:13],
                                                 in1=rs[:, :], op0=ALU.mult, op1=ALU.mult).then_inc(scl_v, 1)
                    evac(dve, "v", "wm", 2, lambda i, a: dve.tensor_copy(
                        WMT[:, 4 * i:4 * i + 4, :], a.rearrange("p (g t) -> p g t", g=4)))
                    cm["vtok"]()
                    for i in range(8):
                        evacuated(dve, "u", i)
                    for g in range(8):
                        full(dve, "mix", g)
                        a = ACC("mix", g)
                        dve.tensor_tensor(mixT[:, g, 0:SEQ].rearrange("p (n t) -> p n t", n=2),
                                          a[:, 0:SEQ].rearrange("p (n t) -> p n t", n=2),
                                          BSG[:, g, :].unsqueeze(1).to_broadcast([P, 2, P]), ALU.add)
                        dve.tensor_tensor(mixT[:, g, S0:NTOK].rearrange("p (b s) -> p b s", b=8),
                                          a[:, S0:NTOK].rearrange("p (b s) -> p b s", b=8),
                                          BSG[:, g, 0:DS].unsqueeze(1).to_broadcast([P, DB, DS]), ALU.add)\
                            .then_inc(emptied["v"], 1)
                        evacuated(dve, "mix", g)
                        dve.tensor_tensor(mixT[:, g, :], mixT[:, g, :], qT[:, g, :], ALU.mult).then_inc(mixed, 1)
                residual(f"o{l}")
                evacuated(dve, f"o{l}", 7)
                center(f"mean{3 * l}", zT, 8, centered, 2)
                normalise(3 * l)
                if l:
                    cm["mk"](l)
                    cm["mv"](l)
                link(dve.memset(QX, 0.0))
                cm["xq"](l)
                for i in range(8):
                    evacuated(dve, f"xq{l}", i)
                for f in range(8):
                    h = f // 2
                    last = dve.tensor_copy(QX[:, :, f, 4 * h:4 * h + 4],
                                           qT[:, f, S0:NTOK].rearrange("p (b q) -> p b q", q=4))
                last.then_inc(qx_ready, 1)
                for h in range(4):
                    full(dve, f"xs{l}", h)
                    link(dve.tensor_reduce(st[:, 2 * h:2 * h + 2], ACC(f"xs{l}", h).rearrange("p (t k) -> p t k", t=2),
                                           X, ALU.max))
                    dve.tensor_scalar(st[:, 16 + 2 * h:18 + 2 * h], st[:, 2 * h:2 * h + 2], -1.0, None, ALU.mult)\
                        .then_inc(negmax, 1)
                for b in range(4):
                    cm["xkt"](l, b)
                ex = 26 + 2 * l
                evacuated(dve, f"xs{l}", 3)
                link(dve.reciprocal(st[:, 48:56], st[:, 32:40]))
                dve.tensor_tensor(PX, PX, st[:, 48:56].unsqueeze(2).to_broadcast([P, 8, 256]), ALU.mult).then_inc(probs, 1)

                def mem_softmax(g):
                    dve.wait_ge(xk_read, 8 * l + 4 * g + 4)
                    link(dve.tensor_reduce(st[:, 64:65], psS[:, g, 0:256], X, ALU.max))
                    dve.tensor_scalar(st[:, 65 + g:66 + g], st[:, 64:65], -1.0, None, ALU.mult).then_inc(negmax, 1)
                    dve.wait_ge(exp_done, ex + g + 1)
                    link(dve.reciprocal(st[:, 70:71], st[:, 68 + g:69 + g]))
                    dve.tensor_scalar(XP[:, g, :], XP[:, g, :], st[:, 70:71], None, ALU.mult).then_inc(probs, 1)
                    evac(dve, "v", f"xspt{l}{g}", 1, lambda i, a: dve.tensor_copy(
                        XPTS, a[:, 0:256].rearrange("p (t m) -> p t m", t=2)))

                def mem_rows(g):
                    dve.wait_ge(values_used, DB * (1 + l) + 4 * g + 4)
                    dve.tensor_copy(XPV[:, 1, :], psN[:, :]).then_inc(xpv_ready, 1)
                    for half in range(2):
                        full(dve, f"xpvt{l}{g}", half)
                        a = ACC(f"xpvt{l}{g}", half).rearrange("p (f b c) -> p f b c", f=4, b=4)
                        for f in range(4):
                            h = 2 * half + f // 2
                            ins = dve.tensor_copy(mixT[:, 4 * half + f, S0 + 16 * g:S0 + 16 * g + 16].rearrange("p (b q) -> p b q", b=4),
                                                  a[:, f, :, 4 * h:4 * h + 4])
                        ins.then_inc(emptied["v"], 1)

                ptpo(dve, "v", XPTPO, l)
                for b in (4, 5):
                    cm["xkt"](l, b)
                mem_softmax(0)
                mem_rows(0)
                for b in (6, 7):
                    cm["xkt"](l, b)
                mem_softmax(1)
                mem_rows(1)
                residual(f"xo{l}")
                evacuated(dve, f"xo{l}", 7)
                center(f"mean{3 * l + 1}", zT, 8, centered, 2)
                cm["mktok"](l)
                normalise(3 * l + 1)

                dve.memset(ones, 1.0)
                evacuated(dve, f"router{l}", 0)
                dve.wait_ge(in_misc, 16)
                sc, sel, cmp_ = RT[:, 48:96], RT[:, 96:144], RT[:, 144:336]
                eq = RT[:, 336:528]
                top, gsc, v, best = RT[:, 528:576], RT[:, 576:588], RT[:, 588:600], RT[:, 600:612]
                mx, tmp = RT[:, 612:615], RT[:, 616:664]
                link(dve.tensor_tensor(sel.rearrange("p (t e) -> p t e", t=3), sc.rearrange("p (t e) -> p t e", t=3),
                                       rbias[:, :].unsqueeze(1).to_broadcast([P, 3, NE]), ALU.add))
                s3 = sel.rearrange("p (g e) -> p g e", e=4)
                other = s3.unsqueeze(2).to_broadcast([P, 12, 4, 4])
                self_ = s3.unsqueeze(3).to_broadcast([P, 12, 4, 4])
                c4 = cmp_.rearrange("p (g e o) -> p g e o", e=4, o=4)
                e4 = eq.rearrange("p (g e o) -> p g e o", e=4, o=4)
                dve.tensor_tensor(c4, other, self_, ALU.is_gt)
                link(dve.tensor_tensor(e4, other, self_, ALU.is_equal))
                link(dve.tensor_tensor(eq.rearrange("p (g c) -> p g c", c=16), eq.rearrange("p (g c) -> p g c", c=16),
                                       cst[:, C_TRI:C_TRI + 16].unsqueeze(1).to_broadcast([P, 12, 16]), ALU.mult))
                link(dve.tensor_tensor(cmp_, cmp_, eq, ALU.add))
                link(dve.tensor_reduce(top, cmp_.rearrange("p (g o) -> p g o", o=4), X, ALU.add))
                link(dve.tensor_scalar(top, top, 1.5, None, ALU.is_lt))
                link(dve.tensor_tensor(tmp, sel, top, ALU.mult))
                link(dve.tensor_reduce(gsc, tmp.rearrange("p (g e) -> p g e", e=4), X, ALU.add))
                g3 = gsc.rearrange("p (t g) -> p t g", g=4)
                v3 = v.rearrange("p (t g) -> p t g", g=4)
                b3 = best.rearrange("p (t g) -> p t g", g=4)
                link(dve.tensor_reduce(mx, g3, X, ALU.max))
                link(dve.tensor_tensor(v3, g3, mx.unsqueeze(2).to_broadcast([P, 3, 4]), ALU.is_equal))
                link(dve.tensor_tensor(v3, v3, cst[:, C_FIRST:C_FIRST + 4].unsqueeze(1).to_broadcast([P, 3, 4]), ALU.mult))
                link(dve.tensor_reduce(mx, v3, X, ALU.max))
                link(dve.tensor_tensor(b3, v3, mx.unsqueeze(2).to_broadcast([P, 3, 4]), ALU.is_equal))
                link(dve.tensor_tensor(top.rearrange("p (g e) -> p g e", e=4), top.rearrange("p (g e) -> p g e", e=4),
                                       best.unsqueeze(2).to_broadcast([P, 12, 4]), ALU.mult))
                once = cst[:, C_ONCE:C_ONCE + 48].rearrange("p (t e) -> p t e", t=3)
                dve.tensor_tensor(MASK, top.rearrange("p (t e) -> p t e", t=3), once, ALU.mult).then_inc(comb_ready, 1)
                dve.wait_ge(out_mem, 32 * (l + 1))
                dve.memset(XE[:, :, NROW:], 0.0)
                full(dve, f"rank{l}", 0)
                R = ACC(f"rank{l}", 0)
                dve.wait_ge(comb_ready, l + 1)
                link(dve.tensor_copy(CNT, R[:, 48:64]))
                link(dve.tensor_tensor_scan(START, ones[:, 0:NE], CNT, 0.0, ALU.mult, ALU.add))
                link(dve.tensor_tensor(START, START, CNT, ALU.subtract))
                dve.tensor_tensor(POS, R[:, 0:48].rearrange("p (t e) -> p t e", t=3),
                                  START.unsqueeze(1).to_broadcast([P, 3, NE]), ALU.add).then_inc(emptied["v"], 1)
                evacuated(dve, f"rank{l}", 0)
                link(dve.scalar_tensor_tensor(out=POS, in0=POS, scalar=1.0, in1=MASK, op0=ALU.add, op1=ALU.mult))
                dve.tensor_reduce(ROW[:, 0, :], POS, X, ALU.max)
                link(dve.tensor_reduce(ROW[:, 1, :], POS, X, ALU.add))
                link(dve.tensor_tensor(ROW[:, 1, :], ROW[:, 1, :], ROW[:, 0, :], ALU.subtract))
                link(dve.tensor_scalar(ROWB, ROW, -float(NTOK), None, ALU.add))
                seq = cst[:, C_SLOT:C_SLOT + NTOK]
                for half, at in ((0, ROW), (1, ROWB)):
                    for t in range(3):
                        last = dve.tensor_scalar(GA[:, t, :], seq, at[:, 0, t:t + 1], None, ALU.is_equal)
                    link(last)
                    for t in range(3):
                        last = dve.scalar_tensor_tensor(out=G[:, t, NTOK * half:NTOK * half + NTOK], in0=seq,
                                                        scalar=at[:, 1, t:t + 1], in1=GA[:, t, :],
                                                        op0=ALU.is_equal, op1=ALU.add)
                    last.then_inc(rows_ready, 1)
                    dve.wait_ge(rows_ready, 2 * l + half + 1)
                link(dve.tensor_scalar(MORE, CNT, CAP + 0.5, None, ALU.is_gt))
                for c in range(2, NFURTHER + 1):
                    link(dve.scalar_tensor_tensor(out=MORE, in0=CNT, scalar=c * CAP + 0.5, in1=MORE, op0=ALU.is_gt, op1=ALU.add))
                link(dve.tensor_tensor_scan(SCAN, ones[:, 0:NE], MORE, 0.0, ALU.mult, ALU.add))
                link(dve.tensor_tensor(SCAN, SCAN, MORE, ALU.subtract))
                dve.memset(START17[:, NE:], 0.0)
                dve.tensor_copy(STARTI[:, 0:NE], START)
                dve.tensor_copy(MOREI, MORE)
                dve.tensor_copy(BEFOREI, SCAN).then_inc(ranks_ready, 1)
                cm["xg"](l)
                link(dve.tensor_tensor(tmp, sc, top, ALU.mult))
                link(dve.tensor_reduce(mx, tmp.rearrange("p (t e) -> p t e", t=3), X, ALU.add))
                link(dve.reciprocal(mx, mx))
                link(dve.tensor_tensor(COMB, tmp.rearrange("p (t e) -> p t e", t=3),
                                       mx.unsqueeze(2).to_broadcast([P, 3, NE]), ALU.mult))
                for pick in range(2):
                    link(dve.tensor_tensor(PICK, POS, ROW[:, pick, :].unsqueeze(2).to_broadcast([P, 3, NE]), ALU.is_equal))
                    link(dve.tensor_tensor(PICK, PICK, COMB, ALU.mult))
                    link(dve.tensor_reduce(WT[:, pick, :], PICK, X, ALU.add))
                for half, at in ((0, ROW), (1, ROWB)):
                    for t in range(3):
                        dve.tensor_scalar(GA[:, t, :], seq, at[:, 1, t:t + 1], WT[:, 1, t:t + 1], ALU.is_equal, ALU.mult)
                        last = dve.tensor_scalar(GW[:, t, NTOK * half:NTOK * half + NTOK], seq, at[:, 0, t:t + 1],
                                                 WT[:, 0, t:t + 1], ALU.is_equal, ALU.mult)
                    link(last)
                    w = slice(NTOK * half, NTOK * half + NTOK)
                    last = dve.tensor_tensor(GW[:, :, w], GW[:, :, w], GA, ALU.add)
                    if half:
                        last.then_inc(weights_ready, 1)
                    else:
                        link(last)
                dve.wait_ge(weights_ready, l + 1)
                dve.wait_ge(ranks_ready, l + 1)

                def chunk(S, n):
                    for j in range(2):
                        dve.wait_ge(S.silu, 2 * n + j + 1)
                        dve.tensor_tensor(H[:, P * j:P * j + P], SG[:, P * j:P * j + P], psS[:, j, P:2 * P], ALU.mult).then_inc(S.h, 1)
                        dve.wait_ge(S.turned, 2 * n + j + 1)
                        dve.tensor_copy(HT[:, j, :], (psN, acc[:, 1, :])[j][:, 0:P]).then_inc(S.ht, 1)
                    dve.wait_ge(S.down, n + 1)
                    for j in range(2):
                        dve.tensor_copy(YS[:, 256 * j:256 * j + 256], psV[:, 256 * j:256 * j + 256]).then_inc(S.y, 1)

                with dve.Fori(0, NE // 2) as i:
                    for e in range(2):
                        n = 2 * i + e
                        extra = dve.value_load(MOREI[0:1, bass.ds(n, 1)], min_val=0, max_val=NFURTHER)
                        with dve.If(extra > 0):
                            before = dve.value_load(BEFOREI[0:1, bass.ds(n, 1)], min_val=0, max_val=NROW // CAP)
                            with dve.Fori(0, extra) as c:
                                chunk(more[l], before + c)
                        chunk(first, NE * l + n)
                cm["gt"](l)
                cm["yt"](l)
                residual(f"ms{l}")
                evacuated(dve, f"ms{l}", 7)
                center(f"mean{3 * l + 2}", zT, 8, centered, 2)
                normalise(3 * l + 2)
            cm["y"]()

        @block.scalar
        def _(act):
            cm = common(act, "s")
            act.dma_start(cst[:, :], const).then_inc(in_const, 16)
            cm["x"]()
            cm["q"]()
            cm["k"]()
            cm["v"]()
            for i in range(4):
                full(act, "g", i)
                act.activation(zT[:, i, :], ACC("g", i)[:, 0:NTOK], ACT.Sigmoid).then_inc(emptied["s"], 1)
            cm["state"]()
            for i in range(2):
                full(act, "sbias", i)
                act.activation(SBIAS[:, 512 * i:512 * i + 512], ACC("sbias", i), ACT.Copy).then_inc(emptied["s"], 1)
            evacuated(act, "a", 3)
            cm["ktok"]()
            cm["kt"](0)
            cm["cnew"]()
            act.wait_ge(negmax, 1)

            def prompt_exp(h):
                for t in range(2):
                    r = slice(0, 128) if t == 0 else slice(128, 384)
                    act.activation(SALL[:, h, r], SALL[:, h, r], ACT.Exp, bias=st[:, 16 + 8 * t + h:17 + 8 * t + h],
                                   accum_out=st[:, 32 + 8 * t + h:33 + 8 * t + h]).then_inc(exp_done, 1)

            cm["kt"](1, prompt_exp)
            cm["kt"](2)
            ptpo(act, "s", PTPO)

            def sample_softmax(g):
                act.wait_ge(negmax, 2 + g)
                for j in range(5):
                    r = slice(MOBA * j, MOBA * j + MOBA) if j < 4 else slice(PAST, PAST + 32)
                    act.activation(SS[:, r], SS[:, r], ACT.Exp, bias=st[:, 88 + j:89 + j],
                                   accum_out=st[:, 96 + j:97 + j]).then_inc(exp_done, 1)

            def weighted_values(g):
                act.wait_ge(smp_out, g + 1)
                act.activation(PV, psV[:, :], ACT.Copy).then_inc(smp_read, 1)

            def memory_keys(l, tiles):
                for i in tiles:
                    full(act, f"mk{l}", i)
                    act.activation(mkT[:, 2 * i:2 * i + 2, :], ACC(f"mk{l}", i).rearrange("p (f m) -> p f m", f=2), ACT.Copy)\
                        .then_inc(emptied["s"], 1)

            cm["kt"](3)
            cm["kt"](4, lambda i: sample_softmax(0) if i == 7 else None)
            cm["kt"](5)
            cm["spt"](0)
            weighted_values(0)
            sample_rows(act, "s", 0)
            cm["kt"](6)
            cm["kt"](7)
            evac(act, "s", "memT0", 8, lambda i, a: act.activation(memT[:, i, :], a[:, 0:256], ACT.Copy))
            memory_keys(0, (0, 1))
            sample_softmax(1)
            cm["spt"](1)
            weighted_values(1)
            sample_rows(act, "s", 1)

            def root(signal, stage):
                evacuated(act, stage, 0)
                act.activation(std[:, :], rs[:, :], ACT.Sqrt).then_inc(signal, 1)

            evacuated(act, "cmean", 0)
            act.wait_ge(out_even, 16 * 2)
            act.activation(zT[:, 0:4, :], mixT[:, 4:8, :], ACT.Square).then_inc(sq_c, 1)
            memory_keys(0, (2,))
            root(std_c, "cvar")
            for f in range(4):
                act.wait_ge(scl_c, f + 1)
                act.activation(mixT[:, 4 + f, :], mixT[:, 4 + f, :], ACT.Silu, bias=cparT[:, f, 33:34],
                               scale=cparT[:, f, 32:33]).then_inc(cv_ready, 1)
            memory_keys(0, (3,))

            def squares(nth):
                for c in range(4):
                    if c < 3:
                        act.wait_ge(centered, 3 * nth + c + 1)
                    else:
                        evacuated(act, f"mean{nth}", 0)
                    act.activation(mixT[:, 2 * c:2 * c + 2, :], zT[:, 2 * c:2 * c + 2, :], ACT.Square).then_inc(squared, 1)

            def memory_values(l, tiles):
                for i in tiles:
                    full(act, f"mv{l}", i)
                    act.activation(mvtok[:, i % 2, 512 * (i // 2):512 * (i // 2) + 512], ACC(f"mv{l}", i), ACT.Copy)\
                        .then_inc(emptied["s"], 1)

            def finish(nth):
                root(std_ready, f"var{nth}")
                for f in range(8):
                    act.wait_ge(scaled, 8 * nth + f + 1)
                    act.activation(xT[:, f, :], zT[:, f, :], ACT.Identity, bias=parT[:, f, 6 + nth:7 + nth]).then_inc(x_ready, 1)

            for l in range(DEPTH):
                if l:
                    for i in range(8):
                        full(act, "u", i)
                        act.activation(qT[:, i, :], ACC("u", i)[:, 0:NTOK], ACT.Gelu).then_inc(emptied["s"], 1)
                    for i in range(8):
                        full(act, "vv", i)
                        act.activation(vT[:, i, :], ACC("vv", i)[:, 0:NTOK], ACT.Gelu).then_inc(emptied["s"], 1)
                    for c in range(4):
                        if c < 3:
                            act.wait_ge(cen_v, c + 1)
                        else:
                            evacuated(act, "vmean", 0)
                        act.activation(mixT[:, 2 * c:2 * c + 2, :], vT[:, 2 * c:2 * c + 2, :], ACT.Square).then_inc(sq_v, 1)
                    root(std_v, "vvar")
                    for f in range(8):
                        act.wait_ge(scl_v, f + 1)
                        act.activation(vT[:, f, :], vT[:, f, :], ACT.Identity, bias=parT[:, f, 13:14]).then_inc(vn_ready, 1)
                    cm["vtok"]()
                squares(3 * l)
                if l:
                    evac(act, "s", f"memT{l}", 8, lambda i, a: act.activation(memT[:, i, :], a[:, 0:256], ACT.Copy))
                else:
                    memory_values(l, (0, 1))
                finish(3 * l)
                if l:
                    cm["mk"](l)
                    cm["mv"](l)
                else:
                    memory_values(l, (2, 3))
                cm["xq"](l)
                nm = 3 + 6 * l
                for h in range(4):
                    act.wait_ge(negmax, nm + h + 1)
                    for t in range(2):
                        ins = act.activation(PX[:, 2 * h + t, :], ACC(f"xs{l}", h)[:, 256 * t:256 * t + 256], ACT.Exp,
                                             bias=st[:, 16 + 2 * h + t:17 + 2 * h + t],
                                             accum_out=st[:, 32 + 2 * h + t:33 + 2 * h + t])
                    ins.then_inc(emptied["s"], 1)
                for b in range(4):
                    cm["xkt"](l, b)

                def mem_softmax(g):
                    act.wait_ge(negmax, nm + 4 + g + 1)
                    act.activation(XP[:, g, :], psS[:, g, 0:256], ACT.Exp, bias=st[:, 65 + g:66 + g],
                                   accum_out=st[:, 68 + g:69 + g]).then_inc(exp_done, 1)

                def mem_rows(g):
                    act.wait_ge(values_used, DB * (1 + l) + 4 * g + 4)
                    act.activation(XPV[:, 0, :], psV[:, :], ACT.Copy).then_inc(xpv_ready, 1)

                ptpo(act, "s", XPTPO, l)
                for b in (4, 5):
                    cm["xkt"](l, b)
                mem_softmax(0)
                mem_rows(0)
                for b in (6, 7):
                    cm["xkt"](l, b)
                mem_softmax(1)
                mem_rows(1)
                squares(3 * l + 1)
                cm["mktok"](l)
                finish(3 * l + 1)
                full(act, f"router{l}", 0)
                act.activation(RT[:, 48:96], ACC(f"router{l}", 0)[:, 0:48], ACT.Sigmoid)\
                    .then_inc(emptied["s"], 1)
                act.wait_ge(out_mem, 32 * (l + 1))
                cm["xtok"](l)
                cm["xg"](l)

                def take(S, xs, at):
                    act.activation(xs, XE[:, :, at], ACT.Copy).then_inc(S.xs, 1)


                def chunk(S, n, at, between):
                    for j in range(2):
                        act.wait_ge(S.parts, 2 * n + j + 1)
                        act.activation(SG[:, P * j:P * j + P], psS[:, j, 0:P], ACT.Silu).then_inc(S.silu, 1)
                    between()
                    act.wait_ge(S.y_turned, n + 1)
                    act.activation(YT[:, :, at].rearrange("p (h j) m -> p h j m", h=2),
                                   acc[:, 0, :].rearrange("p (j h m) -> p h j m", j=4, h=2), ACT.Copy).then_inc(S.yt, 1)

                act.wait_ge(ranks_ready, l + 1)
                act.activation(SG[:, 0:1], cst[:, 0:1], ACT.Copy).then_inc(first.yt, 1)
                act.wait_ge(first.yt, (NE + 1) * l + 1)
                for i in range(2 * FT):
                    evacuated(act, f"xg{l}", i)
                take(more[l], XSM, slice(CAP, 2 * CAP))
                take(first, XS, slice(0, CAP))
                with act.Fori(0, NE // 2) as i:
                    for e in range(2):
                        n = 2 * i + e

                        def next_rows():
                            following = act.value_load(STARTI[0:1, bass.ds(n + 1, 1)], min_val=0, max_val=NROW)
                            act.wait_ge(first.parts, 2 * NE * l + 2 * n + 2)
                            take(first, XS, bass.ds(following, CAP))
                            take(more[l], XSM, bass.ds(following + CAP, CAP))

                        start = act.value_load(STARTI[0:1, bass.ds(n, 1)], min_val=0, max_val=NROW)
                        extra = act.value_load(MOREI[0:1, bass.ds(n, 1)], min_val=0, max_val=NFURTHER)
                        with act.If(extra > 0):
                            before = act.value_load(BEFOREI[0:1, bass.ds(n, 1)], min_val=0, max_val=NROW // CAP)
                            with act.Fori(0, extra) as c:
                                k = before + c

                                def further_rows():
                                    act.wait_ge(more[l].parts, 2 * k + 2)
                                    take(more[l], XSM, after_further(start, c))

                                chunk(more[l], k, further(start, c), further_rows)
                        chunk(first, NE * l + n, bass.ds(start, CAP), next_rows)
                cm["gt"](l)
                cm["yt"](l)
                squares(3 * l + 2)
                finish(3 * l + 2)
            cm["y"]()

        @block.gpsimd
        def _(pool):
            pool.dma_start(prow[0:6, :], ln_g.rearrange("l k d -> (l k) d")).then_inc(in_rows, 16)
            pool.dma_start(prow[6:12, :], ln_b.rearrange("l k d -> (l k) d")).then_inc(in_rows, 16)
            pool.dma_start(prow[12:13, :], sgu_ln_g).then_inc(in_rows, 16)
            pool.dma_start(prow[13:14, :], sgu_ln_b).then_inc(in_rows, 16)
            pool.dma_start(crow[0:31, :], conv_w[0]).then_inc(in_rows, 16)
            for i, w in enumerate((conv_b, conv_ln_g, conv_ln_b)):
                pool.dma_start(crow[31 + i:32 + i, :], w).then_inc(in_rows, 16)
            for t in range(2):
                pool.dma_start(strow[0:120, t, :], state_conv[0, 4 * t:4 * t + 4].rearrange("b t c -> (b t) c")).then_inc(in_rows, 16)
            pool.dma_start(wrt[:, :, :], w_router.rearrange("(k p) e -> p k e", p=P)).then_inc(in_rows, 16)
            pool.dma_start(rbias[:, :], router_bias.rearrange("(a e) -> a e", a=1).to_broadcast([P, NE])).then_inc(in_misc, 16)
            pool.dma_start(tab, table).then_inc(in_table, 16)
            pool.wait_ge(rb_zero, 1)
            for j in range(4):
                pool.dma_start(RB4[32 * j:32 * j + 32, 8 * j:8 * j + 8], rel_bias).then_inc(rb_in, 16)
            evacuated(pool, "dbias", 3)
            pool.affine_select(out=BIAS[:, :, 0:128], in_=BIAS[:, :, 0:128], pattern=[[0, 8], [-1, 128]],
                               compare_op=ALU.is_ge, fill=NEG, base=0, channel_multiplier=1).then_inc(bias_masked, 1)
            pool.affine_select(out=BIAS[:, :, 128:384], in_=BIAS[:, :, 128:384], pattern=[[0, 8], [-1, 256]],
                               compare_op=ALU.is_ge, fill=NEG, base=128, channel_multiplier=1).then_inc(bias_masked, 1)
            evacuated(pool, "v", 0), evacuated(pool, "v", 1), evacuated(pool, "v", 2)
            kv = "l (t p) h d -> p (l t) (h d)"
            pool.dma_start(new_v_prompt[0].rearrange(kv, p=P), vtok[:, 0:2, :]).then_inc(out_rest, 16)
            pool.dma_start(new_v_sample[0].rearrange("b s h d -> (b s) (h d)"), vtok[0:32, 2, :]).then_inc(out_rest, 16)
            pool.dma_start(new_conv_sample[0, :, 0:26, :], state_conv[0, :, 4:30, :]).then_inc(out_rest, 16)
            for i in range(3):
                evacuated(pool, "ktok", i)
            pool.dma_start(new_k_prompt[0].rearrange(kv, p=P), ktok[:, 0:2, :]).then_inc(out_even, 16)
            pool.dma_start(new_k_sample[0].rearrange("b s h d -> (b s) (h d)"), ktok[0:32, 2, :]).then_inc(out_even, 16)
            evacuated(pool, "cnew", 0), evacuated(pool, "cnew", 1)
            pool.dma_start(new_conv_prompt[0, 0], cnew[0:30, 0, :]).then_inc(out_rest, 16)
            pool.dma_start(new_conv_sample[0, :, 26:30, :], cnew[0:32, 1, :]).then_inc(out_rest, 16)

            def last_channels():
                f = 3
                y, ys = mixT[:, 4 + f, 0:SEQ], mixT[:, 4 + f, S0:NTOK].rearrange("p (b s) -> p b s", b=8)
                t, ts = rs[:, 0:SEQ], rs[:, S0:NTOK].rearrange("p (b s) -> p b s", b=8)
                evacuated(pool, "cpar", 0), evacuated(pool, "a", 3), evacuated(pool, "state", 3)
                for w in range(CW):
                    u, us, tap = UP[:, f, w:w + SEQ], US[:, f, :, w:w + DS], cparT[:, f, w:w + 1]
                    if w == 0:
                        pool.tensor_scalar(y, u, tap, cparT[:, f, 31:32], ALU.mult, ALU.add)
                        pool.tensor_scalar(ys, us, tap, cparT[:, f, 31:32], ALU.mult, ALU.add).then_inc(conv_pool, 1)
                        continue
                    pool.wait_ge(conv_pool, 2 * w - 1)
                    pool.tensor_scalar(t, u, tap, None, ALU.mult)
                    pool.tensor_scalar(ts, us, tap, None, ALU.mult).then_inc(conv_pool, 1)
                    pool.wait_ge(conv_pool, 2 * w)
                    pool.tensor_tensor(y, y, t, ALU.add)
                    pool.tensor_tensor(ys, ys, ts, ALU.add).then_inc(conv_pool, 1)

            for l in range(DEPTH):
                if l:
                    evacuated(pool, "vtok", 4), evacuated(pool, "vtok", 5)
                    pool.dma_start(new_gmlp_v[0].rearrange("b s d -> (b s) d"), gvtok[0:32, 2, :]).then_inc(out_rest, 16)
                if l:
                    pool.wait_ge(mixed, 8)
                    pool.wait_ge(out_rest, 16 * 6)
                pool.dma_start(memtok, mem_prompt[0].rearrange("(t p) d -> p t d", p=P)).then_inc(mem_in, 16)
                if l == 0:
                    last_channels()
                for i in range(4):
                    evacuated(pool, f"mv{l}", i), evacuated(pool, f"mktok{l}", i)
                pool.dma_start(new_mem_v[l, 0].rearrange("(t p) h d -> p t (h d)", p=P), mvtok).then_inc(out_mem, 16)
                pool.dma_start(new_mem_k[l, 0].rearrange("(t p) h d -> p t (h d)", p=P), mktok).then_inc(out_mem, 16)
                evacuated(pool, f"xpvt{l}1", 1)
                if l == 0:
                    pool.memset(WBD, 0.0).then_inc(wbd_zero, 1)
                    pool.wait_ge(wbd_zero, 1)
                    pool.dma_start(WLD, sgu_w[0].rearrange("g t s -> t g s")).then_inc(g_in, 16)
                    pool.dma_start(BSG, sgu_b.rearrange("a g t -> a (g t)").to_broadcast([P, D])
                                   .rearrange("p (g t) -> p g t", g=8)).then_inc(g_in, 16)
                    for b in range(DB):
                        for g in range(8):
                            pool.dma_start(WBD[4 * b:4 * b + 4, g, 4 * b:4 * b + 4],
                                           sgu_w[0, g, 0:4, 0:4].rearrange("t s -> s t"),
                                           allow_slow_non_contiguous=True).then_inc(wbd_in, 16)
                    pool.wait_ge(g_in, 32)
                    pool.affine_select(out=WLD, in_=WLD, pattern=[[0, 8], [-1, 128]], compare_op=ALU.is_ge, fill=0.0,
                                       base=0, channel_multiplier=1).then_inc(w_masked, 1)
                    pool.wait_ge(wbd_in, 16 * 64)
                    pool.affine_select(out=WBD, in_=WBD, pattern=[[0, 8], [1, 32]], compare_op=ALU.is_ge, fill=0.0,
                                       base=0, channel_multiplier=-1).then_inc(w_masked, 1)
            for i in range(6):
                evacuated(pool, "y", i)
            pool.dma_start(y_prompt[0].rearrange("(t p) d -> p t d", p=P), ytok[:, 0:2, :]).then_inc(out_rest, 16)
            pool.dma_start(y_sample.rearrange("b s d -> (b s) d"), ytok[0:32, 2, :]).then_inc(out_rest, 16)
            pool.wait_ge(out_rest, 16 * 8)
            pool.wait_ge(out_even, 32)
            pool.wait_ge(out_mem, 32 * DEPTH)


_INS = ['x_prompt', 'x_sample', 'cache_k', 'cache_v', 'state_conv', 'cache_mem_k', 'cache_mem_v', 'page_table',
        'mem_prompt', 'rel_bias', 'w_in_even', 'conv_w', 'conv_b', 'conv_ln_g', 'conv_ln_b', 'w_out_even',
        'w_in_odd', 'sgu_ln_g', 'sgu_ln_b', 'sgu_w', 'sgu_b', 'w_out_odd', 'w_xq', 'w_xkv', 'w_xo',
        'w_router', 'router_bias', 'w_exp_gate', 'w_exp_up', 'w_exp_down', 'ln_g', 'ln_b']
_OUTS = [(1, SEQ, D), (DB, DS, D), (1, 1, SEQ, HA, HD), (1, 1, SEQ, HA, HD), (1, DB, DS, HA, HD), (1, DB, DS, HA, HD),
         (1, 1, CW - 1, CC), (1, DB, CW - 1, CC), (DEPTH, 1, NMEM, HX, HDX), (DEPTH, 1, NMEM, HX, HDX),
         (1, DB, DS, D)]


def kernel(**inputs):
    import numpy as _np
    import concourse.bacc as _bacc
    from concourse import mybir as _mybir
    from concourse.bass_utils import run_bass_kernel_spmd as _run

    nc = _bacc.Bacc("TRN2", target_bir_lowering=False, num_devices=1)
    consts = dict(zip(("const", "table"), shape_constants()))
    arrays, args = {}, []
    for name in _INS + list(consts):
        a = _np.ascontiguousarray(inputs[name] if name in inputs else consts[name])
        arrays[f"in_{name}"] = a
        args.append(nc.dram_tensor(f"in_{name}", a.shape, _mybir.dt.from_np(a.dtype), kind="ExternalInput").ap())
    for i, shape in enumerate(_OUTS):
        args.append(nc.dram_tensor(f"out_{i}", shape, _mybir.dt.float32, kind="ExternalOutput").ap())
    build(nc, *args)
    r = _run(nc, [arrays], core_ids=[0])
    return tuple(r.results[0][f"out_{i}"] for i in range(len(_OUTS)))
```
